# Optimizing a Trainium2 kernel written in Bass

```python
import jax, jax.numpy as jnp
from jax import lax
import numpy as np
import math

D_MODEL = 1024
BATCH = 1
SEQ = 1024
DEPTH = 1

CONV_W = D_MODEL // 2
N_HEADS = 8
HEAD_DIM = (D_MODEL - CONV_W) // N_HEADS
ATTN_W = N_HEADS * HEAD_DIM
IN_COLS = 3 * CONV_W + 3 * ATTN_W
CONV_K = 3
D_FF = 2816
PLE_DIM = 256
DILATED_PAIRS = ((128, 1), (512, 4), (2048, 16))
BLOCK = 128
EPS = 1e-6


def rmsnorm(a, g):
    af = a.astype(jnp.float32)
    af = af * lax.rsqrt(jnp.mean(af * af, axis=-1, keepdims=True) + EPS)
    return (af * g.astype(jnp.float32)).astype(a.dtype)

def causal_dwconv3(u, w, b):
    up = jnp.pad(u, ((0, 0), (CONV_K - 1, 0), (0, 0)))
    t = u.shape[1]
    return up[:, 0:t] * w[0] + up[:, 1:t + 1] * w[1] + up[:, 2:t + 2] * w[2] + b

def alibi_slopes(n):
    return jnp.exp2(-8.0 * jnp.arange(1, n + 1, dtype=jnp.float32) / n)

def dilated_branch(q, k, v, slopes, window, dilation):
    b, t, h, hd = q.shape
    steps = window // dilation
    L = t // dilation
    nb = -(-L // BLOCK)
    lp = nb * BLOCK

    def to_blocks(a):
        a = a.reshape(b, L, dilation, h, hd).transpose(0, 2, 3, 1, 4)
        a = jnp.pad(a, ((0, 0), (0, 0), (0, 0), (0, lp - L), (0, 0)))
        return a.reshape(b, dilation, h, nb, BLOCK, hd)

    def with_prev(a):
        prev = jnp.pad(a[:, :, :, :-1], ((0, 0), (0, 0), (0, 0), (1, 0), (0, 0), (0, 0)))
        return jnp.concatenate([prev, a], axis=4)

    qb = to_blocks(q)
    kk = with_prev(to_blocks(k))
    vv = with_prev(to_blocks(v))

    s = jnp.einsum('brhnqd,brhnkd->brhnqk', qb, kk) * (hd ** -0.5)
    qi = jnp.arange(BLOCK)[:, None] + BLOCK
    kj = jnp.arange(2 * BLOCK)[None, :]
    step = qi - kj
    band = (step >= 0) & (step <= steps)
    first = (jnp.arange(nb)[:, None, None] == 0) & (kj < BLOCK)[None]
    mask = band[None] & ~first
    dist = (step * dilation).astype(jnp.float32)
    bias = -slopes[:, None, None] * dist[None]
    s = jnp.where(mask, s + bias[:, None], -jnp.inf)
    m = jnp.max(s, axis=-1, keepdims=True)
    e = jnp.exp(s - m)
    den = jnp.sum(e, axis=-1, keepdims=True)
    o = jnp.einsum('brhnqk,brhnkd->brhnqd', e, vv) / den
    lse = (m + jnp.log(den))[..., 0]

    o = o.reshape(b, dilation, h, lp, hd)[:, :, :, :L]
    o = o.transpose(0, 3, 1, 2, 4).reshape(b, t, h, hd)
    lse = lse.reshape(b, dilation, h, lp)[:, :, :, :L]
    lse = lse.transpose(0, 3, 1, 2).reshape(b, t, h)
    return o, lse

def dilated_attention(q, k, v):
    slopes = alibi_slopes(q.shape[2])
    outs, lses = [], []
    for window, dilation in DILATED_PAIRS:
        o, lse = dilated_branch(q, k, v, slopes, window, dilation)
        outs.append(o)
        lses.append(lse)
    wts = jax.nn.softmax(jnp.stack(lses, axis=0), axis=0)
    o = jnp.sum(wts[..., None] * jnp.stack(outs, axis=0), axis=0)
    return o

def first_inputs(seed: int = 0) -> dict:
    key = jax.random.key(seed)
    ks = jax.random.split(key, 24)
    f32 = jnp.float32

    def nrm(k, shape, fan):
        return jax.random.normal(k, shape, f32) * (fan ** -0.5)

    def gain(k, shape):
        return 1.0 + 0.05 * jax.random.normal(k, shape, f32)

    def bias(k, shape):
        return 0.01 * jax.random.normal(k, shape, f32)

    return {
        'x': jax.random.normal(ks[0], (BATCH, SEQ, D_MODEL), f32),
        'p': jax.random.normal(ks[1], (DEPTH, BATCH, SEQ, PLE_DIM), f32),
        'g_mix': gain(ks[2], (DEPTH, D_MODEL)),
        'w_in': nrm(ks[3], (DEPTH, D_MODEL, IN_COLS), D_MODEL),
        'conv_w': nrm(ks[4], (DEPTH, CONV_K, CONV_W), CONV_K),
        'conv_b': bias(ks[5], (DEPTH, CONV_W)),
        'q_norm_g': gain(ks[6], (DEPTH, HEAD_DIM)),
        'k_norm_g': gain(ks[7], (DEPTH, HEAD_DIM)),
        'g_out_conv': gain(ks[8], (DEPTH, CONV_W)),
        'g_out_attn': gain(ks[9], (DEPTH, ATTN_W)),
        'w_out': nrm(ks[10], (DEPTH, CONV_W + ATTN_W, D_MODEL), CONV_W + ATTN_W),
        'g_ffn': gain(ks[11], (DEPTH, D_MODEL)),
        'w_gate': nrm(ks[12], (DEPTH, D_MODEL, D_FF), D_MODEL),
        'w_up': nrm(ks[13], (DEPTH, D_MODEL, D_FF), D_MODEL),
        'ffn_conv_w': nrm(ks[14], (DEPTH, CONV_K, D_FF), CONV_K),
        'ffn_conv_b': bias(ks[15], (DEPTH, D_FF)),
        'w_down': nrm(ks[16], (DEPTH, D_FF, D_MODEL), D_FF),
        'g_ple': gain(ks[17], (DEPTH, D_MODEL)),
        'w_ple_gate': nrm(ks[18], (DEPTH, D_MODEL, D_MODEL), D_MODEL),
        'w_ple_proj': nrm(ks[19], (DEPTH, PLE_DIM, D_MODEL), PLE_DIM),
    }

def first_block(x, p, g_mix, w_in, conv_w, conv_b, q_norm_g, k_norm_g, g_out_conv,
              g_out_attn, w_out, g_ffn, w_gate, w_up, ffn_conv_w, ffn_conv_b, w_down,
              g_ple, w_ple_gate, w_ple_proj):
    b, t, _ = x.shape
    for i in range(DEPTH):
        h = rmsnorm(x, g_mix[i])
        z = h @ w_in[i]
        zb, zc, zx, zq, zk, zv = jnp.split(
            z, np.cumsum([CONV_W, CONV_W, CONV_W, ATTN_W, ATTN_W]), axis=-1)
        y_c = zb * causal_dwconv3(zc * zx, conv_w[i], conv_b[i])
        q = rmsnorm(zq.reshape(b, t, N_HEADS, HEAD_DIM), q_norm_g[i]).astype(jnp.float32)
        k = rmsnorm(zk.reshape(b, t, N_HEADS, HEAD_DIM), k_norm_g[i]).astype(jnp.float32)
        v = zv.reshape(b, t, N_HEADS, HEAD_DIM).astype(jnp.float32)
        y_a = dilated_attention(q, k, v).reshape(b, t, ATTN_W).astype(x.dtype)
        y = jnp.concatenate([rmsnorm(y_c, g_out_conv[i]), rmsnorm(y_a, g_out_attn[i])], axis=-1)
        x = x + y @ w_out[i]
        h = rmsnorm(x, g_ffn[i])
        gate = causal_dwconv3(h @ w_gate[i], ffn_conv_w[i], ffn_conv_b[i])
        x = x + (jax.nn.silu(gate) * (h @ w_up[i])) @ w_down[i]
        ple_gate = jax.nn.sigmoid(rmsnorm(x, g_ple[i]) @ w_ple_gate[i])
        x = x + ple_gate * (p[i].astype(x.dtype) @ w_ple_proj[i])
    return x


CHUNK = 64
Q_BLOCK = 128
HEAD_DIM_2 = 64
MIX_WIDTH = D_MODEL
A_WIDTH = MIX_WIDTH // 2
B_WIDTH = MIX_WIDTH - A_WIDTH
A_HEADS = A_WIDTH // HEAD_DIM_2
B_HEADS = B_WIDTH // HEAD_DIM_2
KV_LATENT = 128
IDX_HEADS = 4
IDX_DIM = 32
TOPK_MAX = 256
NUM_BUCKETS = 32
MAX_DISTANCE = 128
ROPE_BASE = 10000.0
RMS_EPS = 1e-6
GN_EPS = 1e-5
FFN_HIDDEN = ((-(-(8 * D_MODEL) // 3) + 255) // 256) * 256

IN_SIZES = [A_WIDTH, KV_LATENT, IDX_HEADS * IDX_DIM, IDX_DIM, IDX_HEADS,
            B_WIDTH, B_WIDTH, B_WIDTH, B_WIDTH]
IN_WIDTH = sum(IN_SIZES)
IN_OFFSETS = [int(o) for o in np.cumsum(IN_SIZES)[:-1]]


def rmsnorm_2(x, w):
    xf = x.astype(jnp.float32)
    y = xf * lax.rsqrt(jnp.mean(xf * xf, axis=-1, keepdims=True) + RMS_EPS)
    return (y * w.astype(jnp.float32)).astype(x.dtype)

def t5_bucket(rel):
    half = NUM_BUCKETS // 2
    max_exact = half // 2
    ret = jnp.where(rel > 0, half, 0)
    n = jnp.abs(rel)
    nf = jnp.maximum(n, 1).astype(jnp.float32)
    large = max_exact + (jnp.log(nf / max_exact) / math.log(MAX_DISTANCE / max_exact)
                         * (half - max_exact)).astype(jnp.int32)
    large = jnp.minimum(large, half - 1)
    return ret + jnp.where(n < max_exact, n, large)

def rotary(x, pos):
    half = x.shape[-1] // 2
    inv = ROPE_BASE ** (-jnp.arange(half, dtype=jnp.float32) / half)
    ang = pos.astype(jnp.float32)[:, None] * inv[None, :]
    cos = jnp.cos(ang)[:, None, :]
    sin = jnp.sin(ang)[:, None, :]
    x1, x2 = x[..., :half], x[..., half:]
    return jnp.concatenate([x1 * cos - x2 * sin, x1 * sin + x2 * cos], axis=-1)

def indexed_sparse_attention(q, k, v, iq, ik, iw, rel_bias):
    b, s, h, dh = q.shape
    topk = min(TOPK_MAX, s // 4)
    n_blocks = s // Q_BLOCK
    key_pos = jnp.arange(s)
    idx_scale = IDX_DIM ** -0.5
    w_scale = IDX_HEADS ** -0.5

    def block(i):
        t0 = i * Q_BLOCK
        qb = lax.dynamic_slice_in_dim(q, t0, Q_BLOCK, axis=1)
        iqb = lax.dynamic_slice_in_dim(iq, t0, Q_BLOCK, axis=1)
        iwb = lax.dynamic_slice_in_dim(iw, t0, Q_BLOCK, axis=1)
        qpos = t0 + jnp.arange(Q_BLOCK)
        limit = (qpos // CHUNK + 1) * CHUNK
        admissible = key_pos[None, :] < limit[:, None]
        dots = jnp.einsum('bthd,bsd->bths', iqb, ik).astype(jnp.float32) * idx_scale
        score = jnp.einsum('bth,bths->bts', iwb.astype(jnp.float32) * w_scale,
                           jax.nn.relu(dots))
        score = jnp.where(admissible[None], score, -jnp.inf)
        _, idx = lax.top_k(score, topk)
        valid = idx < limit[None, :, None]
        kg = jax.vmap(lambda kb, ib: kb[ib])(k, idx)
        vg = jax.vmap(lambda vb, ib: vb[ib])(v, idx)
        logits = jnp.einsum('bthd,btkd->bhtk', qb, kg).astype(jnp.float32) * dh ** -0.5
        bias = rel_bias[t5_bucket(idx - qpos[None, :, None])]
        logits = logits + jnp.transpose(bias, (0, 3, 1, 2)).astype(jnp.float32)
        logits = jnp.where(valid[:, None], logits, -jnp.inf)
        p = jax.nn.softmax(logits, axis=-1)
        return jnp.einsum('bhtk,btkd->bthd', p.astype(v.dtype), vg)

    outs = lax.map(block, jnp.arange(n_blocks))
    return jnp.moveaxis(outs, 0, 1).reshape(b, s, h * dh)

def chunkwise_retention(q, k, v):
    b, s, h, dh = q.shape
    nc = s // CHUNK
    log_g = jnp.log1p(-(2.0 ** (-5.0 - jnp.arange(h, dtype=jnp.float32))))
    j = jnp.arange(CHUNK, dtype=jnp.float32)
    rel = j[:, None] - j[None, :]
    inner_decay = jnp.where(rel[None] >= 0,
                            jnp.exp(jnp.maximum(rel, 0.0)[None] * log_g[:, None, None]), 0.0)
    query_decay = jnp.exp((j + 1.0)[:, None] * log_g[None, :])[None, :, :, None]
    key_decay = jnp.exp((CHUNK - 1.0 - j)[:, None] * log_g[None, :])[None, :, :, None]
    chunk_decay = jnp.exp(CHUNK * log_g)[None, :, None, None]

    def to_chunks(t):
        return jnp.transpose(t.reshape(b, nc, CHUNK, h, dh), (1, 0, 2, 3, 4))

    def step(state, xs):
        qc, kc, vc = xs
        scores = jnp.einsum('bihd,bjhd->bhij', qc, kc) * inner_decay[None]
        inner = jnp.einsum('bhij,bjhd->bihd', scores, vc)
        cross = jnp.einsum('bihd,bhde->bihe', qc, state) * query_decay
        new_state = state * chunk_decay + jnp.einsum('bjhd,bjhe->bhde', kc * key_decay, vc)
        return new_state, inner + cross

    state0 = jnp.zeros((b, h, dh, dh), jnp.float32)
    _, ys = lax.scan(step, state0, (to_chunks(q), to_chunks(k), to_chunks(v)))
    return jnp.transpose(ys, (1, 0, 2, 3, 4)).reshape(b, s, h, dh)

def second_inputs(seed: int = 0) -> dict:
    key = jax.random.key(seed)
    ks = jax.random.split(key, 20)
    f32 = jnp.float32

    def nrm(k, shape, fan_in):
        return jax.random.normal(k, shape, f32) * fan_in ** -0.5

    def gain(k, shape):
        return 1.0 + 0.02 * jax.random.normal(k, shape, f32)

    return {
        "x": jax.random.normal(ks[0], (BATCH, SEQ, D_MODEL), f32),
        "norm1_w": gain(ks[1], (DEPTH, D_MODEL)),
        "w_in": nrm(ks[2], (DEPTH, D_MODEL, IN_WIDTH), D_MODEL),
        "q_norm_w": gain(ks[3], (DEPTH, HEAD_DIM_2)),
        "k_norm_w": gain(ks[4], (DEPTH, HEAD_DIM_2)),
        "kv_norm_w": gain(ks[5], (DEPTH, KV_LATENT)),
        "w_uk": nrm(ks[6], (DEPTH, KV_LATENT, HEAD_DIM_2), KV_LATENT),
        "w_uv": nrm(ks[7], (DEPTH, KV_LATENT, HEAD_DIM_2), KV_LATENT),
        "rel_bias": 0.1 * jax.random.normal(ks[8], (NUM_BUCKETS, A_HEADS), f32),
        "ret_gn_w": gain(ks[9], (DEPTH, B_WIDTH)),
        "ret_gn_b": 0.02 * jax.random.normal(ks[10], (DEPTH, B_WIDTH), f32),
        "w_out": nrm(ks[11], (DEPTH, MIX_WIDTH, D_MODEL), MIX_WIDTH),
        "norm2_w": gain(ks[12], (DEPTH, D_MODEL)),
        "w_gate": nrm(ks[13], (DEPTH, D_MODEL, FFN_HIDDEN), D_MODEL),
        "w_up": nrm(ks[14], (DEPTH, D_MODEL, FFN_HIDDEN), D_MODEL),
        "w_down": nrm(ks[15], (DEPTH, FFN_HIDDEN, D_MODEL), FFN_HIDDEN),
    }

def second_block(x, norm1_w, w_in, q_norm_w, k_norm_w, kv_norm_w, w_uk, w_uv, rel_bias,
              ret_gn_w, ret_gn_b, w_out, norm2_w, w_gate, w_up, w_down):
    b, s, _ = x.shape
    pos = jnp.arange(s)
    for l in range(DEPTH):
        h = rmsnorm_2(x, norm1_w[l])
        z = h @ w_in[l]
        qa, c_kv, iq, ik, iw, qb, kb, vb, gb = jnp.split(z, IN_OFFSETS, axis=-1)

        qa = rmsnorm_2(qa.reshape(b, s, A_HEADS, HEAD_DIM_2), q_norm_w[l])
        c = rmsnorm_2(c_kv, kv_norm_w[l])
        ka = rmsnorm_2(c @ w_uk[l], k_norm_w[l])
        va = c @ w_uv[l]
        out_a = indexed_sparse_attention(qa, ka, va,
                                         iq.reshape(b, s, IDX_HEADS, IDX_DIM), ik, iw, rel_bias)

        qr = rotary(qb.reshape(b, s, B_HEADS, HEAD_DIM_2).astype(jnp.float32), pos)
        kr = rotary(kb.reshape(b, s, B_HEADS, HEAD_DIM_2).astype(jnp.float32), pos) * HEAD_DIM_2 ** -0.5
        vr = vb.reshape(b, s, B_HEADS, HEAD_DIM_2).astype(jnp.float32)
        y = chunkwise_retention(qr, kr, vr)
        mu = jnp.mean(y, axis=-1, keepdims=True)
        var = jnp.mean(jnp.square(y - mu), axis=-1, keepdims=True)
        y = ((y - mu) * lax.rsqrt(var + GN_EPS)).reshape(b, s, B_WIDTH)
        y = y * ret_gn_w[l].astype(jnp.float32) + ret_gn_b[l].astype(jnp.float32)
        out_b = (jax.nn.silu(gb.astype(jnp.float32)) * y).astype(x.dtype)

        x = x + jnp.concatenate([out_a, out_b], axis=-1) @ w_out[l]

        h2 = rmsnorm_2(x, norm2_w[l])
        x = x + (jax.nn.silu(h2 @ w_gate[l]) * (h2 @ w_up[l])) @ w_down[l]
    return x


def setup_inputs(seed=0):
    out = dict(first_inputs(seed))
    for name, value in second_inputs(seed + 1).items():
        if name != "x":
            out[name + "_2"] = value
    return out


def reference(
    x, p, g_mix, w_in, conv_w, conv_b, q_norm_g, k_norm_g, g_out_conv, g_out_attn, w_out, g_ffn,
    w_gate, w_up, ffn_conv_w, ffn_conv_b, w_down, g_ple, w_ple_gate, w_ple_proj, norm1_w_2,
    w_in_2, q_norm_w_2, k_norm_w_2, kv_norm_w_2, w_uk_2, w_uv_2, rel_bias_2, ret_gn_w_2,
    ret_gn_b_2, w_out_2, norm2_w_2, w_gate_2, w_up_2, w_down_2,
):
    x = first_block(
        x, p, g_mix, w_in, conv_w, conv_b, q_norm_g, k_norm_g, g_out_conv, g_out_attn, w_out,
        g_ffn, w_gate, w_up, ffn_conv_w, ffn_conv_b, w_down, g_ple, w_ple_gate, w_ple_proj,
    )
    return second_block(
        x, norm1_w_2, w_in_2, q_norm_w_2, k_norm_w_2, kv_norm_w_2, w_uk_2, w_uv_2, rel_bias_2,
        ret_gn_w_2, ret_gn_b_2, w_out_2, norm2_w_2, w_gate_2, w_up_2, w_down_2,
    )


_drawn_inputs = setup_inputs


def setup_inputs(seed=0):
    import zlib

    import numpy as np

    out = dict(_drawn_inputs(seed))
    spreads = {}
    factors = {'conv_b': 8.0,
     'ffn_conv_b': 8.0,
     'g_ple': 7.038,
     'norm1_w_2': 4.484,
     'q_norm_w_2': 8.0,
     'k_norm_w_2': 8.0,
     'kv_norm_w_2': 8.0,
     'rel_bias_2': 8.0,
     'ret_gn_w_2': 8.0,
     'ret_gn_b_2': 8.0,
     'norm2_w_2': 5.919}
    for name, (base, spread) in spreads.items():
        noise = np.random.default_rng([zlib.crc32(name.encode()), seed]).standard_normal(out[name].shape)
        drawn = base * np.exp(spread * noise) if base else spread * noise
        out[name] = __import__('jax').numpy.asarray(drawn.astype(out[name].dtype))
    for name, factor in factors.items():
        out[name] = (out[name] * factor).astype(out[name].dtype)
    return out
```

```python
from contextlib import ExitStack

import concourse.bass as bass
from concourse import mybir

ALU = mybir.AluOpType
ACT = mybir.ActivationFunctionType
F32 = mybir.dt.float32
F32R = mybir.dt.float32r
I32 = mybir.dt.int32
NEG = -1.0e30

T = 1024
NH = 8
GROUPS = [(0, 5), (5, 10), (10, 14), (14, 18), (18, 22)]
NF = 22

COLS = [("g_mix", 8), ("g_ffn", 8), ("g_ple", 8), ("norm1_w_2", 8), ("norm2_w_2", 8),
        ("conv_w", 12), ("conv_b", 4), ("ffn_conv_w", 66), ("ffn_conv_b", 22),
        ("g_out_conv", 4), ("g_out_attn", 4), ("q_norm_g", 1), ("k_norm_g", 1),
        ("q_norm_w_2", 1), ("k_norm_w_2", 1), ("kv_norm_w_2", 1), ("ret_gn_w_2", 4), ("ret_gn_b_2", 4),
        ("kdec", 8), ("g128", 4), ("eps6", 1), ("eps5", 1)]
COL = {}
_at = 0
for _n, _w in COLS:
    COL[_n] = _at
    _at += _w
NCOL = _at

MATS = [("ones", 128), ("ones128", 128), ("bd", 128), ("ident", 128), ("perm", 128), ("adm", 128), ("ones512", 128)]
MAT = {}
_at = 0
for _n, _w in MATS:
    MAT[_n] = (_at, _w)
    _at += _w
NMAT = _at


class Prog:

    def __init__(self, nc, sems):
        self.sems = sems
        self.eng = {"V": nc.vector, "A": nc.scalar, "T": nc.tensor, "G": nc.gpsimd, "S": nc.sync}
        self.n = {s: 0 for s in sems}
        self.seen = {e: {} for e in "VATGS"}
        self.last = None

    def wait(self, e, *toks):
        for t in toks:
            if t is None:
                continue
            if isinstance(t, list):
                self.wait(e, *t)
                continue
            s, v = t
            if self.seen[e].get(s, 0) < v:
                self.seen[e][s] = v
                self.eng[e].wait_ge(self.sems[s], v)

    def do(self, e, fn, *toks):
        self.wait(e, *toks)
        self.n[e] += 1
        fn(self.eng[e]).then_inc(self.sems[e], 1)
        return (e, self.n[e])

    def mm(self, fn, *toks):
        self.wait("T", *toks)
        self.last = fn(self.eng["T"])

    def mark(self):
        if self.last is not None:
            self.n["T"] += 1
            self.last.then_inc(self.sems["T"], 1)
            self.last = None
        return ("T", self.n["T"])

    def dma(self, e, s, fn, *toks):
        self.wait(e, *toks)
        self.n[s] += 16
        fn(self.eng[e]).then_inc(self.sems[s], 16)
        return (s, self.n[s])


class Ring:

    def __init__(self, n):
        self.n, self.at, self.free = n, 0, [[] for _ in range(n)]

    def take(self, k=1):
        if self.at % k:
            self.at += k - self.at % k
        i = self.at % self.n
        self.at += k
        w = []
        for j in range(i, i + k):
            assert self.free[j] is not None, "buffer still held"
            w += self.free[j]
            self.free[j] = None
        return i, w

    def give(self, i, *toks, k=1):
        for j in range(i, i + k):
            assert self.free[j] is None
            self.free[j] = list(toks)


def build(nc, d):
    ctx = ExitStack()
    used = set()

    def sbt(stack, name, shape, dt=F32):
        assert name not in used
        used.add(name)
        return stack.enter_context(nc.sbuf_tensor(name, shape, dt))

    DS = ["w0", "w1", "w2", "cst", "col", "x0", "x1", "x2", "x3", "x4", "x5", "x6", "x7", "t0", "t1", "sp", "rb", "rl", "out"]
    sems = {s: ctx.enter_context(nc.semaphore("s_" + s)) for s in list("VATG") + DS}
    P = Prog(nc, sems)
    PS = ctx.enter_context(nc.psum_tensor("PS", [128, 4096], F32))
    PB = Ring(8)

    def ps(b, n=512):
        return PS[:, 512 * b:512 * b + n]

    Hh = sbt(ctx, "Hh", [128, 8, T], F32R)
    Hl = sbt(ctx, "Hl", [128, 8, T], F32R)
    Wr = sbt(ctx, "Wr", [128, 3, 1024])
    Wh = sbt(ctx, "Wh", [128, 3, 1024], F32R)
    Wl = sbt(ctx, "Wl", [128, 3, 1024], F32R)
    acc = sbt(ctx, "acc", [128, T])
    rr = sbt(ctx, "rr", [128, T])
    K1 = sbt(ctx, "K1", [128, 2, T])
    cols = sbt(ctx, "cols", [128, NCOL])
    mats = sbt(ctx, "mats", [128, NMAT])
    sml = sbt(ctx, "sml", [128, 512])
    K1R = Ring(2)

    def col(name, j=0):
        return cols[:, COL[name] + j:COL[name] + j + 1]

    def mat(name, j=0, n=None):
        at, w = MAT[name]
        n = w if n is None else n
        return mats[:, at + j:at + j + n]

    ident = mat("ident")
    gq1, gq2 = sml[:, 100:101], sml[:, 101:102]
    t_cols = P.dma("S", "col", lambda e: e.dma_start(cols[:, :], d["cols"]))
    t_cst = P.dma("S", "cst", lambda e: e.dma_start(mats[:, :], d["mats"]))

    t_gq = P.do("V", lambda e: e.tensor_scalar(gq1, col("q_norm_g"), 0.125, None, ALU.mult), t_cols)
    t_gq = P.do("V", lambda e: e.tensor_scalar(gq2, col("q_norm_w_2"), 0.125, None, ALU.mult), t_cols)

    units = []
    units += [(d["wqk1"], n, 1024) for n in range(8)]
    units += [(d["wv1"], n, 1024) for n in range(4)]
    units += [(d["wc1"], n, 1024) for n in range(12)]
    units += [(d["wo1"], n, 1024) for n in range(8)]

    def ffn_units(g, u, dn):
        out = []
        for a, b in GROUPS:
            for f in range(a, b):
                out += [(g, f, 1024), (u, f, 1024)]
            out += [(dn, m, (a, b)) for m in range(8)]
        return out
    units += ffn_units(d["wg1"], d["wu1"], d["wd1"])
    for m in range(8):
        units += [(d["wpg"], m, 1024), (d["wpp"], m, 256)]
    units += [(d["wi2"], n, 1024) for n in range(24)]
    units += [(d["wo2"], n, 1024) for n in range(8)]
    units += ffn_units(d["wg2"], d["wu2"], d["wd2"])

    raw_t, raw_free, cv_t, w_free = {}, {}, {}, {}
    ws = {"load": 0, "conv": 0, "use": 0}

    def ncols(n):
        return n if isinstance(n, int) else 128 * (n[1] - n[0])

    def load_unit():
        u = ws["load"]
        ws["load"] += 1
        if u >= len(units):
            return
        src, i, n = units[u]
        s = u % 3
        w = ncols(n)
        ap = src[i, :, 0:w] if isinstance(n, int) else src[i, :, 128 * n[0]:128 * n[1]]
        raw_t[u] = P.dma("S", f"w{s}", lambda e: e.dma_start(Wr[:, s, 0:w], ap), raw_free.get(u - 3))

    def conv_unit():
        u = ws["conv"]
        ws["conv"] += 1
        if u >= len(units):
            return
        w = ncols(units[u][2])
        s = u % 3
        a = P.do("A", lambda e: e.activation(Wh[:, s, 0:w], Wr[:, s, 0:w], ACT.Copy), raw_t[u], w_free.get(u - 3))
        g = P.do("G", lambda e: e.tensor_tensor(Wl[:, s, 0:w], Wr[:, s, 0:w], Wh[:, s, 0:w].bitcast(F32),
                                                ALU.subtract), a)
        raw_free[u] = g
        cv_t[u] = [a, g]

    for _ in range(3):
        load_unit()

    def use_unit():
        u = ws["use"]
        ws["use"] += 1
        while ws["conv"] <= min(u + 1, len(units) - 1) and (ws["conv"] < 3 or ws["conv"] - 3 in w_free):
            conv_unit()
            load_unit()
        assert ws["conv"] > u
        return u, u % 3, cv_t[u]

    def done_unit(u, tok):
        w_free[u] = tok

    later = []

    def flush():
        while later:
            later.pop(0)()

    def run_later(n):
        for _ in range(n):
            later.pop(0)()

    def dense(nk, xh, xl, xt, consumer, halves=(0, 1)):
        u, s, wt = use_unit()
        for half in halves:
            pend = len(later)
            b, bw = PB.take()
            for k in range(nk):
                xk = xt[k] if isinstance(xt, dict) else xt
                for n, (wa, xa) in enumerate(((Wl, xh), (Wh, xl), (Wh, xh))):
                    P.mm(lambda e, b=b, wa=wa, xa=xa, k=k, half=half, n=n: e.matmul(
                        ps(b), wa[:, s, 128 * k:128 * k + 128], xa(k, half),
                        start=(k == 0 and n == 0), stop=(k == nk - 1 and n == 2)), wt, bw, xk)
            tok = P.mark()
            run_later(pend)
            consumer(half, b, tok)
        done_unit(u, tok)

    def hk(t):
        return lambda k, half: t[:, k, 512 * half:512 * half + 512]

    Hhk, Hlk = hk(Hh), hk(Hl)

    def dense_tok(xt, consumer):
        flush()
        banks = [PB.take() for _ in range(8)]
        for kg in range(4):
            u, s, wt = use_unit()
            for i in range(8):
                b, bw = banks[i]
                for k2 in range(2):
                    k = 2 * kg + k2
                    for n, (wa, xa) in enumerate(((Wl, Hh), (Wh, Hl), (Wh, Hh))):
                        P.mm(lambda e, b=b, wa=wa, xa=xa, k=k, k2=k2, i=i, n=n, s=s: e.matmul(
                            ps(b), xa[:, k, 128 * i:128 * i + 128], wa[:, s, 512 * k2:512 * k2 + 512],
                            start=(k == 0 and n == 0), stop=(k == 7 and n == 2)), wt, bw, xt[k] if isinstance(xt, dict) else xt)
                if kg == 3:
                    consumer(i, b, P.mark())
            done_unit(u, P.mark())

    class Sum:
        def __init__(self, eng="G"):
            self.t, self.first, self.eng = None, True, eng

        def add(self, x, sl, tok):
            key = (sl.start, sl.stop)
            if key not in self.done:
                self.done[key] = P.do("A", lambda e: e.activation(acc[:, sl], x, ACT.Square), tok, self.prev)
                return self.done[key]
            i, w = K1R.take()
            n = sl.stop - sl.start
            a = P.do("A", lambda e: e.activation(K1[:, i, 0:n], x, ACT.Square), tok, w)
            g = P.do(self.eng, lambda e: e.tensor_tensor(acc[:, sl], acc[:, sl], K1[:, i, 0:n], ALU.add),
                     a, self.done[key])
            K1R.give(i, g)
            self.done[key] = g
            return a

    def new_sum(eng="G", prev=None):
        s = Sum(eng)
        s.done, s.prev = {}, prev
        return s

    acc_free = {"t": None}
    rr_free = {"t": None}

    def rnorm(ones, toks, out=None):
        ts = []
        for half in range(2):
            b, bw = PB.take()
            P.mm(lambda e, b=b, half=half: e.matmul(ps(b), ones, acc[:, 512 * half:512 * half + 512],
                                                    start=True, stop=True), bw, toks, t_cst)
            t = P.mark()
            a = P.do("A", lambda e, b=b, half=half: e.activation(rr[:, 512 * half:512 * half + 512], ps(b), ACT.Sqrt,
                                                                 bias=col("eps6")), t, rr_free["t"], t_cols)
            PB.give(b, a)
            ts.append(P.do("V", lambda e, half=half: e.reciprocal(rr[:, 512 * half:512 * half + 512],
                                                                  rr[:, 512 * half:512 * half + 512]), a))
        acc_free["t"] = t
        return ts[-1]

    def split(dh, dl, src, tok, w, eng="V"):
        a = P.do("A", lambda e: e.activation(dh, src, ACT.Copy), tok, w)
        v = P.do(eng, lambda e: e.tensor_tensor(dl, src, dh.bitcast(F32), ALU.subtract), a, tok, w)
        return a, v

    def norm_to_h(X, gname, rt, xtoks, hw):
        out = {}
        for k in range(8):
            i, w = K1R.take()
            v = P.do("V", lambda e, k=k, i=i: e.scalar_tensor_tensor(
                out=K1[:, i, :], in0=X[:, k, :], scalar=col(gname, k), in1=rr[:, :], op0=ALU.mult, op1=ALU.mult),
                rt, xtoks, w)
            a, l = split(Hh[:, k, :], Hl[:, k, :], K1[:, i, :], v, hw)
            K1R.give(i, a, l)
            out[k] = [a, l]
        rr_free["t"] = v
        return out

    def headnorm(half, b, tok, out, gcol, ones="bd"):
        i, w = K1R.take()
        sq = K1[:, i, 0:512]
        r = K1[:, i, 512:1024]
        a = P.do("A", lambda e: e.activation(sq, ps(b), ACT.Square), tok, w)
        res = {}

        def second():
            b2, bw = PB.take()
            P.mm(lambda e: e.matmul(ps(b2), mat(ones), sq, start=True, stop=True), bw, a, t_cst)
            t = P.mark()
            a2 = P.do("A", lambda e: e.activation(r, ps(b2), ACT.Sqrt, bias=col("eps6")), t, t_cols)
            PB.give(b2, a2)
            v = P.do("V", lambda e: e.reciprocal(r, r), a2)
            v2 = P.do("V", lambda e: e.scalar_tensor_tensor(out=out, in0=ps(b), scalar=gcol, in1=r,
                                                            op0=ALU.mult, op1=ALU.mult), v, tok)
            PB.give(b, v2)
            K1R.give(i, v2)
            res["t"] = v2
        later.append(second)
        return res

    stX = ExitStack()
    X = sbt(stX, "X1", [128, 8, T])
    xt = []
    sm = new_sum("V")
    for k in range(8):
        t = P.dma("S", f"x{k}", lambda e, k=k: e.dma_start(X[:, k, :], d["xT"][k]))
        xt.append(t)
    for k in range(8):
        sm.add(X[:, k, :], slice(0, T), xt[k])
    rt = rnorm(mat("ones"), list(sm.done.values()))
    ht = norm_to_h(X, "g_mix", rt, xt, None)
    x_dead = [ht[7][0], ht[7][1], rt]
    stX.close()

    stM = ExitStack()
    QT = sbt(stM, "QT", [128, 4, T])
    KT = sbt(stM, "KT", [128, 4, T])
    Vt = sbt(stM, "Vt", [128, 8, 512])
    stY = ExitStack()
    YC = sbt(stY, "YC", [128, 4, T])
    ZC = sbt(stY, "ZC", [128, 2, T + 2])
    qk_t = []
    P.wait("V", x_dead)
    P.wait("A", x_dead)
    for n in range(8):
        dst, g = (KT, col("k_norm_g")) if n < 4 else (QT, gq1)

        def cons(half, b, tok, dst=dst, g=g, n=n):
            qk_t.append(headnorm(half, b, tok, dst[:, n % 4, 512 * half:512 * half + 512], g))
        dense(8, Hhk, Hlk, ht, cons)
    flush()
    v_t = []

    def cons_v(i, b, tok):
        a = P.do("A", lambda e: e.activation(Vt[:, i, :], ps(b), ACT.Copy), tok)
        PB.give(b, a)
        v_t.append(a)
    dense_tok(ht, cons_v)
    zpad = P.do("V", lambda e: e.memset(ZC[:, :, 0:2], 0.0))
    smc = new_sum("G", acc_free["t"])
    st = {}
    yc_t = []
    for j in range(4):
        z = j % 2

        def cons_c(half, b, tok, z=z, j=j):
            st["c", half] = (b, tok)
            i, w = (st["ki"] if half else K1R.take())
            st["ki"] = (i, w)
            a = P.do("A", lambda e: e.activation(K1[:, i, 512 * half:512 * half + 512], ps(b), ACT.Copy), tok, w)
            PB.give(b, a)
            st["ca", half] = a

        def cons_x(half, b, tok, z=z, j=j):
            i, _ = st["ki"]
            v = P.do("V", lambda e: e.tensor_tensor(ZC[:, z, 2 + 512 * half:514 + 512 * half], ps(b),
                                                    K1[:, i, 512 * half:512 * half + 512], ALU.mult),
                     tok, st["ca", half], zpad)
            PB.give(b, v)
            if half:
                K1R.give(i, v)
                y = YC[:, j, :]
                v = P.do("V", lambda e: e.tensor_scalar(y, ZC[:, z, 2:T + 2], col("conv_w", 8 + j), col("conv_b", j),
                                                        ALU.mult, ALU.add), v)
                v = P.do("V", lambda e: e.scalar_tensor_tensor(out=y, in0=ZC[:, z, 1:T + 1], scalar=col("conv_w", 4 + j),
                                                               in1=y, op0=ALU.mult, op1=ALU.add), v)
                v = P.do("V", lambda e: e.scalar_tensor_tensor(out=y, in0=ZC[:, z, 0:T], scalar=col("conv_w", j),
                                                               in1=y, op0=ALU.mult, op1=ALU.add), v)
                st["y"] = v

        def cons_b(half, b, tok, z=z, j=j):
            sl = slice(512 * half, 512 * half + 512)
            v = P.do("V", lambda e: e.tensor_tensor(YC[:, j, sl], ps(b), YC[:, j, sl], ALU.mult), tok, st["y"])
            PB.give(b, v)
            smc.add(YC[:, j, sl], sl, v)
            yc_t.append(v)
        dense(8, Hhk, Hlk, ht, cons_c)
        dense(8, Hhk, Hlk, ht, cons_x)
        dense(8, Hhk, Hlk, ht, cons_b)
    win_done = P.mark()
    yh = {}
    rt = rnorm(mat("ones512"), list(smc.done.values()))
    for j in range(4):
        i, w = K1R.take()
        v = P.do("V", lambda e, j=j, i=i: e.scalar_tensor_tensor(
            out=K1[:, i, :], in0=YC[:, j, :], scalar=col("g_out_conv", j), in1=rr[:, :], op0=ALU.mult, op1=ALU.mult),
            rt, yc_t, w)
        a, l = split(Hh[:, j, :], Hl[:, j, :], K1[:, i, :], v, win_done)
        K1R.give(i, a, l)
        yh[j] = [a, l]
    rr_free["t"] = v
    stY.close()
    yc_dead = [a, l, v]

    stA = ExitStack()
    TB = [acc, rr]
    PP = sbt(stA, "PP", [128, 2, T])
    PT = sbt(stA, "PT", [128, 2, T])
    YA = sbt(stA, "YA", [128, 8, 512])
    mn = sbt(stA, "mn", [128, 64])
    sx = sbt(stA, "sx", [128, 64])
    rx = sbt(stA, "rx", [128, 64])
    for e in "VAG":
        P.wait(e, yc_dead)
    P.wait("T", yc_dead)

    def attention(steps, names, qk, bias, vv, out, pre=None, post=None):
        PPb, PTb, mnb, sxb, rxb = names
        pp = Ring(2)
        pt = Ring(2)
        q = {}

        def stage0(s):
            if pre:
                pre(s)
            h, i = steps[s]
            W = 128 * (i + 1)
            nb = 1 if W <= 512 else 2
            b, bw = PB.take(nb)
            for c in range(nb):
                w = min(512, W - 512 * c)
                lh, rh, tk = qk(h, i, 512 * c, w)
                P.mm(lambda e, b=b, c=c, w=w, lh=lh, rh=rh: e.matmul(ps(b + c, w), lh, rh, start=True, stop=True), bw, tk)
            t = P.mark()
            p, pw = pp.take()
            bap, bt, brel = bias(h, i, W)
            v = P.do("V", lambda e: e.tensor_tensor_reduce(
                out=PPb[:, p, 0:W], in0=PS[:, 512 * b:512 * b + W], in1=bap, scale=-1.0, scalar=3.0e38,
                op0=ALU.add, op1=ALU.min, accum_out=mnb[:, s % 64:s % 64 + 1]), t, bt, pw)
            PB.give(b, v, k=nb)
            brel(v)
            a = P.do("A", lambda e: e.activation(PPb[:, p, 0:W], PPb[:, p, 0:W], ACT.Exp, bias=mnb[:, s % 64:s % 64 + 1],
                                                 scale=-1.0, accum_out=sxb[:, s % 64:s % 64 + 1]), v)
            q[s] = (W, nb, p, a)

        def stage1(s):
            W, nb, p, a = q[s]
            h, i = steps[s]
            b, bw = PB.take(nb)
            for c in range(i + 1):
                P.mm(lambda e, c=c: e.transpose(PS[:, 512 * b + 128 * c:512 * b + 128 * c + 128],
                                                PPb[:, p, 128 * c:128 * c + 128], ident), bw, a, t_cst)
            t = P.mark()
            pp.give(p, t)
            r = P.do("V", lambda e: e.reciprocal(rxb[:, s % 64:s % 64 + 1], sxb[:, s % 64:s % 64 + 1]), a)
            k, kw = pt.take()
            tt = []
            for c in range(nb):
                w = min(512, W - 512 * c)
                src = ps(b + c, w)
                dst = PTb[:, k, 512 * c:512 * c + w]
                if c == 0:
                    tt.append(P.do("A", lambda e, dst=dst, src=src: e.activation(dst, src, ACT.Copy), t, kw))
                else:
                    tt.append(P.do("V", lambda e, dst=dst, src=src: e.tensor_copy(dst, src), t, kw))
            PB.give(b, *tt, k=nb)
            q[s] = (k, tt, r)

        def stage2(s):
            h, i = steps[s]
            k, tt, r = q.pop(s)
            b, bw = PB.take()
            for c in range(i + 1):
                va, vt = vv(h, c)
                P.mm(lambda e, c=c, va=va: e.matmul(ps(b, 64), PTb[:, k, 128 * c:128 * c + 128], va,
                                                    start=(c == 0), stop=(c == i)), bw, tt, vt)
            t = P.mark()
            pt.give(k, t)
            oap, ow = out(h, i)
            v = P.do("V", lambda e: e.tensor_scalar(oap, ps(b, 64), rxb[:, s % 64:s % 64 + 1], None, ALU.mult), t, r, ow)
            PB.give(b, v)
            if post:
                post(s, v)

        n = len(steps)
        for s in range(n + 2):
            if s < n:
                stage0(s)
            if 1 <= s <= n:
                stage1(s - 1)
            if s >= 2:
                stage2(s - 2)

    tb_t = {}
    tb_free = {}

    def load_tb(h):
        if h < 8:
            tb_t[h] = P.dma("S", f"t{h % 2}", lambda e: e.dma_start(TB[h % 2][:, :], d["T1"][h]),
                            tb_free.get(h - 2), yc_dead, acc_free["t"])
    load_tb(0)
    load_tb(1)
    steps = [(h, i) for h in range(8) for i in range(8)]
    vlast = {}

    def qk1(h, i, c, w):
        r = slice(64 * (h % 2), 64 * (h % 2) + 64)
        return QT[r, h // 2, 128 * i:128 * i + 128], KT[r, h // 2, c:c + w], [x["t"] for x in qk_t]

    def bias1(h, i, W):
        def rel(v):
            tb_free[h] = v
            if i == 7:
                load_tb(h + 2)
        return TB[h % 2][:, T - W:T], tb_t[h], rel

    ya_t = {}

    def post1(s, v):
        ya_t[steps[s]] = v

    attention(steps, (PP, PT, mn, sx, rx), qk1, bias1,
              lambda h, c: (Vt[:, c, 64 * h:64 * h + 64], v_t),
              lambda h, i: (YA[:, i, 64 * h:64 * h + 64], None), post=post1)
    ss = sml[:, 0:8]
    for i in range(8):
        k, w = K1R.take()
        a = P.do("A", lambda e, i=i, k=k: e.activation(K1[:, k, 0:512], YA[:, i, :], ACT.Square,
                                                       accum_out=sml[:, i:i + 1]), [ya_t[h, i] for h in range(8)], w)
        K1R.give(k, a)
    a = P.do("A", lambda e: e.activation(sml[:, 8:16], ss, ACT.Sqrt, bias=col("eps6"), scale=1.0 / 512), a, t_cols)
    v = P.do("V", lambda e: e.reciprocal(sml[:, 16:24], sml[:, 8:16]), a)

    def tok_to_h(src, i, j0, w, pre, gain, eng="V", hw=None):
        b, bw = PB.take()
        for c in range(4):
            P.mm(lambda e, c=c: e.transpose(PS[:, 512 * b + 128 * c:512 * b + 128 * c + 128],
                                            src[:, 128 * c:128 * c + 128], ident), bw, w, t_cst)
        t = P.mark()
        pv = ps(b).rearrange("p (c n) -> p c n", c=4)
        k, kw = K1R.take()
        tmp = K1[:, k, 0:512].rearrange("p (c n) -> p c n", c=4)
        if gain is not None:
            v = P.do("V", lambda e: e.tensor_tensor(tmp, pv, gain, ALU.mult), t, kw)
        else:
            v = P.do("V", lambda e: e.tensor_copy(tmp, pv), t, kw)
        PB.give(b, v)
        a, l = split(Hh[:, j0:j0 + 4, 128 * i:128 * i + 128], Hl[:, j0:j0 + 4, 128 * i:128 * i + 128], tmp, v, hw, eng)
        K1R.give(k, a, l)
        return t, a, l

    ga = cols[:, COL["g_out_attn"]:COL["g_out_attn"] + 4].rearrange("p (c n) -> p c n", n=1).to_broadcast([128, 4, 128])
    yat = []
    for i in range(8):
        v2 = P.do("V", lambda e, i=i: e.tensor_scalar(YA[:, i, :], YA[:, i, :], sml[:, 16 + i:17 + i], None, ALU.mult), v, a)
        t, a3, l3 = tok_to_h(YA[:, i, :], i, 4, v2, None, ga, hw=win_done)
        yat += [a3, l3]
    for j in range(4, 8):
        yh[j] = yat
    acc_free["t"], rr_free["t"] = tb_free[6], tb_free[7]
    stA.close()
    stM.close()
    mix_dead = [t, a3, l3]

    def out_proj(name, src, srct, yh, dead):
        st = ExitStack()
        X = sbt(st, name, [128, 8, T])
        xt = [P.dma("S", f"x{k}", lambda e, k=k: e.dma_start(X[:, k, :], src[k]), dead, srct) for k in range(8)]
        sm = new_sum("G", acc_free["t"])
        xo = {}
        for m in range(8):
            def cons(half, b, tok, m=m):
                sl = slice(512 * half, 512 * half + 512)
                v = P.do("V", lambda e: e.tensor_tensor(X[:, m, sl], ps(b), X[:, m, sl], ALU.add), tok, xt[m])
                PB.give(b, v)
                sm.add(X[:, m, sl], sl, v)
                xo[m, half] = v
            dense(8, Hhk, Hlk, yh, cons)
        return st, X, sm, xo, P.mark()

    def ffn(X, gname, xo, sm, hdone, conv, last):
        rt = rnorm(mat("ones"), list(sm.done.values()))
        ht = norm_to_h(X, gname, rt, list(xo.values()), hdone)
        st = ExitStack()
        HGh = sbt(st, "HGh" + gname, [128, 5, T], F32R)
        HGl = sbt(st, "HGl" + gname, [128, 5, T], F32R)
        GB = sbt(st, "GB" + gname, [128, 2, T + 2])
        SG = sbt(st, "SG" + gname, [128, T])
        zp = P.do("V", lambda e: e.memset(GB[:, :, 0:2], 0.0), hdone)
        hg_free = [hdone]
        s = {"sg": None}
        gbf = [None, None]
        nsm = new_sum("G", acc_free["t"])
        nxo = {}
        for g, (fa, fb) in enumerate(GROUPS):
            hg_t = {}
            for f in range(fa, fb):
                z = f % 2

                def cons_g(half, b, tok, f=f, z=z):
                    if conv:
                        a = P.do("A", lambda e: e.activation(GB[:, z, 2 + 512 * half:514 + 512 * half], ps(b), ACT.Copy),
                                 tok, gbf[z], zp)
                        PB.give(b, a)
                        if half:
                            v = P.do("V", lambda e: e.tensor_scalar(SG[:, :], GB[:, z, 2:T + 2], col("ffn_conv_w", 44 + f),
                                                                    col("ffn_conv_b", f), ALU.mult, ALU.add), a, s["sg"])
                            v = P.do("V", lambda e: e.scalar_tensor_tensor(
                                out=SG[:, :], in0=GB[:, z, 1:T + 1], scalar=col("ffn_conv_w", 22 + f), in1=SG[:, :],
                                op0=ALU.mult, op1=ALU.add), v)
                            v = P.do("V", lambda e: e.scalar_tensor_tensor(
                                out=SG[:, :], in0=GB[:, z, 0:T], scalar=col("ffn_conv_w", f), in1=SG[:, :],
                                op0=ALU.mult, op1=ALU.add), v)
                            s["silu"] = P.do("A", lambda e: e.activation(GB[:, z, 2:T + 2], SG[:, :], ACT.Silu), v)
                            s["sg"] = s["silu"]
                    else:
                        a = P.do("A", lambda e: e.activation(GB[:, z, 2 + 512 * half:514 + 512 * half], ps(b), ACT.Silu),
                                 tok, gbf[z], zp)
                        PB.give(b, a)
                        s["silu"] = a

                def cons_u(half, b, tok, f=f, z=z, fa=fa):
                    sl = slice(512 * half, 512 * half + 512)
                    gs = GB[:, z, 2 + 512 * half:514 + 512 * half]
                    v = P.do("V", lambda e: e.tensor_tensor(gs, ps(b), gs, ALU.mult), tok, s["silu"])
                    PB.give(b, v)
                    a, l = split(HGh[:, f - fa, sl], HGl[:, f - fa, sl], gs, v, hg_free, eng="V")
                    gbf[z] = [a, l]
                    hg_t[f - fa, half] = [a, l]
                dense(8, Hhk, Hlk, ht, cons_g)
                dense(8, Hhk, Hlk, ht, cons_u)
            for m in range(8):
                def cons_d(half, b, tok, m=m, g=g):
                    sl = slice(512 * half, 512 * half + 512)
                    v = P.do("V", lambda e: e.tensor_tensor(X[:, m, sl], ps(b), X[:, m, sl], ALU.add), tok,
                             xo[m, half], nxo.get((m, half)))
                    PB.give(b, v)
                    nxo[m, half] = v
                    if g == len(GROUPS) - 1:
                        last(m, half, v, nsm)
                toks = {k: [hg_t[k, 0], hg_t[k, 1]] for k in range(fb - fa)}
                dense(fb - fa, hk(HGh), hk(HGl), toks, cons_d)
            hg_free = [P.mark()]
        st.close()
        return nsm, nxo, P.mark()

    def add_sq(X):
        def last(m, half, v, nsm):
            sl = slice(512 * half, 512 * half + 512)
            nsm.add(X[:, m, sl], sl, v)
        return last

    stX, X, sm, xo, hd = out_proj("X2", d["xT"], None, yh, mix_dead)
    sm, xo, hd = ffn(X, "g_ffn", xo, sm, hd, True, add_sq(X))

    rt = rnorm(mat("ones"), list(sm.done.values()))
    ht = norm_to_h(X, "g_ple", rt, list(xo.values()), hd)
    stP = ExitStack()
    PR = sbt(stP, "PR", [128, 2, T])
    Ph = sbt(stP, "Ph", [128, 2, T], F32R)
    Pl = sbt(stP, "Pl", [128, 2, T], F32R)
    SGP = sbt(stP, "SGP", [128, 2, T])
    pt = P.dma("S", "sp", lambda e: e.dma_start(PR[:, :, :], d["pT"]), hd, list(xo.values()), rt)
    pa, pl = split(Ph[:, :, :], Pl[:, :, :], PR[:, :, :], pt, hd)
    sgf = [None, None]
    nsm = new_sum("G", acc_free["t"])
    nxo = {}
    spt = []
    for m in range(8):
        z = m % 2
        s = {}

        def cons_g(half, b, tok, z=z):
            a = P.do("A", lambda e: e.activation(SGP[:, z, 512 * half:512 * half + 512], ps(b), ACT.Sigmoid), tok, sgf[z])
            PB.give(b, a)
            s["a"] = a

        def cons_p(half, b, tok, z=z, m=m):
            sl = slice(512 * half, 512 * half + 512)
            v = P.do("V", lambda e: e.tensor_tensor(SGP[:, z, sl], ps(b), SGP[:, z, sl], ALU.mult), tok, s["a"])
            PB.give(b, v)
            v = P.do("V", lambda e: e.tensor_tensor(X[:, m, sl], SGP[:, z, sl], X[:, m, sl], ALU.add), v, xo[m, half])
            sgf[z] = v
            nsm.add(X[:, m, sl], sl, v)
            nxo[m, half] = v
            if half:
                spt.append(P.dma("S", f"x{m}", lambda e: e.dma_start(d["spill"][m], X[:, m, :]), v))
        dense(8, Hhk, Hlk, ht, cons_g)
        dense(2, hk(Ph), hk(Pl), [pa, pl], cons_p)
    hd = P.mark()
    stP.close()

    rt = rnorm(mat("ones"), list(nsm.done.values()))
    ht = norm_to_h(X, "norm1_w_2", rt, list(nxo.values()), hd)
    stX.close()
    dead = [ht[7][0], ht[7][1]] + spt
    for e in "VAGT":
        P.wait(e, dead)
    stN = ExitStack()
    KA = sbt(stN, "KA", [128, T])
    VA = sbt(stN, "VA", [128, 8, 64])
    SC = sbt(stN, "SC", [128, 4224])
    OB = sbt(stN, "OB", [128, 4, T])
    IW = sbt(stN, "IW", [128, 8, 4])
    stI = ExitStack()
    IQ = sbt(stI, "IQ", [128, T])
    IK = sbt(stI, "IK", [128, T])
    CT = sbt(stI, "CT", [128, T])
    IWT = sbt(stI, "IWT", [128, T])
    wkv = sbt(stI, "wkv", [128, 192])
    rb = sbt(stI, "rb", [32, 8 + 384])
    RR = sbt(stI, "RR", [128, 8, 384])
    ct = {}
    tkv = P.dma("S", "rl", lambda e: e.dma_start(wkv[:, :], d["wkv"]), dead)
    trb = P.dma("S", "rb", lambda e: e.dma_start(rb[:, :], d["rb"]), dead)
    for h in range(8):
        b, bw = PB.take()
        P.mm(lambda e, b=b, h=h: e.matmul(ps(b, 384), rb[:, h:h + 1].to_broadcast([32, 128]), rb[:, 8:392],
                                          start=True, stop=True), bw, trb)
        t = P.mark()
        a = P.do("A", lambda e, b=b, h=h: e.activation(RR[:, h, :], ps(b, 384), ACT.Copy), t)
        PB.give(b, a)
    t = P.dma("S", "rb", lambda e: e.dma_start(d["rscr"], RR[:, :, :]), a)
    t_scr = t

    def copy_cons(dst, fn=None, eng="A", tag=None):
        def cons(half, b, tok):
            sl = slice(512 * half, 512 * half + 512)
            if eng == "A":
                v = P.do("A", lambda e: e.activation(dst[:, sl], ps(b), fn or ACT.Copy), tok, ct.get(tag + "f"))
            else:
                v = P.do("V", lambda e: e.tensor_copy(dst[:, sl], ps(b)), tok, ct.get(tag + "f"))
            PB.give(b, v)
            ct.setdefault(tag, [])
            ct[tag] = [v] if half == 0 else ct[tag] + [v]
        return cons

    dense(8, Hhk, Hlk, ht, copy_cons(IQ[:, :], tag="iq"))
    dense(8, Hhk, Hlk, ht, copy_cons(IK[:, :], tag="ik"))
    dense(8, Hhk, Hlk, ht, copy_cons(IWT[:, :], tag="iw"))
    b, bw = PB.take(2)
    for i in range(8):
        P.mm(lambda e, i=i: e.transpose(PS[:, 512 * b + 128 * i:512 * b + 128 * i + 128],
                                        IWT[:, 128 * i:128 * i + 128], ident), bw, ct["iw"])
    t = P.mark()
    iwv = PS[:, 512 * b:512 * b + 1024].rearrange("p (i n) -> p i n", i=8)[:, :, 0:4]
    t_iw = P.do("V", lambda e: e.tensor_scalar(IW[:, :, :], iwv, 0.5, None, ALU.mult), t)
    PB.give(b, t_iw, k=2)
    SOFF = {}
    at = 0
    for i in range(2, 8):
        SOFF[i] = at
        at += 128 * (i + 1)
    ct["sc"] = {}

    def index_scores(i):
        W = 128 * (i + 1)
        nb = 1 if W <= 512 else 2
        sc = SC[:, SOFF[i]:SOFF[i] + W]
        for h in range(4):
            b, bw = PB.take(nb)
            r = slice(32 * h, 32 * h + 32)
            for c in range(nb):
                w = min(512, W - 512 * c)
                P.mm(lambda e, c=c, w=w, r=r: e.matmul(ps(b + c, w), IQ[r, 128 * i:128 * i + 128],
                                                       IK[r, 512 * c:512 * c + w], start=True, stop=True),
                     bw, ct["iq"], ct["ik"])
            t = P.mark()
            k, kw = K1R.take()
            a = P.do("A", lambda e, k=k, b=b: e.activation(K1[:, k, 0:W], PS[:, 512 * b:512 * b + W], ACT.Relu,
                                                           scale=32.0 ** -0.5), t, kw)
            PB.give(b, a, k=nb)
            if h == 0:
                v = P.do("V", lambda e, k=k: e.tensor_scalar(sc, K1[:, k, 0:W], IW[:, i, 0:1], None, ALU.mult), a, t_iw)
            else:
                v = P.do("V", lambda e, k=k, h=h: e.scalar_tensor_tensor(
                    out=sc, in0=K1[:, k, 0:W], scalar=IW[:, i, h:h + 1], in1=sc, op0=ALU.mult, op1=ALU.add), a, v)
            K1R.give(k, v)
        d_ = sc[:, W - 128:W]
        v = P.do("V", lambda e: e.scalar_tensor_tensor(out=d_, in0=mat("adm"), scalar=1.0e8, in1=d_, op0=ALU.mult,
                                                       op1=ALU.add), v, t_cst)
        ct["sc"][i] = v

    cu = sml[:, 32:38].bitcast(I32)
    xm = sml[:, 38:44].bitcast(I32)
    cand = sml[:, 44:50]
    cnt = sml[:, 50:56]
    kb_ = sml[:, 56:62].bitcast(I32)
    thr = sml[:, 64:70]

    def topk():
        junk = acc[:, :].bitcast(mybir.dt.bfloat16)
        jt = [None, None]
        v = P.do("V", lambda e: e.memset(cu, 0))
        v = P.do("V", lambda e: e.memset(xm, -1), v)
        for bit in range(31, -1, -1):
            imm = (1 << bit) - (1 << 32 if bit == 31 else 0)
            if bit == 31:
                v = P.do("V", lambda e: e.memset(cand.bitcast(I32), 0), v)
            else:
                v = P.do("V", lambda e, imm=imm: e.tensor_scalar(cand.bitcast(I32), cu, imm, None, ALU.bitwise_or), v)
                v = P.do("V", lambda e: e.tensor_tensor(cand.bitcast(I32), cand.bitcast(I32), xm, ALU.bitwise_xor), v)
            for i in range(2, 8):
                W = 128 * (i + 1)
                c = P.do("V", lambda e, i=i, W=W: e.tensor_scalar(
                    junk[:, T * (i % 2):T * (i % 2) + W], SC[:, SOFF[i]:SOFF[i] + W], cand[:, i - 2:i - 1], None, ALU.is_ge, ALU.add,
                    accum_out=cnt[:, i - 2:i - 1]), v, ct["sc"][i], jt[i % 2])
                jt[i % 2] = c
            if bit == 31:
                v = P.do("V", lambda e: e.tensor_scalar(kb_, cnt, 255.5, -2147483648.0, ALU.is_ge, ALU.mult), c)
                v = P.do("V", lambda e: e.tensor_copy(cu, kb_), v)
                w_ = P.do("V", lambda e: e.tensor_scalar(cnt, cnt, 255.5, None, ALU.is_ge), v)
                w_ = P.do("V", lambda e: e.tensor_scalar(xm, cnt, -2147483647.0 - 1.0, None, ALU.mult), w_)
                w2 = P.do("V", lambda e: e.tensor_scalar(kb_, cnt, 1.0, None, ALU.subtract), w_)
                v = P.do("V", lambda e: e.tensor_tensor(xm, xm, kb_, ALU.bitwise_or), w2)
            else:
                v = P.do("V", lambda e, bit=bit: e.tensor_scalar(kb_, cnt, 255.5, float(1 << bit), ALU.is_ge, ALU.mult), c)
                v = P.do("V", lambda e: e.tensor_tensor(cu, cu, kb_, ALU.bitwise_or), v)
            yield
        v = P.do("V", lambda e: e.tensor_tensor(thr.bitcast(I32), cu, xm, ALU.bitwise_xor), v)
        ct["thr"] = v
        while True:
            yield

    for i in range(2, 8):
        index_scores(i)
    cn = []

    def cons_c(half, b, tok):
        cn.append(headnorm(half, b, tok, CT[:, 512 * half:512 * half + 512], col("kv_norm_w_2"), ones="ones128"))
    dense(8, Hhk, Hlk, ht, cons_c)
    flush()
    kn = []
    for half in range(2):
        b, bw = PB.take()
        P.mm(lambda e, b=b, half=half: e.matmul(ps(b), wkv[:, 0:128], CT[:, 512 * half:512 * half + 512],
                                                start=True, stop=True), bw, [x["t"] for x in cn], tkv)
        t = P.mark()
        flush()
        kn.append(headnorm(half, b, t, KA[:, 512 * half:512 * half + 512], col("k_norm_w_2")))
    b, bw = PB.take()
    for i in range(8):
        P.mm(lambda e, i=i: e.matmul(PS[:, 512 * b + 64 * i:512 * b + 64 * i + 64], CT[:, 128 * i:128 * i + 128],
                                     wkv[:, 128:192], start=True, stop=True), bw)
    t = P.mark()
    t_va = P.do("A", lambda e: e.activation(VA[:, :, :], ps(b).rearrange("p (i n) -> p i n", i=8), ACT.Copy), t)
    PB.give(b, t_va)
    flush()
    idead = [t_va, t] + [x["t"] for x in kn + cn] + [v for v in ct["sc"].values()] + [t_iw, t_scr]
    stI.close()
    stR = ExitStack()
    VB = sbt(stR, "VB", [128, 8, 128])
    DQ = sbt(stR, "DQ", [128, 1536])
    CS = sbt(stR, "CS", [128, 2, T])
    QR = sbt(stR, "QR", [128, T])
    KR = sbt(stR, "KR", [128, T])
    QD = sbt(stR, "QD", [128, T])
    RW = rr
    YT = sbt(stR, "YT", [128, 8, 128])
    GG = sbt(stR, "GG", [128, T])
    SD = sbt(stR, "SD", [128, 2, 256])
    KD = sbt(stR, "KD", [128, 2, 128])
    ST = sbt(stR, "ST", [128, 2, 64])
    bst = sbt(stR, "bst", [128, 16, 6])
    bag = sbt(stR, "bag", [128, 16, 2])
    rsd = sbt(stR, "rsd", [128, 16])
    for e in "VAGT":
        P.wait(e, idead)
    t_cs = P.dma("S", "sp", lambda e: e.dma_start(CS[:, :, :], d["cs"]), idead)
    t_dq = P.dma("S", "rl", lambda e: e.dma_start(DQ[:, :], d["dq"]), idead, rr_free["t"], acc_free["t"])
    P.wait("A", rr_free["t"])
    P.wait("V", acc_free["t"])
    tk = topk()
    vb_t = {"f": None}
    rel_t = {"qr": None, "kr": None, "qd": None, "gg": None, "rw": None, "yt": None}
    ob_t = []

    def rotary(dst, free):
        out = []
        for half in range(2):
            sl = slice(512 * half, 512 * half + 512)
            b, bw = PB.take()
            P.mm(lambda e, b=b, sl=sl: e.matmul(ps(b), mat("perm"), RW[:, sl], start=True, stop=True), bw, ct["rw"])
            t = P.mark()
            g = P.do("G", lambda e, sl=sl: e.tensor_tensor(dst[:, sl], RW[:, sl], CS[:, 0, sl], ALU.mult),
                     ct["rw"], t_cs, free)
            k, kw = K1R.take()
            v = P.do("V", lambda e, b=b, sl=sl, k=k: e.tensor_tensor(K1[:, k, 0:512], ps(b), CS[:, 1, sl], ALU.mult),
                     t, kw, t_cs)
            PB.give(b, v)
            g2 = P.do("G", lambda e, sl=sl, k=k: e.tensor_tensor(dst[:, sl], dst[:, sl], K1[:, k, 0:512], ALU.add), v, g)
            K1R.give(k, g2)
            out.append(g2)
        ct["rwf"] = [t, g]
        return out

    for j in range(4):
        dense(8, Hhk, Hlk, ht, copy_cons(RW[:, :], tag="rw"))
        qr = rotary(QR, rel_t["qr"])
        qdv = DQ[:, 1024 + 128 * j:1024 + 128 * j + 128].rearrange("p (a n) -> p a n", a=1).to_broadcast([128, 8, 128])
        qd = P.do("G", lambda e, qdv=qdv: e.tensor_tensor(QD[:, :].rearrange("p (a n) -> p a n", a=8),
                                                          QR[:, :].rearrange("p (a n) -> p a n", a=8), qdv, ALU.mult),
                  qr, rel_t["qd"], t_dq)
        next(tk)
        dense(8, Hhk, Hlk, ht, copy_cons(RW[:, :], tag="rw"))
        kr = rotary(KR, rel_t["kr"])
        next(tk)
        dense(8, Hhk, Hlk, ht, copy_cons(RW[:, :], tag="rw"))
        b, bw = PB.take(2)
        for c in range(8):
            P.mm(lambda e, b=b, c=c: e.transpose(PS[:, 512 * b + 128 * c:512 * b + 128 * c + 128],
                                                 RW[:, 128 * c:128 * c + 128], ident), bw, ct["rw"])
        t = P.mark()
        ct["rwf"] = [t]
        vbt = []
        for half in range(2):
            vbt.append(P.do("A", lambda e, b=b, half=half: e.activation(
                VB[:, 4 * half:4 * half + 4, :], ps(b + half).rearrange("p (c n) -> p c n", c=4), ACT.Copy),
                t, vb_t["f"]))
        PB.give(b, vbt[1], k=2)
        ct["ggf"] = rel_t["gg"]
        dense(8, Hhk, Hlk, ht, copy_cons(GG[:, :], fn=ACT.Silu, tag="gg"))
        for c in range(8):
            if c % 2:
                next(tk)
            sl = slice(128 * c, 128 * c + 128)
            z = c % 2
            b, bw = PB.take(2)
            for h in range(2):
                r = slice(64 * h, 64 * h + 64)
                P.mm(lambda e, b=b, h=h, r=r, sl=sl: e.matmul(ps(b + h, 128), KR[r, sl], QR[r, sl], start=True,
                                                              stop=True), bw, kr, qr)
            t = P.mark()
            sdv = SD[:, z, :].rearrange("p (h n) -> p h n", h=2)
            v_sd = P.do("V", lambda e, b=b, sdv=sdv, j=j: e.tensor_tensor(
                sdv, PS[:, 512 * b:512 * b + 1024].rearrange("p (h n) -> p h n", h=2)[:, :, 0:128],
                DQ[:, 256 * j:256 * j + 256].rearrange("p (h n) -> p h n", h=2), ALU.mult), t, ct.get(("sdf", z)), t_dq)
            PB.give(b, v_sd, k=2)
            b, bw = PB.take()
            P.mm(lambda e, b=b, sl=sl: e.transpose(ps(b, 128), KR[:, sl], ident), bw)
            t_kr = t = P.mark()
            for h in range(2):
                a_kd = P.do("A", lambda e, b=b, h=h, z=z, j=j: e.activation(
                    KD[:, z, 64 * h:64 * h + 64], ps(b, 128)[:, 64 * h:64 * h + 64], ACT.Copy,
                    scale=col("kdec", 2 * j + h)), t, ct.get(("kdf", z)))
            PB.give(b, a_kd)
            b, bw = PB.take(2)
            for h in range(2):
                r = slice(64 * h, 64 * h + 64)
                o = slice(512 * (b + h), 512 * (b + h) + 64)
                P.mm(lambda e, z=z, h=h, o=o, c=c, j=j: e.matmul(
                    PS[:, o], SD[:, z, 128 * h:128 * h + 128], VB[:, c, 64 * h:64 * h + 64],
                    start=True, stop=(c == 0)), bw, v_sd, vbt)
                if c:
                    P.mm(lambda e, z=z, h=h, o=o, r=r, sl=sl: e.matmul(
                        PS[:, o], QD[r, sl], ST[r, z, :], start=False, stop=True), qd, ct["st"])
            t_y = P.mark()
            ct["sdf", z] = t_y
            for h in range(2):
                v = P.do("V", lambda e, b=b, h=h, c=c: e.bn_stats(bst[:, 2 * c + h, :], ps(b + h, 64)), t_y)
                v_bag = P.do("V", lambda e, h=h, c=c: e.bn_aggr(bag[:, 2 * c + h, :], bst[:, 2 * c + h, :]), v)
            a_y = P.do("A", lambda e, b=b, c=c: e.activation(YT[:, c, :].rearrange("p (h n) -> p h n", h=2), PS[:, 512 * b:512 * b + 1024].rearrange("p (h n) -> p h n", h=2)[:, :, 0:64], ACT.Copy), v, t_y, rel_t["yt"])
            PB.give(b, v, a_y, k=2)
            if c < 7:
                b, bw = PB.take()
                P.mm(lambda e, b=b, z=z, c=c, j=j: e.matmul(ps(b, 128), KD[:, z, :], VB[:, c, :],
                                                            start=True, stop=True), bw, a_kd)
                t = P.mark()
                ct["kdf", z] = t
                sv = []
                for h in range(2):
                    r = slice(64 * h, 64 * h + 64)
                    o = slice(512 * b + 64 * h, 512 * b + 64 * h + 64)
                    if c == 0:
                        sv.append(P.do("V", lambda e, r=r, o=o, z=z: e.tensor_copy(ST[r, 1 - z, :], PS[r, o]), t, t_y))
                    else:
                        sv.append(P.do("V", lambda e, r=r, o=o, z=z, j=j: e.scalar_tensor_tensor(
                            out=ST[r, 1 - z, :], in0=ST[r, z, :], scalar=cols[r, COL["g128"] + j:COL["g128"] + j + 1],
                            in1=PS[r, o], op0=ALU.mult, op1=ALU.add), t, t_y, ct["st"]))
                PB.give(b, *sv)
                ct["st"] = sv
        rel_t["qr"] = rel_t["kr"] = rel_t["qd"] = vb_t["f"] = t_y
        vg = P.do("V", lambda e: e.tensor_copy(rsd[:, :], bag[:, :, 1]), v_bag)
        a = P.do("A", lambda e: e.activation(rsd[:, :], rsd[:, :], ACT.Sqrt, bias=col("eps5")), vg)
        v = P.do("V", lambda e: e.reciprocal(rsd[:, :], rsd[:, :]), a)
        b, bw = PB.take(2)
        for c in range(8):
            for h in range(2):
                v2 = P.do("V", lambda e, c=c, h=h: e.tensor_scalar(
                    YT[:, c, 64 * h:64 * h + 64], YT[:, c, 64 * h:64 * h + 64], bag[:, 2 * c + h, 0:1],
                    rsd[:, 2 * c + h:2 * c + h + 1], ALU.subtract, ALU.mult), v, a_y)
            P.mm(lambda e, b=b, c=c: e.transpose(PS[:, 512 * b + 128 * c:512 * b + 128 * c + 128], YT[:, c, :], ident),
                 bw, v2)
        t = P.mark()
        rel_t["yt"] = t
        for half in range(2):
            sl = slice(512 * half, 512 * half + 512)
            k, kw = K1R.take()
            a = P.do("A", lambda e, b=b, half=half, k=k, j=j: e.activation(
                K1[:, k, 0:512], ps(b + half), ACT.Identity, bias=col("ret_gn_b_2", j), scale=col("ret_gn_w_2", j)), t, kw)
            v = P.do("V", lambda e, k=k, sl=sl, j=j: e.tensor_tensor(OB[:, j, sl], K1[:, k, 0:512], GG[:, sl], ALU.mult),
                     a, ct["gg"])
            K1R.give(k, v)
            ob_t.append(v)
        PB.give(b, a, k=2)
        rel_t["gg"] = v
    ret_dead = [P.mark(), a, v, qd, qr, kr, t_kr]
    stR.close()
    QA = sbt(stN, "QA", [128, 4, T])
    BN = sbt(stN, "BN", [128, 8, 256])
    for e in "VAGT":
        P.wait(e, ret_dead)
    r0 = d["rscr"]
    rsrc = bass.AP(tensor=r0.tensor, offset=127, ap=[[8 * 384 - 1, 128], [384, 8], [1, 256]])
    t_bn = P.dma("S", "rb", lambda e: e.dma_start(BN[:, :, :], rsrc), t_scr, ret_dead)
    qa_t = []
    for j in range(4):
        def cons(half, b, tok, j=j):
            qa_t.append(headnorm(half, b, tok, QA[:, j, 512 * half:512 * half + 512], gq2))
        dense(8, Hhk, Hlk, ht, cons)
        next(tk)
    flush()
    win_done = P.mark()
    for _ in range(33):
        next(tk)
    yh = {}
    for j in range(4):
        a, l = split(Hh[:, 4 + j, :], Hl[:, 4 + j, :], OB[:, j, :], ob_t, win_done, eng="G")
        yh[4 + j] = [a, l]
    rdead = [win_done, a, l, v] + [x["t"] for x in qa_t]

    stA = ExitStack()
    MM = sbt(stA, "MM", [128, 2, T])
    MN = sbt(stA, "MN", [128, 2, 256])
    SE = [acc, rr]
    PP2 = OB[:, 0:2, :]
    PT2 = OB[:, 2:4, :]
    YA2 = sbt(stA, "YA2", [128, 2, 512])
    mn2 = sbt(stA, "mn2", [128, 64])
    sx2 = sbt(stA, "sx2", [128, 64])
    rx2 = sbt(stA, "rx2", [128, 64])
    one = sbt(stA, "one", [128, T])
    for e in "VAGT":
        P.wait(e, rdead)
    t_one = P.do("V", lambda e: e.memset(one[:, :], 1.0))
    need = sml[:, 72:80]
    mt = {}
    mm_free = [None, None]

    def mask(i):
        W = 128 * (i + 1)
        nr = min(256, W)
        if i < 2:
            v = P.do("V", lambda e: e.memset(MN[:, i % 2, 0:nr], 0.0), mt.get(("mn", i % 2)))
            v = P.do("V", lambda e: e.tensor_copy(MN[:, i % 2, nr - 128:nr], mat("adm")), v)
            mt[i] = v
            return
        sc = SC[:, SOFF[i]:SOFF[i] + W]
        th = thr[:, i - 2:i - 1]
        eq, rk = SE[0][:, 0:W], SE[1][:, 0:W]
        v1 = P.do("V", lambda e: e.tensor_scalar(eq, sc, th, None, ALU.is_equal), ct["thr"])
        v2 = P.do("V", lambda e: e.tensor_tensor_scan(rk, one[:, 0:W], eq, 0.0, ALU.mult, ALU.add), v1, t_one)
        v3 = P.do("V", lambda e: e.tensor_scalar(sc, sc, th, None, ALU.is_gt, ALU.add, accum_out=need[:, i:i + 1]), v1)
        v4 = P.do("V", lambda e: e.tensor_scalar(need[:, i:i + 1], need[:, i:i + 1], -1.0, 256.0, ALU.mult, ALU.add), v3)
        v5 = P.do("V", lambda e: e.scalar_tensor_tensor(out=eq, in0=rk, scalar=need[:, i:i + 1], in1=eq,
                                                        op0=ALU.is_le, op1=ALU.mult), v4, v2)
        v6 = P.do("V", lambda e: e.tensor_tensor(eq, eq, sc, ALU.add), v5)
        v7 = P.do("V", lambda e: e.tensor_scalar(MM[:, 0, 0:W], eq, -NEG, NEG, ALU.mult, ALU.add), v6, mm_free)
        v8 = P.do("V", lambda e: e.tensor_scalar(MM[:, 1, 0:W], eq, -NEG, NEG, ALU.mult, ALU.add), v6, mm_free)
        mt[i] = P.do("V", lambda e: e.tensor_copy(MN[:, i % 2, :], MM[:, 0, W - 256:W]), v7, v8, mt.get(("mn", i % 2)))

    steps2 = [(h, i) for i in range(8) for h in range(8)]
    bt = {}

    def pre2(s):
        h, i = steps2[s]
        if h == 0:
            mask(i)
        z = h % 2
        W = 128 * (i + 1)
        nr = min(256, W)
        g = P.do("G", lambda e: e.tensor_tensor(MM[:, z, W - nr:W], MN[:, i % 2, 0:nr], BN[:, h, 256 - nr:256], ALU.add),
                 mt[i], mm_free[z], t_bn)
        mt["mn", i % 2] = g
        bt[s] = g
        ct["s"] = s

    def bias2(h, i, W):
        z = h % 2

        def rel(v):
            mm_free[z] = v
        return MM[:, z, 0:W], bt[ct["s"]], rel

    def qk2(h, i, c, w):
        r = slice(64 * (h % 2), 64 * (h % 2) + 64)
        return QA[r, h // 2, 128 * i:128 * i + 128], KA[r, c:c + w], [x["t"] for x in qa_t + kn]

    ya_f = [None, None]
    ya_t = []
    yat = []

    def post2(s, v):
        h, i = steps2[s]
        ya_t.append(v)
        if h == 7:
            t, a, l = tok_to_h(YA2[:, i % 2, :], i, 0, ya_t[-8:], None, None, hw=win_done)
            ya_f[i % 2] = t
            yat.extend([a, l])

    attention(steps2, (PP2, PT2, mn2, sx2, rx2), qk2, bias2,
              lambda h, c: (VA[:, c, :], t_va),
              lambda h, i: (YA2[:, i % 2, 64 * h:64 * h + 64], ya_f[i % 2]), pre=pre2, post=post2)
    for j in range(4):
        yh[j] = yat
    acc_free["t"] = rr_free["t"] = ya_t[-1]
    stA.close()
    stN.close()
    dead = [yat[-1], yat[-2], P.mark(), ya_t[-1], yh[7], bt[63]]
    stX, X, sm, xo, hd = out_proj("X3", d["spill"], spt, yh, dead)
    outs = []

    def last(m, half, v, nsm):
        if half:
            outs.append(P.dma("S", "out", lambda e: e.dma_start(d["out"][m], X[:, m, :]), v))
    sm, xo, hd = ffn(X, "norm2_w_2", xo, sm, hd, False, last)
    P.wait("S", outs[-1])
    assert ws["use"] == len(units), (ws, len(units))

    stX.close()
    ctx.close()


def _consts(np):
    f = np.float32
    p = np.arange(128)
    m = {}
    m["ones"] = np.full((128, 128), 1.0 / 1024, f)
    m["ones128"] = np.full((128, 128), 1.0 / 128, f)
    m["bd"] = ((p[:, None] // 64) == (p[None, :] // 64)).astype(f) / 64
    m["ident"] = np.eye(128, dtype=f)
    pm = np.zeros((128, 128), f)
    for b in (0, 64):
        for i in range(32):
            pm[b + 32 + i, b + i] = -1.0
            pm[b + i, b + 32 + i] = 1.0
    m["perm"] = pm
    m["adm"] = np.where((p[:, None] < 64) & (p[None, :] >= 64), f(NEG), f(0)).astype(f)
    h = np.arange(8)
    lg = np.log1p(-(2.0 ** (-5.0 - h)))
    D = np.zeros((128, 8, 128), np.float64)
    rel = p[None, :] - p[:, None]
    for n in range(8):
        D[:, n, :] = np.where(rel >= 0, np.exp(np.maximum(rel, 0) * lg[n]), 0.0) * 0.125
    m["D"] = D.reshape(128, 1024).astype(f)
    qd = np.zeros((128, 4, 128), np.float64)
    for j in range(4):
        for half in range(2):
            qd[64 * half:64 * half + 64, j, :] = np.exp((p + 1.0) * lg[2 * j + half])[None, :]
    m["qdec"] = qd.reshape(128, 512).astype(f)
    m["ones512"] = np.full((128, 128), 1.0 / 512, f)
    mats = np.concatenate([m[n] for n, _ in MATS], axis=1)
    dq = np.concatenate([m["D"], m["qdec"]], axis=1)
    kdec = (np.exp((127.0 - p)[:, None] * lg[None, :]) * 0.125).astype(f)
    g128 = np.zeros((128, 4), f)
    for j in range(4):
        for half in range(2):
            g128[64 * half:64 * half + 64, j] = np.exp(128 * lg[2 * j + half])
    dist = 896 + p[:, None] - np.arange(1024)[None, :]
    c = ((dist <= 128).astype(int) + ((dist % 4 == 0) & (dist <= 512)) + (dist % 16 == 0)) * (dist >= 0)
    base = np.where(c > 0, np.log(np.maximum(c, 1)), NEG)
    T1 = np.stack([np.where(c > 0, base - (2.0 ** -(n + 1.0)) * dist, NEG) for n in range(8)]).astype(f)
    inv = (10000.0 ** (-np.arange(32, dtype=np.float64) / 32)).astype(f)
    ang = (np.arange(1024, dtype=f)[None, :] * inv[p % 32][:, None]).astype(f).astype(np.float64)
    cs = np.stack([np.cos(ang), np.sin(ang)], axis=1).astype(f)
    rel = np.arange(384) - 255
    n = np.abs(rel)
    nf = np.maximum(n, 1).astype(f)
    large = 8 + (np.log(nf / f(8)) / f(np.log(16.0)) * f(8)).astype(np.int32)
    bucket = np.where(rel > 0, 16, 0) + np.where(n < 8, n, np.minimum(large, 15))
    oh = (np.arange(32)[:, None] == bucket[None, :]).astype(f)
    oh[15, :] -= 1.0
    return mats, dq, kdec, g128, T1, cs, oh


def kernel(**inputs):
    import numpy as np
    import concourse.bacc as _bacc
    from concourse.bass_utils import run_bass_kernel_spmd as _run

    x = {k: np.asarray(v) for k, v in inputs.items()}
    f = np.float32
    mats, dq, kdec, g128, T1, cs, oh = _consts(np)

    def fm(w):
        K, N = w.shape
        return w.reshape(K // 128, 128, N // 128, 128).transpose(2, 1, 0, 3).reshape(N // 128, 128, K)

    def tm(w):
        return w.reshape(4, 2, 128, 512).transpose(0, 2, 1, 3).reshape(4, 128, 1024)

    w1, w2 = x["w_in"][0], x["w_in_2"][0]
    a = {}
    a["xT"] = x["x"][0].T.reshape(8, 128, 1024)
    a["pT"] = x["p"][0, 0].T.reshape(2, 128, 1024).transpose(1, 0, 2)
    a["wqk1"] = fm(np.concatenate([w1[:, 2048:2560], w1[:, 1536:2048]], axis=1))
    a["wv1"] = tm(w1[:, 2560:3072])
    wb, wc, wx = w1[:, 0:512], w1[:, 512:1024], w1[:, 1024:1536]
    a["wc1"] = fm(np.concatenate([w[:, 128 * j:128 * j + 128] for j in range(4) for w in (wc, wx, wb)], axis=1))
    a["wo1"] = fm(x["w_out"][0])
    a["wg1"], a["wu1"] = fm(x["w_gate"][0]), fm(x["w_up"][0])
    a["wd1"] = fm(x["w_down"][0])
    a["wpg"], a["wpp"] = fm(x["w_ple_gate"][0]), fm(x["w_ple_proj"][0])
    o = np.cumsum([0, 512, 128, 128, 32, 4, 512, 512, 512, 512])
    qa, ckv, iq, ik, iw, qb, kb, vb, gb = (w2[:, o[n]:o[n + 1]] for n in range(9))
    parts = [iq, ik, ik, ik, ik, iw, np.zeros((1024, 124), f), ckv]
    for j in range(4):
        s = slice(128 * j, 128 * j + 128)
        parts += [qb[:, s], kb[:, s], vb[:, s], gb[:, s]]
    parts += [qa]
    a["wi2"] = fm(np.concatenate(parts, axis=1))
    a["wo2"] = fm(x["w_out_2"][0])
    a["wg2"], a["wu2"], a["wd2"] = fm(x["w_gate_2"][0]), fm(x["w_up_2"][0]), fm(x["w_down_2"][0])
    uk = x["w_uk_2"][0]
    a["wkv"] = np.concatenate([uk, uk, x["w_uv_2"][0]], axis=1)
    a["rb"] = np.concatenate([x["rel_bias_2"], oh], axis=1)
    a["T1"], a["cs"], a["mats"], a["dq"] = T1, cs, mats, dq

    def pp(v):
        return v.reshape(-1, 128).T

    c = {n: pp(x[n][0]) for n in ("g_mix", "g_ffn", "g_ple", "norm1_w_2", "norm2_w_2", "g_out_conv", "g_out_attn",
                                  "kv_norm_w_2", "ret_gn_w_2", "ret_gn_b_2")}
    c["conv_w"], c["conv_b"] = pp(x["conv_w"][0].reshape(-1)), pp(x["conv_b"][0])
    c["ffn_conv_w"], c["ffn_conv_b"] = pp(x["ffn_conv_w"][0].reshape(-1)), pp(x["ffn_conv_b"][0])
    for n in ("q_norm_g", "k_norm_g", "q_norm_w_2", "k_norm_w_2"):
        c[n] = np.concatenate([x[n][0], x[n][0]])[:, None]
    c["kdec"], c["g128"] = kdec, g128
    c["eps6"], c["eps5"] = np.full((128, 1), 1e-6, f), np.full((128, 1), 1e-5, f)
    a["cols"] = np.concatenate([c[n] for n, _ in COLS], axis=1)

    nc = _bacc.Bacc("TRN2", target_bir_lowering=False, num_devices=1)
    arrays, d = {}, {}
    for n, v in a.items():
        v = np.ascontiguousarray(v)
        assert v.dtype == f, n
        arrays["in_" + n] = v
        d[n] = nc.dram_tensor("in_" + n, v.shape, F32, kind="ExternalInput").ap()
    d["out"] = nc.dram_tensor("out_0", (8, 128, 1024), F32, kind="ExternalOutput").ap()
    d["spill"] = nc.dram_tensor("spill", (8, 128, 1024), F32, kind="Internal").ap()
    d["rscr"] = nc.dram_tensor("rscr", (128, 8, 384), F32, kind="Internal").ap()
    build(nc, d)
    r = _run(nc, [arrays], core_ids=[0])
    return np.ascontiguousarray(r.results[0]["out_0"].reshape(1024, 1024).T)[None]
```

```python
from contextlib import ExitStack

import concourse.bass as bass
from concourse import mybir

ALU = mybir.AluOpType
ACT = mybir.ActivationFunctionType
F32 = mybir.dt.float32
F32R = mybir.dt.float32r
I32 = mybir.dt.int32
NEG = -1.0e30

T = 1024
NH = 8
GROUPS = [(0, 5), (5, 10), (10, 14), (14, 18), (18, 22)]
NF = 22

COLS = [("g_mix", 8), ("g_ffn", 8), ("g_ple", 8), ("norm1_w_2", 8), ("norm2_w_2", 8),
        ("conv_w", 12), ("conv_b", 4), ("ffn_conv_w", 66), ("ffn_conv_b", 22),
        ("g_out_conv", 4), ("g_out_attn", 4), ("q_norm_g", 1), ("k_norm_g", 1),
        ("q_norm_w_2", 1), ("k_norm_w_2", 1), ("kv_norm_w_2", 1), ("ret_gn_w_2", 4), ("ret_gn_b_2", 4),
        ("kdec", 8), ("g128", 4), ("eps6", 1), ("eps5", 1)]
COL = {}
_at = 0
for _n, _w in COLS:
    COL[_n] = _at
    _at += _w
NCOL = _at

MATS = [("ident", 128), ("perm", 128), ("adm", 128), ("sel", 128), ("col1", 5)]
MAT = {}
_at = 0
for _n, _w in MATS:
    MAT[_n] = (_at, _w)
    _at += _w
NMAT = _at


class Prog:

    def __init__(self, nc, sems):
        self.sems = sems
        self.eng = {"V": nc.vector, "A": nc.scalar, "T": nc.tensor, "G": nc.gpsimd, "S": nc.sync}
        self.n = {s: 0 for s in sems}
        self.seen = {e: {} for e in "VATGS"}
        self.last = None

    def wait(self, e, *toks):
        for t in toks:
            if t is None:
                continue
            if isinstance(t, list):
                self.wait(e, *t)
                continue
            s, v = t
            if self.seen[e].get(s, 0) < v:
                self.seen[e][s] = v
                self.eng[e].wait_ge(self.sems[s], v)

    def do(self, e, fn, *toks):
        self.wait(e, *toks)
        self.n[e] += 1
        fn(self.eng[e]).then_inc(self.sems[e], 1)
        return (e, self.n[e])

    def mm(self, fn, *toks):
        self.wait("T", *toks)
        self.last = fn(self.eng["T"])

    def mark(self):
        if self.last is not None:
            self.n["T"] += 1
            self.last.then_inc(self.sems["T"], 1)
            self.last = None
        return ("T", self.n["T"])

    def dma(self, e, s, fn, *toks):
        self.wait(e, *toks)
        self.n[s] += 16
        fn(self.eng[e]).then_inc(self.sems[s], 16)
        return (s, self.n[s])


class Ring:

    def __init__(self, n):
        self.n, self.clock, self.free, self.since = n, n, [[] for _ in range(n)], list(range(n))

    def take(self, k=1):
        at = [i for i in range(0, self.n, k) if all(self.free[j] is not None for j in range(i, i + k))]
        assert at, "buffers still held"
        i = min(at, key=lambda i: max(self.since[i:i + k]))
        w = []
        for j in range(i, i + k):
            w += self.free[j]
            self.free[j] = None
        return i, w

    def give(self, i, *toks, k=1):
        for j in range(i, i + k):
            assert self.free[j] is None
            self.free[j] = list(toks)
            self.since[j] = self.clock
            self.clock += 1


def build(nc, d):
    ctx = ExitStack()
    used = set()

    def sbt(stack, name, shape, dt=F32):
        assert name not in used
        used.add(name)
        return stack.enter_context(nc.sbuf_tensor(name, shape, dt))

    DS = ["w0", "w1", "w2", "cst", "col", "x0", "x1", "x2", "x3", "x4", "x5", "x6", "x7", "y0", "y1", "y2", "y3", "y4", "y5", "y6", "y7", "z0", "z1", "q0", "q1", "q2", "q3", "b0", "b1", "b2", "b3", "t0", "t1", "sp", "rb", "rl", "out"]
    sems = {s: ctx.enter_context(nc.semaphore("s_" + s)) for s in list("VATG") + DS}
    P = Prog(nc, sems)
    PS = ctx.enter_context(nc.psum_tensor("PS", [128, 4096], F32))
    PB = Ring(8)

    def ps(b, n=512):
        return PS[:, 512 * b:512 * b + n]

    Hh = sbt(ctx, "Hh", [128, 8, T], F32R)
    Hl = sbt(ctx, "Hl", [128, 8, T], F32R)
    Wr = sbt(ctx, "Wr", [128, 3, 1024])
    Wh = sbt(ctx, "Wh", [128, 3, 1024], F32R)
    Wl = sbt(ctx, "Wl", [128, 3, 1024], F32R)
    acc = sbt(ctx, "acc", [128, T])
    rr = sbt(ctx, "rr", [128, T])
    K1 = sbt(ctx, "K1", [128, 4, 512])
    cols = sbt(ctx, "cols", [128, NCOL])
    mats = sbt(ctx, "mats", [128, NMAT])
    sml = sbt(ctx, "sml", [128, 512])
    K1R = Ring(4)

    def col(name, j=0):
        return cols[:, COL[name] + j:COL[name] + j + 1]

    def mat(name, j=0, n=None):
        at, w = MAT[name]
        n = w if n is None else n
        return mats[:, at + j:at + j + n]

    ident = mat("ident")
    gq1, gq2 = sml[:, 100:101], sml[:, 101:102]
    ident = mat("ident")
    gq1, gq2 = sml[:, 100:101], sml[:, 101:102]

    units = []
    units += [(d["wqk1"], n, 1024) for n in range(8)]
    units += [(d["wv1"], n, 1024) for n in range(4)]
    units += [(d["wc1"], n, 1024) for n in range(12)]
    units += [(d["wo1"], n, 1024) for n in range(8)]

    def ffn_units(g, u, dn):
        out = []
        for a, b in GROUPS:
            for f in range(a, b):
                out += [(g, f, 1024), (u, f, 1024)]
            out += [(dn, m, (a, b)) for m in range(8)]
        return out
    units += ffn_units(d["wg1"], d["wu1"], d["wd1"])
    for m in range(8):
        units += [(d["wpg"], m, 1024), (d["wpp"], m, 256)]
    units += [(d["wi2"], n, 1024) for n in range(23)]
    units += [(d["wo2"], n, 1024) for n in range(8)]
    units += ffn_units(d["wg2"], d["wu2"], d["wd2"])

    raw_t, raw_free, cv_t, w_free = {}, {}, {}, {}
    ws = {"load": 0, "conv": 0, "use": 0}

    def ncols(n):
        return n if isinstance(n, int) else 128 * (n[1] - n[0])

    def load_unit():
        u = ws["load"]
        ws["load"] += 1
        if u >= len(units):
            return
        src, i, n = units[u]
        s = u % 3
        w = ncols(n)
        ap = src[i, :, 0:w] if isinstance(n, int) else src[i, :, 128 * n[0]:128 * n[1]]
        raw_t[u] = P.dma("S", f"w{s}", lambda e: e.dma_start(Wr[:, s, 0:w], ap), raw_free.get(u - 3))

    def conv_unit():
        u = ws["conv"]
        ws["conv"] += 1
        if u >= len(units):
            return
        w = ncols(units[u][2])
        s = u % 3
        a = P.do("A", lambda e: e.activation(Wh[:, s, 0:w], Wr[:, s, 0:w], ACT.Copy), raw_t[u], w_free.get(u - 3))
        g = P.do("G", lambda e: e.tensor_tensor(Wl[:, s, 0:w], Wr[:, s, 0:w], Wh[:, s, 0:w].bitcast(F32),
                                                ALU.subtract), a)
        raw_free[u] = g
        cv_t[u] = [a, g]

    def use_unit():
        u = ws["use"]
        ws["use"] += 1
        while ws["conv"] <= min(u + 1, len(units) - 1) and (ws["conv"] < 3 or ws["conv"] - 3 in w_free):
            conv_unit()
            load_unit()
        assert ws["conv"] > u
        return u, u % 3, cv_t[u]

    def done_unit(u, tok):
        w_free[u] = tok

    later = []
    bg, bg2 = [], []

    def flush():
        while later:
            later.pop(0)()

    def run_later(n):
        for _ in range(n):
            later.pop(0)()

    def tick():
        for q, n in ((bg, 1), (bg2, 2)):
            for _ in range(n):
                if q:
                    try:
                        next(q[0])
                    except StopIteration:
                        q.pop(0)

    def drain():
        while bg:
            tick()

    def tk_of(xt, k, half):
        if not isinstance(xt, dict):
            return xt
        return xt[k, half] if (k, half) in xt else xt[k]

    def dense(nk, xh, xl, xt, consumer, halves=(0, 1), ticks=True):
        u, s, wt = use_unit()
        for half in halves:
            pend = len(later)
            b, bw = PB.take()
            for k in range(nk):
                xk = tk_of(xt, k, half)
                for n, (wa, xa) in enumerate(((Wl, xh), (Wh, xl), (Wh, xh))):
                    P.mm(lambda e, b=b, wa=wa, xa=xa, k=k, half=half, n=n: e.matmul(
                        ps(b), wa[:, s, 128 * k:128 * k + 128], xa(k, half),
                        start=(k == 0 and n == 0), stop=(k == nk - 1 and n == 2)), wt, bw, xk)
                if ticks and k % 3 == 2:
                    tick()
            tok = P.mark()
            run_later(pend)
            consumer(half, b, tok)
            if ticks:
                tick()
        done_unit(u, tok)

    def hk(t):
        return lambda k, half: t[:, k, 512 * half:512 * half + 512]

    Hhk, Hlk = hk(Hh), hk(Hl)

    def dense_tok(xt, consumer):
        flush()
        banks = [PB.take() for _ in range(8)]
        for kg in range(4):
            u, s, wt = use_unit()
            for i in range(8):
                b, bw = banks[i]
                for k2 in range(2):
                    k = 2 * kg + k2
                    for n, (wa, xa) in enumerate(((Wl, Hh), (Wh, Hl), (Wh, Hh))):
                        P.mm(lambda e, b=b, wa=wa, xa=xa, k=k, k2=k2, i=i, n=n, s=s: e.matmul(
                            ps(b), xa[:, k, 128 * i:128 * i + 128], wa[:, s, 512 * k2:512 * k2 + 512],
                            start=(k == 0 and n == 0), stop=(k == 7 and n == 2)), wt, bw, tk_of(xt, k, i // 4))
                if kg == 3:
                    consumer(i, b, P.mark())
            done_unit(u, P.mark())

    class Sum:
        def __init__(self, eng="G"):
            self.t, self.first, self.eng = None, True, eng

        def add(self, x, sl, tok, fast=False):
            key = (sl.start, sl.stop)
            if key not in self.done:
                self.done[key] = P.do("A", lambda e: e.activation(acc[:, sl], x, ACT.Square), tok, self.prev)
                return self.done[key]
            i, w = K1R.take()
            n = sl.stop - sl.start
            a = P.do("A", lambda e: e.activation(K1[:, i, 0:n], x, ACT.Square), tok, w)
            g = P.do("V" if fast else self.eng, lambda e: e.tensor_tensor(acc[:, sl], acc[:, sl], K1[:, i, 0:n], ALU.add),
                     a, self.done[key])
            K1R.give(i, g)
            self.done[key] = g
            return a

    def new_sum(eng="G", prev=None):
        s = Sum(eng)
        s.done, s.prev = {}, prev
        return s

    acc_free = {"t": None}
    rr_free = {"t": None}

    def rnorm(j, toks):
        b, bw = PB.take()
        for i in range(8):
            P.mm(lambda e, i=i: e.matmul(PS[:, 512 * b + i:512 * b + i + 1], acc[:, 128 * i:128 * i + 128],
                                         mat("col1", j, 1), start=True, stop=True), bw, toks, t_cst)
        t = P.mark()
        acc_free["t"] = t
        a = P.do("A", lambda e: e.activation(sml[:, 104:112], ps(b, 8), ACT.Sqrt, bias=col("eps6")), t, t_cols,
                 rn_free["t"])
        PB.give(b, a)
        v = P.do("V", lambda e: e.reciprocal(sml[:, 112:120], sml[:, 104:112]), a, rn_free["t"])
        b, bw = PB.take(2)
        for i in range(8):
            P.mm(lambda e, i=i: e.matmul(PS[:, 512 * b + 128 * i:512 * b + 128 * i + 128],
                                         sml[:, 112 + i:113 + i].to_broadcast([128, 128]), ident,
                                         start=True, stop=True), bw, v, t_cst)
        t = P.mark()
        rn_free["t"] = t
        return b, t

    rn_free = {"t": None}

    def split(dh, dl, src, tok, w, eng="V"):
        a = P.do("A", lambda e: e.activation(dh, src, ACT.Copy), tok, w)
        v = P.do(eng, lambda e: e.tensor_tensor(dl, src, dh.bitcast(F32), ALU.subtract), a, tok, w)
        return a, v

    def norm_to_h(X, gname, rn, xtok, hw, tiles=range(8), give=True):
        b, rt = rn
        out = {}
        for half in range(2):
            sl = slice(512 * half, 512 * half + 512)
            for k in tiles:
                i, w = K1R.take()
                v = P.do("V", lambda e, k=k, i=i, half=half, sl=sl: e.scalar_tensor_tensor(
                    out=K1[:, i, :], in0=X(k)[:, sl], scalar=col(gname, k), in1=ps(b + half), op0=ALU.mult, op1=ALU.mult),
                    rt, xtok(k, half), w)
                a, l = split(Hh[:, k, sl], Hl[:, k, sl], K1[:, i, :], v, hw, eng="V" if k % 3 == 0 else "G")
                K1R.give(i, a, l)
                out[k, half] = [a, l]
            if give:
                PB.give(b + half, v)
        return out

    hn = Ring(3)

    def headnorm(half, b, tok, out, gcol, one=False):
        i, w = K1R.take()
        sq = K1[:, i, :]
        nh, cj = (1, 3) if one else (2, 1)
        a0 = P.do("A", lambda e: e.activation(out, ps(b), ACT.Copy), tok)
        a = P.do("A", lambda e: e.activation(sq, ps(b), ACT.Square), tok, w)
        PB.give(b, a)
        res = {}

        def second():
            z, zw = hn.take()
            s0 = 128 + 16 * z
            b2, bw = PB.take()
            for t4 in range(4):
                P.mm(lambda e, t4=t4: e.matmul(PS[:, 512 * b2 + nh * t4:512 * b2 + nh * t4 + nh],
                                               sq[:, 128 * t4:128 * t4 + 128], mat("col1", cj, nh),
                                               start=True, stop=True), bw, a, t_cst)
            t = P.mark()
            a2 = P.do("A", lambda e: e.activation(sml[:, s0:s0 + 4 * nh], ps(b2, 4 * nh), ACT.Sqrt, bias=col("eps6")),
                      t, t_cols, zw)
            PB.give(b2, a2)
            v = P.do("V", lambda e: e.reciprocal(sml[:, s0 + 8:s0 + 8 + 4 * nh], sml[:, s0:s0 + 4 * nh]), a2, zw)

            def third():
                r = sml[:, s0 + 8:s0 + 8 + 4 * nh].rearrange("p (h n) -> p h n", n=1)
                a3 = P.do("A", lambda e: e.activation(sq.rearrange("p (h n) -> p h n", h=4 * nh),
                                                      r.to_broadcast([128, 4 * nh, 128 // nh]), ACT.Copy), v, t)
                hn.give(z, a3)

                def fourth():
                    b3, bw = PB.take()
                    for t4 in range(4):
                        P.mm(lambda e, t4=t4: e.transpose(PS[:, 512 * b3 + 128 * t4:512 * b3 + 128 * t4 + 128],
                                                          sq[:, 128 * t4:128 * t4 + 128], ident), bw, a3)
                    t = P.mark()
                    K1R.give(i, t)
                    v2 = P.do("V", lambda e: e.scalar_tensor_tensor(out=out, in0=out, scalar=gcol, in1=ps(b3),
                                                                    op0=ALU.mult, op1=ALU.mult), t, a0)
                    PB.give(b3, v2)
                    res["t"] = v2
                later.append(fourth)
            later.append(third)
        later.append(second)
        return res

    stX = ExitStack()
    X = sbt(stX, "X1", [128, 8, T])
    xt = {}
    for half in range(2):
        sl = slice(512 * half, 512 * half + 512)
        for k in range(8):
            n = 8 * half + k
            xt[k, half] = P.dma("S", f"x{k}" if half == 0 else f"y{k}",
                                lambda e, k=k, sl=sl: e.dma_start(X[:, k, sl], d["xT"][k][:, sl]))
    t_cols = P.dma("S", "col", lambda e: e.dma_start(cols[:, :], d["cols"]))
    t_cst = P.dma("S", "cst", lambda e: e.dma_start(mats[:, :], d["mats"]))
    t_gq = P.do("V", lambda e: e.tensor_scalar(gq1, col("q_norm_g"), 0.125, None, ALU.mult), t_cols)
    t_gq = P.do("V", lambda e: e.tensor_scalar(gq2, col("q_norm_w_2"), 0.125, None, ALU.mult), t_cols)
    for _ in range(3):
        load_unit()
    sm = new_sum("V")
    for half in range(2):
        sl = slice(512 * half, 512 * half + 512)
        for k in range(8):
            sm.add(X[:, k, sl], sl, xt[k, half])
    ht = norm_to_h(lambda k: X[:, k, :], "g_mix", rnorm(0, list(sm.done.values())), lambda k, half: xt[k, half], None)
    x_dead = [ht[7, 1], ht[6, 1]]
    stX.close()

    stM = ExitStack()
    QT = sbt(stM, "QT", [128, 4, T])
    KT = sbt(stM, "KT", [128, 4, T])
    Vt = sbt(stM, "Vt", [128, 8, 512])
    PP = sbt(stM, "PP", [128, 3, T])
    PT = sbt(stM, "PT", [128, 2, T])
    YX = sbt(stM, "YX", [128, T])
    YC = sbt(stM, "YC", [128, 2, T])
    ZC = sbt(stM, "ZC", [128, 1, T + 2])
    mn = sbt(stM, "mn", [128, 64])
    sx = sbt(stM, "sx", [128, 64])
    rx = sbt(stM, "rx", [128, 64])
    qk_t = []
    for e in "VAGT":
        P.wait(e, x_dead)
    for n in range(8):
        dst, g = (KT, col("k_norm_g")) if n < 4 else (QT, gq1)

        def cons(half, b, tok, dst=dst, g=g, n=n):
            qk_t.append(headnorm(half, b, tok, dst[:, n % 4, 512 * half:512 * half + 512], g))
        dense(8, Hhk, Hlk, ht, cons)
    flush()
    v_t = []

    def cons_v(i, b, tok):
        a = P.do("A", lambda e: e.activation(Vt[:, i, :], ps(b), ACT.Copy), tok)
        PB.give(b, a)
        v_t.append(a)
    dense_tok(ht, cons_v)

    def attention(steps, names, qk, bias, vv, out, pre=None, post=None, vo=lambda h: 64 * (h % 2)):
        PPb, PTb, mnb, sxb, rxb = names
        pp = Ring(3)
        pt = Ring(2)
        q = {}

        def stage0(s):
            if pre:
                pre(s)
            h, i = steps[s]
            W = 128 * (i + 1)
            nb = 1 if W <= 512 else 2
            b, bw = PB.take(nb)
            for c in range(nb):
                w = min(512, W - 512 * c)
                lh, rh, tk = qk(h, i, 512 * c, w)
                P.mm(lambda e, b=b, c=c, w=w, lh=lh, rh=rh: e.matmul(ps(b + c, w), lh, rh, start=True, stop=True), bw, tk)
            t = P.mark()
            p, pw = pp.take()
            bap, bt, brel = bias(h, i, W)
            v = P.do("V", lambda e: e.tensor_tensor_reduce(
                out=PPb[:, p, 0:W], in0=PS[:, 512 * b:512 * b + W], in1=bap, scale=-1.0, scalar=3.0e38,
                op0=ALU.add, op1=ALU.min, accum_out=mnb[:, s % 64:s % 64 + 1]), t, bt, pw)
            PB.give(b, v, k=nb)
            brel(v)
            a = P.do("A", lambda e: e.activation(PPb[:, p, 0:W], PPb[:, p, 0:W], ACT.Exp, bias=mnb[:, s % 64:s % 64 + 1],
                                                 scale=-1.0, accum_out=sxb[:, s % 64:s % 64 + 1]), v)
            q[s] = (W, nb, p, a)

        def stage1(s):
            W, nb, p, a = q[s]
            h, i = steps[s]
            b, bw = PB.take(nb)
            for c in range(i + 1):
                P.mm(lambda e, c=c: e.transpose(PS[:, 512 * b + 128 * c:512 * b + 128 * c + 128],
                                                PPb[:, p, 128 * c:128 * c + 128], ident), bw, a, t_cst)
            t = P.mark()
            pp.give(p, t)
            r = P.do("V", lambda e: e.reciprocal(rxb[:, s % 64:s % 64 + 1], sxb[:, s % 64:s % 64 + 1]), a)
            k, kw = pt.take()
            tt = []
            for c in range(nb):
                w = min(512, W - 512 * c)
                src = ps(b + c, w)
                dst = PTb[:, k, 512 * c:512 * c + w]
                if c == 0:
                    tt.append(P.do("A", lambda e, dst=dst, src=src: e.activation(dst, src, ACT.Copy), t, kw))
                else:
                    tt.append(P.do("V", lambda e, dst=dst, src=src: e.tensor_copy(dst, src), t, kw))
            PB.give(b, *tt, k=nb)
            q[s] = (k, tt, r)

        def stage2(s):
            h, i = steps[s]
            k, tt, r = q.pop(s)
            b, bw = PB.take()
            for c in range(i + 1):
                va, vt = vv(h, c)
                P.mm(lambda e, c=c, va=va: e.matmul(ps(b, 128), PTb[:, k, 128 * c:128 * c + 128], va,
                                                    start=(c == 0), stop=(c == i)), bw, tt, vt)
            t = P.mark()
            pt.give(k, t)
            oap, ow = out(h, i)
            o = vo(h)
            v = P.do("V", lambda e: e.tensor_scalar(oap, PS[:, 512 * b + o:512 * b + o + 64], rxb[:, s % 64:s % 64 + 1], None, ALU.mult), t, r, ow)
            PB.give(b, v)
            if post:
                post(s, v)

        n = len(steps)
        for s in range(n + 3):
            if s < n:
                stage0(s)
            if 2 <= s <= n + 1:
                stage1(s - 2)
            if s >= 3:
                stage2(s - 3)
            yield

    tb = {"free": None}

    def load_tb(h):
        if h < 8:
            tb[h] = P.dma("S", "t0", lambda e: e.dma_start(rr[:, :], d["T1"][h]), tb["free"])
    load_tb(0)
    steps = [(h, i) for h in range(8) for i in range(8)]

    def qk1(h, i, c, w):
        r = slice(64 * (h % 2), 64 * (h % 2) + 64)
        return QT[r, h // 2, 128 * i:128 * i + 128], KT[r, h // 2, c:c + w], [x["t"] for x in qk_t]

    def bias1(h, i, W):
        def rel(v):
            if i == 7:
                tb["free"] = v
                load_tb(h + 1)
        return rr[:, T - W:T], tb[h], rel

    ya_t = {}
    qk_done = {}

    def post1(s, v):
        ya_t[steps[s]] = v

    def ya(h):
        return YX[:, :] if h < 2 else QT[:, h // 2 - 1, :]

    def out1(h, i):
        return ya(h).rearrange("p (i n) -> p i n", i=8)[:, i, 64 * (h % 2):64 * (h % 2) + 64], [P.mark()]

    bg.append(attention(steps, (PP, PT, mn, sx, rx), qk1, bias1,
                        lambda h, c: (Vt[:, c, 128 * (h // 2):128 * (h // 2) + 128], v_t), out1, post=post1))
    zpad = P.do("V", lambda e: e.memset(ZC[:, :, 0:2], 0.0))
    smc = new_sum("G", acc_free["t"])
    st = {"zc": [None], "yc": [None, None]}
    yc_t = []
    for j in range(4):
        z = j % 2

        def cons_c(half, b, tok, z=z, j=j):
            a = P.do("A", lambda e: e.activation(ZC[:, 0, 2 + 512 * half:514 + 512 * half], ps(b), ACT.Copy), tok,
                     st["zc"][0])
            PB.give(b, a)
            st["ca", half] = a

        def cons_x(half, b, tok, z=z, j=j):
            zs = ZC[:, 0, 2 + 512 * half:514 + 512 * half]
            v = P.do("V", lambda e: e.tensor_tensor(zs, ps(b), zs, ALU.mult), tok, st["ca", half], zpad)
            PB.give(b, v)
            if half:
                y = YC[:, z, :]
                v = P.do("V", lambda e: e.tensor_scalar(y, ZC[:, 0, 2:T + 2], col("conv_w", 8 + j), col("conv_b", j),
                                                        ALU.mult, ALU.add), v, st["yc"][z])
                v = P.do("V", lambda e: e.scalar_tensor_tensor(out=y, in0=ZC[:, 0, 1:T + 1], scalar=col("conv_w", 4 + j),
                                                               in1=y, op0=ALU.mult, op1=ALU.add), v)
                v = P.do("V", lambda e: e.scalar_tensor_tensor(out=y, in0=ZC[:, 0, 0:T], scalar=col("conv_w", j),
                                                               in1=y, op0=ALU.mult, op1=ALU.add), v)
                st["zc"][0] = v
                st["y"] = v

        def cons_b(half, b, tok, z=z, j=j):
            sl = slice(512 * half, 512 * half + 512)
            v = P.do("V", lambda e: e.tensor_tensor(YC[:, z, sl], ps(b), YC[:, z, sl], ALU.mult), tok, st["y"])
            PB.give(b, v)
            a = smc.add(YC[:, z, sl], sl, v)
            if half:
                t = P.dma("S", f"z{z}", lambda e: e.dma_start(d["yscr"][j], YC[:, z, :]), v)
                st["yc"][z] = [t, a]
                yc_t.append(t)
        dense(8, Hhk, Hlk, ht, cons_c)
        dense(8, Hhk, Hlk, ht, cons_x)
        dense(8, Hhk, Hlk, ht, cons_b)
    win_done = P.mark()
    rn = rnorm(4, list(smc.done.values()))
    yh_c = {}
    for pair in (0, 2):
        for j in (pair, pair + 1):
            z = j % 2
            yh_c["t", j] = P.dma("S", f"z{z}", lambda e, j=j, z=z: e.dma_start(YC[:, z, :], d["yscr"][j]),
                                 yc_t, st["yc"][z])
        part = norm_to_h(lambda k: YC[:, k % 2, :], "g_out_conv", rn, lambda k, half: yh_c["t", k], win_done,
                         (pair, pair + 1), give=(pair == 2))
        st["yc"] = [[part[pair, 0], part[pair, 1]], [part[pair + 1, 0], part[pair + 1, 1]]]
        yh_c.update(part)
    yh_c = {k: v for k, v in yh_c.items() if k[0] != "t"}
    drain()
    yall = list(ya_t.values())[-1]
    for i in range(8):
        for q4 in range(4):
            k, w = K1R.take()
            src = ya(2 * q4).rearrange("p (i n) -> p i n", i=8)[:, i, :]
            a = P.do("A", lambda e, i=i, k=k, q4=q4, src=src: e.activation(
                K1[:, k, 0:128], src, ACT.Square, accum_out=sml[:, 4 * i + q4:4 * i + q4 + 1]), yall, w)
            K1R.give(k, a)
    v = P.do("V", lambda e: e.tensor_reduce(sml[:, 80:88], sml[:, 0:32].rearrange("p (i n) -> p i n", i=8),
                                            mybir.AxisListType.X, ALU.add), a)
    a = P.do("A", lambda e: e.activation(sml[:, 88:96], sml[:, 80:88], ACT.Sqrt, bias=col("eps6"), scale=1.0 / 512), v, t_cols)
    v = P.do("V", lambda e: e.reciprocal(sml[:, 80:88], sml[:, 88:96]), a)

    def tok_to_h(srcs, i, j0, w, scale, gain, eng="V", hw=None):
        b, bw = PB.take()
        for c in range(4):
            P.mm(lambda e, c=c: e.transpose(PS[:, 512 * b + 128 * c:512 * b + 128 * c + 128], srcs[c], ident),
                 bw, w, t_cst)
        t = P.mark()
        pv = ps(b).rearrange("p (c n) -> p c n", c=4)
        k, kw = K1R.take()
        tmp = K1[:, k, 0:512].rearrange("p (c n) -> p c n", c=4)
        if gain is not None:
            v = P.do("V", lambda e: e.tensor_tensor(tmp, pv, gain, ALU.mult), t, kw)
        else:
            v = P.do("V", lambda e: e.tensor_copy(tmp, pv), t, kw)
        PB.give(b, v)
        a, l = split(Hh[:, j0:j0 + 4, 128 * i:128 * i + 128], Hl[:, j0:j0 + 4, 128 * i:128 * i + 128], tmp, v, hw, eng)
        K1R.give(k, a, l)
        return t, a, l

    ga = cols[:, COL["g_out_attn"]:COL["g_out_attn"] + 4].rearrange("p (c n) -> p c n", n=1).to_broadcast([128, 4, 128])
    yat = {0: [], 1: []}
    v0 = v
    for i in range(8):
        srcs = [ya(2 * q4).rearrange("p (i n) -> p i n", i=8)[:, i, :] for q4 in range(4)]
        for q4 in range(4):
            src = srcs[q4]
            if q4 % 2:
                v2 = P.do("V", lambda e, i=i, src=src: e.tensor_scalar(src, src, sml[:, 80 + i:81 + i], None, ALU.mult), v0)
            else:
                a2 = P.do("A", lambda e, i=i, src=src: e.activation(src, src, ACT.Copy, scale=sml[:, 80 + i:81 + i]), v0)
        t, a3, l3 = tok_to_h(srcs, i, 4, [v2, a2], None, ga, hw=win_done, eng="G" if i % 2 else "V")
        yat[i // 4] += [a3, l3]
    yh = dict(yh_c)
    for j in range(4, 8):
        for half in range(2):
            yh[j, half] = yat[half]
    rr_free["t"] = tb["free"]
    stM.close()
    mix_dead = [t, a3, yat[1], yat[0]] + list(yh_c.values())

    def out_proj(name, src, srct, yh, dead):
        st = ExitStack()
        X = sbt(st, name, [128, 8, T])
        xt = [P.dma("S", f"x{k}", lambda e, k=k: e.dma_start(X[:, k, :], src[k]), dead, srct) for k in range(8)]
        sm = new_sum("G", acc_free["t"])
        xo = {}
        for m in range(8):
            def cons(half, b, tok, m=m):
                sl = slice(512 * half, 512 * half + 512)
                v = P.do("V", lambda e: e.tensor_tensor(X[:, m, sl], ps(b), X[:, m, sl], ALU.add), tok, xt[m])
                PB.give(b, v)
                sm.add(X[:, m, sl], sl, v, m >= 6)
                xo[m, half] = v
            dense(8, Hhk, Hlk, yh, cons)
        return st, X, sm, xo, P.mark()

    def ffn(X, gname, xo, sm, hdone, conv, last):
        ht = norm_to_h(lambda k: X[:, k, :], gname, rnorm(0, list(sm.done.values())), lambda k, half: xo[k, half], hdone)
        st = ExitStack()
        HGh = sbt(st, "HGh" + gname, [128, 5, T], F32R)
        HGl = sbt(st, "HGl" + gname, [128, 5, T], F32R)
        GB = sbt(st, "GB" + gname, [128, 2, T + 2])
        SG = sbt(st, "SG" + gname, [128, T])
        zp = P.do("V", lambda e: e.memset(GB[:, :, 0:2], 0.0), hdone)
        hg_free = [hdone]
        s = {"sg": None}
        gbf = [None, None]
        nsm = new_sum("G", acc_free["t"])
        nxo = {}
        for g, (fa, fb) in enumerate(GROUPS):
            hg_t = {}
            for f in range(fa, fb):
                z = f % 2

                def cons_g(half, b, tok, f=f, z=z):
                    if conv:
                        a = P.do("A", lambda e: e.activation(GB[:, z, 2 + 512 * half:514 + 512 * half], ps(b), ACT.Copy),
                                 tok, gbf[z], zp)
                        PB.give(b, a)
                        if half:
                            v = P.do("V", lambda e: e.tensor_scalar(SG[:, :], GB[:, z, 2:T + 2], col("ffn_conv_w", 44 + f),
                                                                    col("ffn_conv_b", f), ALU.mult, ALU.add), a, s["sg"])
                            v = P.do("V", lambda e: e.scalar_tensor_tensor(
                                out=SG[:, :], in0=GB[:, z, 1:T + 1], scalar=col("ffn_conv_w", 22 + f), in1=SG[:, :],
                                op0=ALU.mult, op1=ALU.add), v)
                            v = P.do("V", lambda e: e.scalar_tensor_tensor(
                                out=SG[:, :], in0=GB[:, z, 0:T], scalar=col("ffn_conv_w", f), in1=SG[:, :],
                                op0=ALU.mult, op1=ALU.add), v)
                            s["silu"] = P.do("A", lambda e: e.activation(GB[:, z, 2:T + 2], SG[:, :], ACT.Silu), v)
                            s["sg"] = s["silu"]
                    else:
                        a = P.do("A", lambda e: e.activation(GB[:, z, 2 + 512 * half:514 + 512 * half], ps(b), ACT.Silu),
                                 tok, gbf[z], zp)
                        PB.give(b, a)
                        s["silu"] = a

                def cons_u(half, b, tok, f=f, z=z, fa=fa):
                    sl = slice(512 * half, 512 * half + 512)
                    gs = GB[:, z, 2 + 512 * half:514 + 512 * half]
                    v = P.do("V", lambda e: e.tensor_tensor(gs, ps(b), gs, ALU.mult), tok, s["silu"])
                    PB.give(b, v)
                    a, l = split(HGh[:, f - fa, sl], HGl[:, f - fa, sl], gs, v, hg_free, eng="V")
                    gbf[z] = [a, l]
                    hg_t[f - fa, half] = [a, l]
                dense(8, Hhk, Hlk, ht, cons_g)
                dense(8, Hhk, Hlk, ht, cons_u)
            for m in range(8):
                def cons_d(half, b, tok, m=m, g=g):
                    sl = slice(512 * half, 512 * half + 512)
                    v = P.do("V", lambda e: e.tensor_tensor(X[:, m, sl], ps(b), X[:, m, sl], ALU.add), tok,
                             xo[m, half], nxo.get((m, half)))
                    PB.give(b, v)
                    nxo[m, half] = v
                    if g == len(GROUPS) - 1:
                        last(m, half, v, nsm)
                toks = hg_t
                dense(fb - fa, hk(HGh), hk(HGl), toks, cons_d)
            hg_free = [P.mark()]
        st.close()
        return nsm, nxo, P.mark()

    def add_sq(X):
        def last(m, half, v, nsm):
            sl = slice(512 * half, 512 * half + 512)
            nsm.add(X[:, m, sl], sl, v, m >= 6)
        return last

    stX, X, sm, xo, hd = out_proj("X2", d["xT"], None, yh, mix_dead)
    sm, xo, hd = ffn(X, "g_ffn", xo, sm, hd, True, add_sq(X))

    ht = norm_to_h(lambda k: X[:, k, :], "g_ple", rnorm(0, list(sm.done.values())), lambda k, half: xo[k, half], hd)
    stP = ExitStack()
    PR = sbt(stP, "PR", [128, 2, T])
    Ph = sbt(stP, "Ph", [128, 2, T], F32R)
    Pl = sbt(stP, "Pl", [128, 2, T], F32R)
    SGP = sbt(stP, "SGP", [128, 2, T])
    pt = P.dma("S", "sp", lambda e: e.dma_start(PR[:, :, :], d["pT"]), hd, list(xo.values()))
    pa, pl = split(Ph[:, :, :], Pl[:, :, :], PR[:, :, :], pt, hd)
    sgf = [None, None]
    nsm = new_sum("G", acc_free["t"])
    nxo = {}
    spt = []
    for m in range(8):
        z = m % 2
        s = {}

        def cons_g(half, b, tok, z=z):
            a = P.do("A", lambda e: e.activation(SGP[:, z, 512 * half:512 * half + 512], ps(b), ACT.Sigmoid), tok, sgf[z])
            PB.give(b, a)
            s["a"] = a

        def cons_p(half, b, tok, z=z, m=m):
            sl = slice(512 * half, 512 * half + 512)
            v = P.do("V", lambda e: e.tensor_tensor(SGP[:, z, sl], ps(b), SGP[:, z, sl], ALU.mult), tok, s["a"])
            PB.give(b, v)
            v = P.do("V", lambda e: e.tensor_tensor(X[:, m, sl], SGP[:, z, sl], X[:, m, sl], ALU.add), v, xo[m, half])
            sgf[z] = v
            nsm.add(X[:, m, sl], sl, v, m >= 6)
            nxo[m, half] = v
            if half:
                spt.append(P.dma("S", f"x{m}", lambda e: e.dma_start(d["spill"][m], X[:, m, :]), v))
        dense(8, Hhk, Hlk, ht, cons_g)
        dense(2, hk(Ph), hk(Pl), [pa, pl], cons_p)
    hd = P.mark()
    stP.close()

    ht = norm_to_h(lambda k: X[:, k, :], "norm1_w_2", rnorm(0, list(nsm.done.values())), lambda k, half: nxo[k, half], hd)
    stX.close()
    dead = [ht[7, 1], ht[6, 1]] + spt
    for e in "VAGT":
        P.wait(e, dead)
    stN = ExitStack()
    KA = sbt(stN, "KA", [128, T])
    VA = sbt(stN, "VA", [128, 8, 64])
    SC = sbt(stN, "SC", [128, 4224])
    IW = sbt(stN, "IW", [128, 8, 4])
    stI = ExitStack()
    IQ = sbt(stI, "IQ", [128, T])
    IK = sbt(stI, "IK", [128, T])
    CT = sbt(stI, "CT", [128, T])
    IWT = sbt(stI, "IWT", [128, T])
    wkv = sbt(stI, "wkv", [128, 192])
    rb = sbt(stI, "rb", [32, 8 + 384])
    RR = sbt(stI, "RR", [128, 8, 384])
    ct = {}
    tkv = P.dma("S", "rl", lambda e: e.dma_start(wkv[:, :], d["wkv"]), dead)
    trb = P.dma("S", "rb", lambda e: e.dma_start(rb[:, :], d["rb"]), dead)
    for h in range(8):
        b, bw = PB.take()
        P.mm(lambda e, b=b, h=h: e.matmul(ps(b, 384), rb[:, h:h + 1].to_broadcast([32, 128]), rb[:, 8:392],
                                          start=True, stop=True), bw, trb)
        t = P.mark()
        a = P.do("A", lambda e, b=b, h=h: e.activation(RR[:, h, :], ps(b, 384), ACT.Copy), t)
        PB.give(b, a)
    t = P.dma("S", "rb", lambda e: e.dma_start(d["rscr"], RR[:, :, :]), a)
    t_scr = t

    def copy_cons(dst, fn=None, eng="A", tag=None):
        def cons(half, b, tok):
            sl = slice(512 * half, 512 * half + 512)
            if eng == "A":
                v = P.do("A", lambda e: e.activation(dst[:, sl], ps(b), fn or ACT.Copy), tok, ct.get(tag + "f"))
            else:
                v = P.do("V", lambda e: e.tensor_copy(dst[:, sl], ps(b)), tok, ct.get(tag + "f"))
            PB.give(b, v)
            ct.setdefault(tag, [])
            ct[tag] = [v] if half == 0 else ct[tag] + [v]
        return cons

    dense(8, Hhk, Hlk, ht, copy_cons(IQ[:, :], tag="iq"))
    dense(8, Hhk, Hlk, ht, copy_cons(IWT[:, :], tag="iw"))
    ct["ik"] = []
    for half in range(2):
        b, bw = PB.take()
        P.mm(lambda e, b=b, half=half: e.matmul(ps(b), mat("sel"), IWT[:, 512 * half:512 * half + 512],
                                                start=True, stop=True), bw, ct["iw"], t_cst)
        t = P.mark()
        a = P.do("A", lambda e, b=b, half=half: e.activation(IK[:, 512 * half:512 * half + 512], ps(b), ACT.Copy), t)
        PB.give(b, a)
        ct["ik"].append(a)
    b, bw = PB.take(2)
    for i in range(8):
        P.mm(lambda e, i=i: e.transpose(PS[:, 512 * b + 128 * i:512 * b + 128 * i + 128],
                                        IWT[:, 128 * i:128 * i + 128], ident), bw, ct["iw"])
    t = P.mark()
    iwv = PS[:, 512 * b:512 * b + 1024].rearrange("p (i n) -> p i n", i=8)[:, :, 32:36]
    t_iw = P.do("V", lambda e: e.tensor_scalar(IW[:, :, :], iwv, 0.5, None, ALU.mult), t)
    PB.give(b, t_iw, k=2)
    SOFF = {}
    at = 0
    for i in range(2, 8):
        SOFF[i] = at
        at += 128 * (i + 1)
    ct["sc"] = {}
    ixr = Ring(2)
    IX = sbt(stI, "IX", [128, 2, T])

    def index_scores(i):
        W = 128 * (i + 1)
        nb = 1 if W <= 512 else 2
        sc = SC[:, SOFF[i]:SOFF[i] + W]
        for h in range(4):
            b, bw = PB.take(nb)
            r = slice(32 * h, 32 * h + 32)
            for c in range(nb):
                w = min(512, W - 512 * c)
                P.mm(lambda e, c=c, w=w, r=r: e.matmul(ps(b + c, w), IQ[r, 128 * i:128 * i + 128],
                                                       IK[r, 512 * c:512 * c + w], start=True, stop=True),
                     bw, ct["iq"], ct["ik"])
            t = P.mark()
            k, kw = ixr.take()
            a = P.do("A", lambda e, k=k, b=b: e.activation(IX[:, k, 0:W], PS[:, 512 * b:512 * b + W], ACT.Relu,
                                                           scale=32.0 ** -0.5), t, kw)
            PB.give(b, a, k=nb)
            if h == 0:
                v = P.do("V", lambda e, k=k: e.tensor_scalar(sc, IX[:, k, 0:W], IW[:, i, 0:1], None, ALU.mult), a, t_iw)
            else:
                v = P.do("V", lambda e, k=k, h=h: e.scalar_tensor_tensor(
                    out=sc, in0=IX[:, k, 0:W], scalar=IW[:, i, h:h + 1], in1=sc, op0=ALU.mult, op1=ALU.add), a, v)
            ixr.give(k, v)
            yield
        d_ = sc[:, W - 128:W]
        v = P.do("V", lambda e: e.scalar_tensor_tensor(out=d_, in0=mat("adm"), scalar=1.0e8, in1=d_, op0=ALU.mult,
                                                       op1=ALU.add), v, t_cst)
        ct["sc"][i] = v

    cu = sml[:, 32:38].bitcast(I32)
    xm = sml[:, 38:44].bitcast(I32)
    cand = sml[:, 44:50]
    cnt = sml[:, 50:56]
    kb_ = sml[:, 56:62].bitcast(I32)
    thr = sml[:, 64:70]

    def topk():
        junk = acc[:, :].bitcast(mybir.dt.bfloat16)
        jt = [None, None]
        v = P.do("V", lambda e: e.memset(cu, 0))
        v = P.do("V", lambda e: e.memset(xm, -1), v)
        for bit in range(31, -1, -1):
            imm = (1 << bit) - (1 << 32 if bit == 31 else 0)
            if bit == 31:
                v = P.do("V", lambda e: e.memset(cand.bitcast(I32), 0), v)
            else:
                v = P.do("V", lambda e, imm=imm: e.tensor_scalar(cand.bitcast(I32), cu, imm, None, ALU.bitwise_or), v)
                v = P.do("V", lambda e: e.tensor_tensor(cand.bitcast(I32), cand.bitcast(I32), xm, ALU.bitwise_xor), v)
            for i in range(2, 8):
                W = 128 * (i + 1)
                c = P.do("V", lambda e, i=i, W=W: e.tensor_scalar(
                    junk[:, T * (i % 2):T * (i % 2) + W], SC[:, SOFF[i]:SOFF[i] + W], cand[:, i - 2:i - 1], None, ALU.is_ge, ALU.add,
                    accum_out=cnt[:, i - 2:i - 1]), v, ct["sc"][i], jt[i % 2])
                jt[i % 2] = c
                yield
            if bit == 31:
                v = P.do("V", lambda e: e.tensor_scalar(kb_, cnt, 255.5, -2147483648.0, ALU.is_ge, ALU.mult), c)
                v = P.do("V", lambda e: e.tensor_copy(cu, kb_), v)
                w_ = P.do("V", lambda e: e.tensor_scalar(cnt, cnt, 255.5, None, ALU.is_ge), v)
                w_ = P.do("V", lambda e: e.tensor_scalar(xm, cnt, -2147483647.0 - 1.0, None, ALU.mult), w_)
                w2 = P.do("V", lambda e: e.tensor_scalar(kb_, cnt, 1.0, None, ALU.subtract), w_)
                v = P.do("V", lambda e: e.tensor_tensor(xm, xm, kb_, ALU.bitwise_or), w2)
            else:
                v = P.do("V", lambda e, bit=bit: e.tensor_scalar(kb_, cnt, 255.5, float(1 << bit), ALU.is_ge, ALU.mult), c)
                v = P.do("V", lambda e: e.tensor_tensor(cu, cu, kb_, ALU.bitwise_or), v)
            yield
        v = P.do("V", lambda e: e.tensor_tensor(thr.bitcast(I32), cu, xm, ALU.bitwise_xor), v)
        ct["thr"] = v

    for i in range(2, 8):
        bg.append(index_scores(i))
    cn = []

    def cons_c(half, b, tok):
        cn.append(headnorm(half, b, tok, CT[:, 512 * half:512 * half + 512], col("kv_norm_w_2"), one=True))
    dense(8, Hhk, Hlk, ht, cons_c)
    flush()
    kn = []
    for half in range(2):
        b, bw = PB.take()
        P.mm(lambda e, b=b, half=half: e.matmul(ps(b), wkv[:, 0:128], CT[:, 512 * half:512 * half + 512],
                                                start=True, stop=True), bw, [x["t"] for x in cn], tkv)
        t = P.mark()
        flush()
        kn.append(headnorm(half, b, t, KA[:, 512 * half:512 * half + 512], col("k_norm_w_2")))
        flush()
    b, bw = PB.take()
    for i in range(8):
        P.mm(lambda e, i=i: e.matmul(PS[:, 512 * b + 64 * i:512 * b + 64 * i + 64], CT[:, 128 * i:128 * i + 128],
                                     wkv[:, 128:192], start=True, stop=True), bw)
    t = P.mark()
    t_va = P.do("A", lambda e: e.activation(VA[:, :, :], ps(b).rearrange("p (i n) -> p i n", i=8), ACT.Copy), t)
    PB.give(b, t_va)
    flush()
    drain()
    idead = [t_va, t] + [x["t"] for x in kn + cn] + [v for v in ct["sc"].values()] + [t_iw, t_scr]
    stI.close()
    stR = ExitStack()
    VB = sbt(stR, "VB", [128, 2, 8, 128])
    DQ = sbt(stR, "DQ", [128, 1536])
    CS = sbt(stR, "CS", [128, 2, T])
    QR = sbt(stR, "QR", [128, 2, T])
    KR = sbt(stR, "KR", [128, 2, T])
    GG = sbt(stR, "GG", [128, 2, T])
    RW = rr
    YT = sbt(stR, "YT", [128, 8, 128])
    K2 = sbt(stR, "K2", [128, 2, 512])
    SD = sbt(stR, "SD", [128, 2, 256])
    KD = sbt(stR, "KD", [128, 2, 128])
    ST = sbt(stR, "ST", [128, 2, 64])
    bst = sbt(stR, "bst", [128, 16, 6])
    bag = sbt(stR, "bag", [128, 16, 2])
    rsd = sbt(stR, "rsd", [128, 16])
    for e in "VAGT":
        P.wait(e, idead)
    t_cs = P.dma("S", "sp", lambda e: e.dma_start(CS[:, :, :], d["cs"]), idead)
    t_dq = P.dma("S", "rl", lambda e: e.dma_start(DQ[:, :], d["dq"]), idead, rr_free["t"], acc_free["t"])
    P.wait("A", rr_free["t"])
    P.wait("V", acc_free["t"])
    bg2.append(topk())
    rel_t = {z: None for z in ((n, y) for n in ("r", "gg") for y in range(2))}
    rel_t["yt"] = None
    ob_t = []

    def rotary(dst, free):
        out = []
        for half in range(2):
            sl = slice(512 * half, 512 * half + 512)
            b, bw = PB.take()
            P.mm(lambda e, b=b, sl=sl: e.matmul(ps(b), mat("perm"), RW[:, sl], start=True, stop=True), bw, ct["rw"])
            t = P.mark()
            g = P.do("G", lambda e, sl=sl: e.tensor_tensor(dst[:, sl], RW[:, sl], CS[:, 0, sl], ALU.mult),
                     ct["rw"], t_cs, free)
            k, kw = K1R.take()
            v = P.do("V", lambda e, b=b, sl=sl, k=k: e.tensor_tensor(K1[:, k, 0:512], ps(b), CS[:, 1, sl], ALU.mult),
                     t, kw, t_cs)
            PB.give(b, v)
            g2 = P.do("G", lambda e, sl=sl, k=k: e.tensor_tensor(dst[:, sl], dst[:, sl], K1[:, k, 0:512], ALU.add), v, g)
            K1R.give(k, g2)
            out.append(g2)
        ct["rwf"] = [t, g]
        return out

    k2r = Ring(2)

    def retention(j, y, qr, kr, vbt, ggt):
        QRy, KRy, VBy, GGy = QR[:, y, :], KR[:, y, :], VB[:, y, :, :], GG[:, y, :]
        for c in range(8):
            sl = slice(128 * c, 128 * c + 128)
            z = c % 2
            b, bw = PB.take(2)
            for h in range(2):
                r = slice(64 * h, 64 * h + 64)
                P.mm(lambda e, b=b, h=h, r=r, sl=sl: e.matmul(ps(b + h, 128), KRy[r, sl], QRy[r, sl], start=True,
                                                              stop=True), bw, kr, qr)
            t = P.mark()
            sdv = SD[:, z, :].rearrange("p (h n) -> p h n", h=2)
            v_sd = P.do("V", lambda e, b=b, sdv=sdv: e.tensor_tensor(
                sdv, PS[:, 512 * b:512 * b + 1024].rearrange("p (h n) -> p h n", h=2)[:, :, 0:128],
                DQ[:, 256 * j:256 * j + 256].rearrange("p (h n) -> p h n", h=2), ALU.mult), t, ct.get(("sdf", z)), t_dq)
            PB.give(b, v_sd, k=2)
            b, bw = PB.take()
            P.mm(lambda e, b=b, sl=sl: e.transpose(ps(b, 128), KRy[:, sl], ident), bw)
            t = P.mark()
            for h in range(2):
                a_kd = P.do("A", lambda e, b=b, h=h, z=z: e.activation(
                    KD[:, z, 64 * h:64 * h + 64], ps(b, 128)[:, 64 * h:64 * h + 64], ACT.Copy,
                    scale=col("kdec", 2 * j + h)), t, ct.get(("kdf", z)))
            PB.give(b, a_kd)
            yield
            b, bw = PB.take(2)
            for h in range(2):
                r = slice(64 * h, 64 * h + 64)
                o = slice(512 * (b + h), 512 * (b + h) + 64)
                P.mm(lambda e, z=z, h=h, o=o, c=c: e.matmul(
                    PS[:, o], SD[:, z, 128 * h:128 * h + 128], VBy[:, c, 64 * h:64 * h + 64],
                    start=True, stop=(c == 0)), bw, v_sd, vbt)
                if c:
                    P.mm(lambda e, z=z, h=h, o=o, r=r, sl=sl: e.matmul(
                        PS[:, o], QRy[r, sl], ST[r, z, :], start=False, stop=True), ct["st"])
            t_y = P.mark()
            ct["sdf", z] = t_y
            yv = PS[:, 512 * b:512 * b + 1024].rearrange("p (h n) -> p h n", h=2)[:, :, 0:64]
            a_y = P.do("A", lambda e, c=c, yv=yv: e.activation(YT[:, c, :].rearrange("p (h n) -> p h n", h=2), yv,
                                                               ACT.Copy), t_y, rel_t["yt"])
            PB.give(b, a_y, k=2)
            if c < 7:
                b, bw = PB.take()
                P.mm(lambda e, b=b, z=z, c=c: e.matmul(ps(b, 128), KD[:, z, :], VBy[:, c, :],
                                                       start=True, stop=True), bw, a_kd)
                t = P.mark()
                ct["kdf", z] = t
                sv = []
                for h in range(2):
                    r = slice(64 * h, 64 * h + 64)
                    o = slice(512 * b + 64 * h, 512 * b + 64 * h + 64)
                    if c == 0:
                        sv.append(P.do("V", lambda e, r=r, o=o, z=z: e.tensor_copy(ST[r, 1 - z, :], PS[r, o]), t, t_y))
                    else:
                        sv.append(P.do("V", lambda e, r=r, o=o, z=z: e.scalar_tensor_tensor(
                            out=ST[r, 1 - z, :], in0=ST[r, z, :], scalar=cols[r, COL["g128"] + j:COL["g128"] + j + 1],
                            in1=PS[r, o], op0=ALU.mult, op1=ALU.add), t, t_y, ct["st"]))
                PB.give(b, *sv)
                ct["st"] = sv
            for h in range(2):
                v = P.do("V", lambda e, h=h, c=c: e.bn_stats(bst[:, 2 * c + h, :], YT[:, c, 64 * h:64 * h + 64]), a_y)
                v_bag = P.do("V", lambda e, h=h, c=c: e.bn_aggr(bag[:, 2 * c + h, :], bst[:, 2 * c + h, :]), v)
            yield
        rel_t["r", y] = t_y
        vg = P.do("V", lambda e: e.tensor_copy(rsd[:, :], bag[:, :, 1]), v_bag)
        a = P.do("A", lambda e: e.activation(rsd[:, :], rsd[:, :], ACT.Sqrt, bias=col("eps5")), vg)
        v = P.do("V", lambda e: e.reciprocal(rsd[:, :], rsd[:, :]), a)
        for c in range(8):
            for h in range(2):
                v2 = P.do("V", lambda e, c=c, h=h: e.tensor_scalar(
                    YT[:, c, 64 * h:64 * h + 64], YT[:, c, 64 * h:64 * h + 64], bag[:, 2 * c + h, 0:1],
                    rsd[:, 2 * c + h:2 * c + h + 1], ALU.subtract, ALU.mult), v, a_y)
        yield
        b, bw = PB.take(2)
        for c in range(8):
            P.mm(lambda e, b=b, c=c: e.transpose(PS[:, 512 * b + 128 * c:512 * b + 128 * c + 128], YT[:, c, :], ident),
                 bw, v2)
        t = P.mark()
        rel_t["yt"] = t
        for half in range(2):
            sl = slice(512 * half, 512 * half + 512)
            k, kw = k2r.take()
            a = P.do("A", lambda e, b=b, half=half, k=k: e.activation(
                K2[:, k, :], ps(b + half), ACT.Identity, bias=col("ret_gn_b_2", j), scale=col("ret_gn_w_2", j)), t, kw)
            PB.give(b + half, a)
            v = P.do("V", lambda e, k=k, sl=sl: e.tensor_tensor(GGy[:, sl], K2[:, k, :], GGy[:, sl], ALU.mult),
                     a, ggt)
            k2r.give(k, v)
        t = P.dma("S", f"y{j}", lambda e: e.dma_start(d["yscr"][j], GGy), v)
        ob_t.append(t)
        rel_t["gg", y] = t
        yield

    for j in range(4):
        y = j % 2
        dense(8, Hhk, Hlk, ht, copy_cons(RW[:, :], tag="rw"))
        qr = rotary(QR[:, y, :], rel_t["r", y])
        qdv = DQ[:, 1024 + 128 * j:1024 + 128 * j + 128].rearrange("p (a n) -> p a n", a=1).to_broadcast([128, 8, 128])
        q8 = QR[:, y, :].rearrange("p (a n) -> p a n", a=8)
        qd = P.do("G", lambda e, qdv=qdv, q8=q8: e.tensor_tensor(q8, q8, qdv, ALU.mult), qr, t_dq)
        dense(8, Hhk, Hlk, ht, copy_cons(RW[:, :], tag="rw"))
        kr = rotary(KR[:, y, :], rel_t["r", y])
        dense(8, Hhk, Hlk, ht, copy_cons(RW[:, :], tag="rw"))
        b, bw = PB.take(2)
        for c in range(8):
            P.mm(lambda e, b=b, c=c: e.transpose(PS[:, 512 * b + 128 * c:512 * b + 128 * c + 128],
                                                 RW[:, 128 * c:128 * c + 128], ident), bw, ct["rw"])
        t = P.mark()
        ct["rwf"] = [t]
        vbt = []
        for half in range(2):
            vbt.append(P.do("A", lambda e, b=b, half=half, y=y: e.activation(
                VB[:, y, 4 * half:4 * half + 4, :], ps(b + half).rearrange("p (c n) -> p c n", c=4), ACT.Copy),
                t, rel_t["r", y]))
        PB.give(b, vbt[1], k=2)
        ct["ggf"] = rel_t["gg", y]
        dense(8, Hhk, Hlk, ht, copy_cons(GG[:, y, :], fn=ACT.Silu, tag="gg"))
        drain()
        bg.append(retention(j, y, [qd], kr, vbt, ct["gg"]))
    qa_t, qs_t = [], []
    stage = [GG[:, 0, :], rr[:, :]]
    sfree = [rel_t["gg", 0], ct["rwf"]]
    for j in range(4):
        z = j % 2
        P.wait("A", sfree[z])
        P.wait("V", sfree[z])
        mine = []

        def cons(half, b, tok, z=z, mine=mine):
            mine.append(headnorm(half, b, tok, stage[z][:, 512 * half:512 * half + 512], gq2))
        dense(8, Hhk, Hlk, ht, cons)

        def put(j=j, z=z, mine=mine):
            later.append(lambda: later.append(lambda: later.append(go)))

            def go():
                sfree[z] = P.dma("S", f"q{j}", lambda e: e.dma_start(d["qscr"][j], stage[z]), [x["t"] for x in mine])
                qs_t.append(sfree[z])
        put()
        flush() if j == 3 else None
        if j < 3:
            run_later(0)
        while j == 1 and len(qs_t) < 1 or j == 2 and len(qs_t) < 2:
            run_later(1)
    flush()
    win_done = P.mark()
    drain()
    ret_dead = [P.mark(), vbt, ob_t, qd, kr, qs_t] + [P.do("V", lambda e: e.memset(sml[:, 98:99], 0.0)),
                                                      P.do("A", lambda e: e.activation(sml[:, 99:100], ident[:, 0:1], ACT.Copy))]
    stR.close()
    QA = sbt(stN, "QA", [128, 4, T])
    BN = sbt(stN, "BN", [128, 8, 256])
    for e in "VAGT":
        P.wait(e, ret_dead)
    for j in range(4):
        qa_t.append({"t": P.dma("S", f"q{j}", lambda e, j=j: e.dma_start(QA[:, j, :], d["qscr"][j]), ret_dead)})
    r0 = d["rscr"]
    rsrc = bass.AP(tensor=r0.tensor, offset=127, ap=[[8 * 384 - 1, 128], [384, 8], [1, 256]])
    t_bn = P.dma("S", "rb", lambda e: e.dma_start(BN[:, :, :], rsrc), t_scr, ret_dead)
    while bg2:
        tick()
    yh = {}
    rdead = [win_done] + [x["t"] for x in qa_t]

    stA = ExitStack()
    MM = sbt(stA, "MM", [128, 2, T])
    MN = sbt(stA, "MN", [128, 2, 256])
    SE = [acc, rr]
    PP2 = sbt(stA, "PP2", [128, 3, T])
    PT2 = sbt(stA, "PT2", [128, 2, T])
    YA2 = sbt(stA, "YA2", [128, 2, 512])
    mn2 = sbt(stA, "mn2", [128, 64])
    sx2 = sbt(stA, "sx2", [128, 64])
    rx2 = sbt(stA, "rx2", [128, 64])
    one = sbt(stA, "one", [128, T])
    for e in "VAGT":
        P.wait(e, rdead)
    t_one = P.do("V", lambda e: e.memset(one[:, :], 1.0))
    need = sml[:, 72:80]
    mt = {}
    mm_free = [None, None]

    def mask(i):
        W = 128 * (i + 1)
        nr = min(256, W)
        if i < 2:
            v = P.do("V", lambda e: e.memset(MN[:, i % 2, 0:nr], 0.0), mt.get(("mn", i % 2)))
            v = P.do("V", lambda e: e.tensor_copy(MN[:, i % 2, nr - 128:nr], mat("adm")), v)
            mt[i] = v
            return
        sc = SC[:, SOFF[i]:SOFF[i] + W]
        th = thr[:, i - 2:i - 1]
        eq, rk = SE[0][:, 0:W], SE[1][:, 0:W]
        v1 = P.do("V", lambda e: e.tensor_scalar(eq, sc, th, None, ALU.is_equal), ct["thr"])
        v2 = P.do("V", lambda e: e.tensor_tensor_scan(rk, one[:, 0:W], eq, 0.0, ALU.mult, ALU.add), v1, t_one)
        v3 = P.do("V", lambda e: e.tensor_scalar(sc, sc, th, None, ALU.is_gt, ALU.add, accum_out=need[:, i:i + 1]), v1)
        v4 = P.do("V", lambda e: e.tensor_scalar(need[:, i:i + 1], need[:, i:i + 1], -1.0, 256.0, ALU.mult, ALU.add), v3)
        v5 = P.do("V", lambda e: e.scalar_tensor_tensor(out=eq, in0=rk, scalar=need[:, i:i + 1], in1=eq,
                                                        op0=ALU.is_le, op1=ALU.mult), v4, v2)
        v6 = P.do("V", lambda e: e.tensor_tensor(eq, eq, sc, ALU.add), v5)
        v7 = P.do("V", lambda e: e.tensor_scalar(MM[:, 0, 0:W], eq, -NEG, NEG, ALU.mult, ALU.add), v6, mm_free)
        v8 = P.do("V", lambda e: e.tensor_scalar(MM[:, 1, 0:W], eq, -NEG, NEG, ALU.mult, ALU.add), v6, mm_free)
        mt[i] = P.do("V", lambda e: e.tensor_copy(MN[:, i % 2, :], MM[:, 0, W - 256:W]), v7, v8, mt.get(("mn", i % 2)))

    steps2 = [(h, i) for i in range(8) for h in range(8)]
    bt = {}

    def pre2(s):
        h, i = steps2[s]
        if h == 0:
            mask(i)
        z = h % 2
        W = 128 * (i + 1)
        nr = min(256, W)
        g = P.do("G", lambda e: e.tensor_tensor(MM[:, z, W - nr:W], MN[:, i % 2, 0:nr], BN[:, h, 256 - nr:256], ALU.add),
                 mt[i], mm_free[z], t_bn)
        mt["mn", i % 2] = g
        bt[s] = g
        ct["s"] = s

    def bias2(h, i, W):
        z = h % 2

        def rel(v):
            mm_free[z] = v
        return MM[:, z, 0:W], bt[ct["s"]], rel

    def qk2(h, i, c, w):
        r = slice(64 * (h % 2), 64 * (h % 2) + 64)
        return QA[r, h // 2, 128 * i:128 * i + 128], KA[r, c:c + w], [x["t"] for x in qa_t + kn]

    ya_f = [None, None]
    ya_t = []
    yat = {0: [], 1: []}

    def post2(s, v):
        h, i = steps2[s]
        ya_t.append(v)
        if h == 7:
            t, a, l = tok_to_h([YA2[:, i % 2, 128 * c:128 * c + 128] for c in range(4)], i, 0, ya_t[-8:], None, None,
                               hw=win_done, eng="G")
            ya_f[i % 2] = t
            yat[i // 4] += [a, l]

    def load_b():
        for j in range(4):
            for half in range(2):
                sl = slice(512 * half, 512 * half + 512)
                k, kw = K1R.take()
                t = P.dma("S", f"b{k}", lambda e: e.dma_start(K1[:, k, :], d["yscr"][j][:, sl]), ob_t[j], kw)
                a, l = split(Hh[:, 4 + j, sl], Hl[:, 4 + j, sl], K1[:, k, :], t, win_done, eng="G")
                K1R.give(k, a, l)
                yh[4 + j, half] = [a, l]
    load_b()
    bg.append(attention(steps2, (PP2, PT2, mn2, sx2, rx2), qk2, bias2,
              lambda h, c: (VA[:, c, :].rearrange("p (a n) -> p a n", a=1).to_broadcast([128, 2, 64]), t_va),
              lambda h, i: (YA2[:, i % 2, 64 * h:64 * h + 64], ya_f[i % 2]), pre=pre2, post=post2))
    drain()
    for j in range(4):
        for half in range(2):
            yh[j, half] = yat[half]
    acc_free["t"] = rr_free["t"] = ya_t[-1]
    stA.close()
    stN.close()
    dead = [yat[1], P.mark(), ya_t[-1], yh[7, 1], bt[63]]
    stX, X, sm, xo, hd = out_proj("X3", d["spill"], spt, yh, dead)
    outs = []

    def last(m, half, v, nsm):
        if half:
            outs.append(P.dma("S", "out", lambda e: e.dma_start(d["out"][m], X[:, m, :]), v))
    sm, xo, hd = ffn(X, "norm2_w_2", xo, sm, hd, False, last)
    P.wait("S", outs[-1])
    assert ws["use"] == len(units), (ws, len(units))

    stX.close()
    ctx.close()


def _consts(np):
    f = np.float32
    p = np.arange(128)
    m = {}
    m["col1"] = np.stack([np.full(128, 1.0 / 1024), (p < 64) / 64.0, (p >= 64) / 64.0, np.full(128, 1.0 / 128),
                          np.full(128, 1.0 / 512)], axis=1).astype(f)
    m["sel"] = ((p[:, None] < 32) & (p[:, None] == p[None, :] % 32)).astype(f)
    m["ident"] = np.eye(128, dtype=f)
    pm = np.zeros((128, 128), f)
    for b in (0, 64):
        for i in range(32):
            pm[b + 32 + i, b + i] = -1.0
            pm[b + i, b + 32 + i] = 1.0
    m["perm"] = pm
    m["adm"] = np.where((p[:, None] < 64) & (p[None, :] >= 64), f(NEG), f(0)).astype(f)
    h = np.arange(8)
    lg = np.log1p(-(2.0 ** (-5.0 - h)))
    D = np.zeros((128, 8, 128), np.float64)
    rel = p[None, :] - p[:, None]
    for n in range(8):
        D[:, n, :] = np.where(rel >= 0, np.exp(-(p[:, None] + 1.0) * lg[n]), 0.0) * 0.125
    m["D"] = D.reshape(128, 1024).astype(f)
    qd = np.zeros((128, 4, 128), np.float64)
    for j in range(4):
        for half in range(2):
            qd[64 * half:64 * half + 64, j, :] = np.exp((p + 1.0) * lg[2 * j + half])[None, :]
    m["qdec"] = qd.reshape(128, 512).astype(f)
    mats = np.concatenate([m[n] for n, _ in MATS], axis=1)
    dq = np.concatenate([m["D"], m["qdec"]], axis=1)
    kdec = (np.exp((127.0 - p)[:, None] * lg[None, :]) * 0.125).astype(f)
    g128 = np.zeros((128, 4), f)
    for j in range(4):
        for half in range(2):
            g128[64 * half:64 * half + 64, j] = np.exp(128 * lg[2 * j + half])
    dist = 896 + p[:, None] - np.arange(1024)[None, :]
    c = ((dist <= 128).astype(int) + ((dist % 4 == 0) & (dist <= 512)) + (dist % 16 == 0)) * (dist >= 0)
    base = np.where(c > 0, np.log(np.maximum(c, 1)), NEG)
    T1 = np.stack([np.where(c > 0, base - (2.0 ** -(n + 1.0)) * dist, NEG) for n in range(8)]).astype(f)
    inv = (10000.0 ** (-np.arange(32, dtype=np.float64) / 32)).astype(f)
    ang = (np.arange(1024, dtype=f)[None, :] * inv[p % 32][:, None]).astype(f).astype(np.float64)
    cs = np.stack([np.cos(ang), np.sin(ang)], axis=1).astype(f)
    rel = np.arange(384) - 255
    n = np.abs(rel)
    nf = np.maximum(n, 1).astype(f)
    large = 8 + (np.log(nf / f(8)) / f(np.log(16.0)) * f(8)).astype(np.int32)
    bucket = np.where(rel > 0, 16, 0) + np.where(n < 8, n, np.minimum(large, 15))
    oh = (np.arange(32)[:, None] == bucket[None, :]).astype(f)
    oh[15, :] -= 1.0
    return mats, dq, kdec, g128, T1, cs, oh


def kernel(**inputs):
    import numpy as np
    import concourse.bacc as _bacc
    from concourse.bass_utils import run_bass_kernel_spmd as _run

    x = {k: np.asarray(v) for k, v in inputs.items()}
    f = np.float32
    mats, dq, kdec, g128, T1, cs, oh = _consts(np)

    def fm(w):
        K, N = w.shape
        return w.reshape(K // 128, 128, N // 128, 128).transpose(2, 1, 0, 3).reshape(N // 128, 128, K)

    def tm(w):
        return w.reshape(4, 2, 128, 512).transpose(0, 2, 1, 3).reshape(4, 128, 1024)

    w1, w2 = x["w_in"][0], x["w_in_2"][0]
    a = {}
    a["xT"] = x["x"][0].T.reshape(8, 128, 1024)
    a["pT"] = x["p"][0, 0].T.reshape(2, 128, 1024).transpose(1, 0, 2)
    a["wqk1"] = fm(np.concatenate([w1[:, 2048:2560], w1[:, 1536:2048]], axis=1))
    a["wv1"] = tm(w1[:, 2560:3072])
    wb, wc, wx = w1[:, 0:512], w1[:, 512:1024], w1[:, 1024:1536]
    a["wc1"] = fm(np.concatenate([w[:, 128 * j:128 * j + 128] for j in range(4) for w in (wc, wx, wb)], axis=1))
    a["wo1"] = fm(x["w_out"][0])
    a["wg1"], a["wu1"] = fm(x["w_gate"][0]), fm(x["w_up"][0])
    a["wd1"] = fm(x["w_down"][0])
    a["wpg"], a["wpp"] = fm(x["w_ple_gate"][0]), fm(x["w_ple_proj"][0])
    o = np.cumsum([0, 512, 128, 128, 32, 4, 512, 512, 512, 512])
    qa, ckv, iq, ik, iw, qb, kb, vb, gb = (w2[:, o[n]:o[n + 1]] for n in range(9))
    parts = [iq, ik, iw, np.zeros((1024, 92), f), ckv]
    for j in range(4):
        s = slice(128 * j, 128 * j + 128)
        parts += [qb[:, s], kb[:, s], vb[:, s], gb[:, s]]
    parts += [qa]
    a["wi2"] = fm(np.concatenate(parts, axis=1))
    a["wo2"] = fm(x["w_out_2"][0])
    a["wg2"], a["wu2"], a["wd2"] = fm(x["w_gate_2"][0]), fm(x["w_up_2"][0]), fm(x["w_down_2"][0])
    uk = x["w_uk_2"][0]
    a["wkv"] = np.concatenate([uk, uk, x["w_uv_2"][0]], axis=1)
    a["rb"] = np.concatenate([x["rel_bias_2"], oh], axis=1)
    a["T1"], a["cs"], a["mats"], a["dq"] = T1, cs, mats, dq

    def pp(v):
        return v.reshape(-1, 128).T

    c = {n: pp(x[n][0]) for n in ("g_mix", "g_ffn", "g_ple", "norm1_w_2", "norm2_w_2", "g_out_conv", "g_out_attn",
                                  "kv_norm_w_2", "ret_gn_w_2", "ret_gn_b_2")}
    c["conv_w"], c["conv_b"] = pp(x["conv_w"][0].reshape(-1)), pp(x["conv_b"][0])
    c["ffn_conv_w"], c["ffn_conv_b"] = pp(x["ffn_conv_w"][0].reshape(-1)), pp(x["ffn_conv_b"][0])
    for n in ("q_norm_g", "k_norm_g", "q_norm_w_2", "k_norm_w_2"):
        c[n] = np.concatenate([x[n][0], x[n][0]])[:, None]
    c["kdec"], c["g128"] = kdec, g128
    c["eps6"], c["eps5"] = np.full((128, 1), 1e-6, f), np.full((128, 1), 1e-5, f)
    a["cols"] = np.concatenate([c[n] for n, _ in COLS], axis=1)

    nc = _bacc.Bacc("TRN2", target_bir_lowering=False, num_devices=1)
    arrays, d = {}, {}
    for n, v in a.items():
        v = np.ascontiguousarray(v)
        assert v.dtype == f, n
        arrays["in_" + n] = v
        d[n] = nc.dram_tensor("in_" + n, v.shape, F32, kind="ExternalInput").ap()
    d["out"] = nc.dram_tensor("out_0", (8, 128, 1024), F32, kind="ExternalOutput").ap()
    d["spill"] = nc.dram_tensor("spill", (8, 128, 1024), F32, kind="Internal").ap()
    d["rscr"] = nc.dram_tensor("rscr", (128, 8, 384), F32, kind="Internal").ap()
    d["qscr"] = nc.dram_tensor("qscr", (4, 128, 1024), F32, kind="Internal").ap()
    d["yscr"] = nc.dram_tensor("yscr", (4, 128, 1024), F32, kind="Internal").ap()
    build(nc, d)
    r = _run(nc, [arrays], core_ids=[0])
    return np.ascontiguousarray(r.results[0]["out_0"].reshape(1024, 1024).T)[None]
```

```python
from contextlib import ExitStack

import concourse.bass as bass
from concourse import mybir

ALU = mybir.AluOpType
ACT = mybir.ActivationFunctionType
F32 = mybir.dt.float32
F32R = mybir.dt.float32r
I32 = mybir.dt.int32
NEG = -1.0e30

T = 1024
NH = 8
GROUPS = [(0, 5), (5, 10), (10, 14), (14, 18), (18, 22)]
NF = 22

COLS = [("g_mix", 8), ("g_ffn", 8), ("g_ple", 8), ("norm1_w_2", 8), ("norm2_w_2", 8),
        ("conv_w", 12), ("conv_b", 4), ("ffn_conv_w", 66), ("ffn_conv_b", 22),
        ("g_out_conv", 4), ("g_out_attn", 4), ("q_norm_g", 1), ("k_norm_g", 1),
        ("q_norm_w_2", 1), ("k_norm_w_2", 1), ("kv_norm_w_2", 1), ("ret_gn_w_2", 4), ("ret_gn_b_2", 4),
        ("kdec", 8), ("g128", 4), ("eps6", 1), ("eps5", 1)]
COL = {}
_at = 0
for _n, _w in COLS:
    COL[_n] = _at
    _at += _w
NCOL = _at

MATS = [("ident", 128), ("perm", 128), ("adm", 128), ("sel", 128), ("col1", 5)]
MAT = {}
_at = 0
for _n, _w in MATS:
    MAT[_n] = (_at, _w)
    _at += _w
NMAT = _at


class Prog:

    def __init__(self, nc, sems):
        self.sems = sems
        self.eng = {"V": nc.vector, "A": nc.scalar, "T": nc.tensor, "G": nc.gpsimd, "S": nc.sync}
        self.n = {s: 0 for s in sems}
        self.seen = {e: {} for e in "VATGS"}
        self.last = None

    def wait(self, e, *toks):
        for t in toks:
            if t is None:
                continue
            if isinstance(t, list):
                self.wait(e, *t)
                continue
            s, v = t
            if self.seen[e].get(s, 0) < v:
                self.seen[e][s] = v
                self.eng[e].wait_ge(self.sems[s], v)

    def do(self, e, fn, *toks):
        self.wait(e, *toks)
        self.n[e] += 1
        fn(self.eng[e]).then_inc(self.sems[e], 1)
        return (e, self.n[e])

    def mm(self, fn, *toks):
        self.wait("T", *toks)
        self.last = fn(self.eng["T"])

    def mark(self):
        if self.last is not None:
            self.n["T"] += 1
            self.last.then_inc(self.sems["T"], 1)
            self.last = None
        return ("T", self.n["T"])

    def dma(self, e, s, fn, *toks):
        self.wait(e, *toks)
        self.n[s] += 16
        fn(self.eng[e]).then_inc(self.sems[s], 16)
        return (s, self.n[s])


class Ring:

    def __init__(self, n):
        self.n, self.clock, self.free, self.since = n, n, [[] for _ in range(n)], list(range(n))

    def take(self, k=1):
        at = [i for i in range(0, self.n, k) if all(self.free[j] is not None for j in range(i, i + k))]
        assert at, "buffers still held"
        i = min(at, key=lambda i: max(self.since[i:i + k]))
        w = []
        for j in range(i, i + k):
            w += self.free[j]
            self.free[j] = None
        return i, w

    def give(self, i, *toks, k=1):
        for j in range(i, i + k):
            assert self.free[j] is None
            self.free[j] = list(toks)
            self.since[j] = self.clock
            self.clock += 1


def build(nc, d):
    ctx = ExitStack()
    used = set()

    def sbt(stack, name, shape, dt=F32):
        assert name not in used
        used.add(name)
        return stack.enter_context(nc.sbuf_tensor(name, shape, dt))

    DS = ["w0", "w1", "w2", "cst", "col", "x0", "x1", "x2", "x3", "x4", "x5", "x6", "x7", "y0", "y1", "y2", "y3", "y4", "y5", "y6", "y7", "z0", "z1", "z2", "z3", "q0", "q1", "q2", "q3", "b0", "b1", "b2", "b3", "t0", "t1", "sp", "rb", "rl", "out"]
    sems = {s: ctx.enter_context(nc.semaphore("s_" + s)) for s in list("VATG") + DS}
    P = Prog(nc, sems)
    PS = ctx.enter_context(nc.psum_tensor("PS", [128, 4096], F32))
    PB = Ring(8)

    def ps(b, n=512):
        return PS[:, 512 * b:512 * b + n]

    Hh = sbt(ctx, "Hh", [128, 8, T], F32R)
    Hl = sbt(ctx, "Hl", [128, 8, T], F32R)
    Wr = sbt(ctx, "Wr", [128, 3, 1024])
    Wh = sbt(ctx, "Wh", [128, 3, 1024], F32R)
    Wl = sbt(ctx, "Wl", [128, 3, 1024], F32R)
    acc = sbt(ctx, "acc", [128, T])
    rr = sbt(ctx, "rr", [128, T])
    K1 = sbt(ctx, "K1", [128, 4, 512])
    cols = sbt(ctx, "cols", [128, NCOL])
    mats = sbt(ctx, "mats", [128, NMAT])
    sml = sbt(ctx, "sml", [128, 512])
    K1R = Ring(4)

    def col(name, j=0):
        return cols[:, COL[name] + j:COL[name] + j + 1]

    def mat(name, j=0, n=None):
        at, w = MAT[name]
        n = w if n is None else n
        return mats[:, at + j:at + j + n]

    ident = mat("ident")
    gq1, gq2 = sml[:, 100:101], sml[:, 101:102]
    ident = mat("ident")
    gq1, gq2 = sml[:, 100:101], sml[:, 101:102]

    units = []
    units += [(d["wqk1"], n, 1024) for n in range(8)]
    units += [(d["wv1"], n, 1024) for n in range(4)]
    units += [(d["wc1"], n, 1024) for n in range(12)]
    units += [(d["wo1"], n, 1024) for n in range(8)]

    def ffn_units(g, u, dn):
        out = []
        for a, b in GROUPS:
            for f in range(a, b):
                out += [(g, f, 1024), (u, f, 1024)]
            out += [(dn, m, (a, b)) for m in range(8)]
        return out
    units += ffn_units(d["wg1"], d["wu1"], d["wd1"])
    units += [(d["wpg"], 0, 1024), (d["wpg"], 1, 1024), (d["wpp"], 0, 256), (d["wpp"], 1, 256)]
    for m in range(2, 8):
        units += [(d["wpg"], m, 1024), (d["wpp"], m, 256)]
    units += [(d["wi2"], n, 1024) for n in range(23)]
    units += [(d["wo2"], n, 1024) for n in range(8)]
    units += ffn_units(d["wg2"], d["wu2"], d["wd2"])

    raw_t, raw_free, cv_t, w_free = {}, {}, {}, {}
    ws = {"load": 0, "conv": 0, "use": 0}

    def ncols(n):
        return n if isinstance(n, int) else 128 * (n[1] - n[0])

    def load_unit():
        u = ws["load"]
        ws["load"] += 1
        if u >= len(units):
            return
        src, i, n = units[u]
        s = u % 3
        w = ncols(n)
        ap = src[i, :, 0:w] if isinstance(n, int) else src[i, :, 128 * n[0]:128 * n[1]]
        raw_t[u] = P.dma("S", f"w{s}", lambda e: e.dma_start(Wr[:, s, 0:w], ap), raw_free.get(u - 3))

    def conv_unit():
        u = ws["conv"]
        ws["conv"] += 1
        if u >= len(units):
            return
        w = ncols(units[u][2])
        s = u % 3
        a = P.do("A", lambda e: e.activation(Wh[:, s, 0:w], Wr[:, s, 0:w], ACT.Copy), raw_t[u], w_free.get(u - 3))
        g = P.do("G", lambda e: e.tensor_tensor(Wl[:, s, 0:w], Wr[:, s, 0:w], Wh[:, s, 0:w].bitcast(F32),
                                                ALU.subtract), a)
        raw_free[u] = g
        cv_t[u] = [a, g]

    def use_unit():
        u = ws["use"]
        ws["use"] += 1
        while ws["conv"] <= min(u + 2, len(units) - 1) and (ws["conv"] < 3 or ws["conv"] - 3 in w_free):
            conv_unit()
            load_unit()
        assert ws["conv"] > u
        return u, u % 3, cv_t[u]

    def ahead():
        while ws["conv"] < len(units) and ws["conv"] - 3 in w_free:
            conv_unit()
            load_unit()

    def done_unit(u, tok):
        w_free[u] = tok

    later = []
    bg, bg2 = [], []

    def flush():
        while later:
            later.pop(0)()

    def run_later(n):
        for _ in range(n):
            later.pop(0)()

    def tick():
        for q, n in ((bg, 1), (bg2, 2)):
            for _ in range(n):
                if q:
                    try:
                        next(q[0])
                    except StopIteration:
                        q.pop(0)

    def drain():
        while bg:
            tick()

    def tk_of(xt, k, half):
        if not isinstance(xt, dict):
            return xt
        return xt[k, half] if (k, half) in xt else xt[k]

    def products(uns, nks, xs, half, at=(2,), order=None):
        banks = [PB.take() for _ in uns]
        nmax = max(nks)
        at = [min(a, nmax - 1) for a in at]
        for k in range(nmax):
            kk = order[k] if order else k
            for (u, s, wt), nk, (xh, xl, xt), (b, bw) in zip(uns, nks, xs, banks):
                if k >= nk:
                    continue
                xk = tk_of(xt, kk, half)
                for n, (wa, xa) in enumerate(((Wl, xh), (Wh, xl), (Wh, xh))):
                    P.mm(lambda e, b=b, wa=wa, xa=xa, k=k, kk=kk, s=s, nk=nk, n=n: e.matmul(
                        ps(b), wa[:, s, 128 * kk:128 * kk + 128], xa(kk, half),
                        start=(k == 0 and n == 0), stop=(k == nk - 1 and n == 2)), wt, bw, xk)
            if k == nmax - 1:
                tok = P.mark()
            if (k + 1) % pace[0] == 0:
                tick()
            if k in at:
                run_later(len(later))
        return [b for b, _ in banks], tok

    pace = [3]

    def dense(nk, xh, xl, xt, consumer, order=None):
        un = use_unit()
        for half in range(2):
            (b,), tok = products([un], [nk], [(xh, xl, xt)], half, order=order)
            consumer(half, b, tok)
            tick()
        done_unit(un[0], tok)

    def dense_pair(one, two, fused=None, order=None):
        us = []
        if fused:
            us = [use_unit(), use_unit()]
            bb, tok = products(us, [one[0], two[0]], [one[1:4], two[1:4]], 0, fused, order)
            one[4](0, bb[0], tok)
            two[4](0, bb[1], tok)
            tick()
        for half in range(1 if fused else 0, 2):
            for n, (nk, xh, xl, xt, consumer) in enumerate((one, two)):
                if n == len(us):
                    us.append(use_unit())
                (b,), tok = products([us[n]], [nk], [(xh, xl, xt)], half, order=order)
                if half:
                    done_unit(us[n][0], tok)
                consumer(half, b, tok)
                tick()

    def hk(t):
        return lambda k, half: t[:, k, 512 * half:512 * half + 512]

    Hhk, Hlk = hk(Hh), hk(Hl)

    def dense_tok(xt, consumer):
        flush()
        banks = [PB.take() for _ in range(8)]
        for kg in range(4):
            u, s, wt = use_unit()
            for i in range(8):
                b, bw = banks[i]
                for k2 in range(2):
                    k = 2 * kg + k2
                    for n, (wa, xa) in enumerate(((Wl, Hh), (Wh, Hl), (Wh, Hh))):
                        P.mm(lambda e, b=b, wa=wa, xa=xa, k=k, k2=k2, i=i, n=n, s=s: e.matmul(
                            ps(b), xa[:, k, 128 * i:128 * i + 128], wa[:, s, 512 * k2:512 * k2 + 512],
                            start=(k == 0 and n == 0), stop=(k == 7 and n == 2)), wt, bw, tk_of(xt, k, i // 4))
                if kg == 3:
                    consumer(i, b, P.mark())
            done_unit(u, P.mark())

    class Sum:
        def __init__(self, eng="G"):
            self.t, self.first, self.eng = None, True, eng

        def add(self, x, sl, tok, fast=False):
            key = (sl.start, sl.stop)
            if key not in self.done:
                self.done[key] = P.do("A", lambda e: e.activation(acc[:, sl], x, ACT.Square), tok, acc_free["t"])
                return self.done[key]
            i, w = K1R.take()
            n = sl.stop - sl.start
            a = P.do("A", lambda e: e.activation(K1[:, i, 0:n], x, ACT.Square), tok, w)
            g = P.do("V" if fast else self.eng, lambda e: e.tensor_tensor(acc[:, sl], acc[:, sl], K1[:, i, 0:n], ALU.add),
                     a, self.done[key])
            K1R.give(i, g)
            self.done[key] = g
            return a

    def new_sum(eng="G"):
        s = Sum(eng)
        s.done = {}
        return s

    acc_free = {"t": None}
    rr_free = {"t": None}

    rn_free = [None, None]

    def rnorm(j, half, toks, then):
        def first():
            b, bw = PB.take()
            s0 = 104 + 4 * half
            for i in range(4):
                c = 512 * half + 128 * i
                P.mm(lambda e, i=i, c=c: e.matmul(PS[:, 512 * b + i:512 * b + i + 1], acc[:, c:c + 128],
                                                  mat("col1", j, 1), start=True, stop=True), bw, toks, t_cst)
            t = P.mark()
            acc_free["t"] = t
            a = P.do("A", lambda e: e.activation(sml[:, s0:s0 + 4], ps(b, 4), ACT.Sqrt, bias=col("eps6")), t, t_cols,
                     rn_free[half])
            PB.give(b, a)
            v = P.do("V", lambda e: e.reciprocal(sml[:, s0 + 8:s0 + 12], sml[:, s0:s0 + 4]), a, rn_free[half])

            def second():
                b, bw = PB.take()
                for i in range(4):
                    P.mm(lambda e, i=i: e.matmul(PS[:, 512 * b + 128 * i:512 * b + 128 * i + 128],
                                                 sml[:, s0 + 8 + i:s0 + 9 + i].to_broadcast([128, 128]), ident,
                                                 start=True, stop=True), bw, v, t_cst)
                t = P.mark()
                rn_free[half] = t
                then(b, t)
            later.append(second)
        later.append(first)

    def split(dh, dl, src, tok, w, eng="V"):
        a = P.do("A", lambda e: e.activation(dh, src, ACT.Copy), tok, w)
        v = P.do(eng, lambda e: e.tensor_tensor(dl, src, dh.bitcast(F32), ALU.subtract), a, tok, w)
        return a, v

    def norm_half(out, half, X, gname, b, rt, xtok, hw, tiles=range(8), give=True):
        sl = slice(512 * half, 512 * half + 512)
        for k in tiles:
            i, w = K1R.take()
            v = P.do("V", lambda e, k=k, i=i: e.scalar_tensor_tensor(
                out=K1[:, i, :], in0=X(k)[:, sl], scalar=col(gname, k), in1=ps(b), op0=ALU.mult, op1=ALU.mult),
                rt, xtok(k, half), w)
            a, l = split(Hh[:, k, sl], Hl[:, k, sl], K1[:, i, :], v, hw, eng="V" if k % 3 == 0 else "G")
            K1R.give(i, a, l)
            out[k, half] = [a, l]
        if give:
            PB.give(b, v)

    def next_norm(X, gname, ht):
        def start(half, sm, xo, hw):
            def part(b, t, tiles, give):
                norm_half(ht, half, lambda k: X[:, k, :], gname, b, t, lambda k, h: xo[k, h], hw, tiles, give)

            def both(b, t):
                part(b, t, range(3), False)
                later.append(lambda: part(b, t, range(3, 8), True))
            rnorm(0, half, [sm.done[512 * half, 512 * half + 512]], both)
        return start

    hn = Ring(3)

    def headnorm(half, b, tok, out, gcol, one=False):
        i, w = K1R.take()
        sq = K1[:, i, :]
        nh, cj = (1, 3) if one else (2, 1)
        a0 = P.do("A", lambda e: e.activation(out, ps(b), ACT.Copy), tok)
        a = P.do("A", lambda e: e.activation(sq, ps(b), ACT.Square), tok, w)
        PB.give(b, a)
        res = {}

        def second():
            z, zw = hn.take()
            s0 = 128 + 16 * z
            b2, bw = PB.take()
            for t4 in range(4):
                P.mm(lambda e, t4=t4: e.matmul(PS[:, 512 * b2 + nh * t4:512 * b2 + nh * t4 + nh],
                                               sq[:, 128 * t4:128 * t4 + 128], mat("col1", cj, nh),
                                               start=True, stop=True), bw, a, t_cst)
            t = P.mark()
            a2 = P.do("A", lambda e: e.activation(sml[:, s0:s0 + 4 * nh], ps(b2, 4 * nh), ACT.Sqrt, bias=col("eps6")),
                      t, t_cols, zw)
            PB.give(b2, a2)
            v = P.do("V", lambda e: e.reciprocal(sml[:, s0 + 8:s0 + 8 + 4 * nh], sml[:, s0:s0 + 4 * nh]), a2, zw)

            def third():
                r = sml[:, s0 + 8:s0 + 8 + 4 * nh].rearrange("p (h n) -> p h n", n=1)
                a3 = P.do("A", lambda e: e.activation(sq.rearrange("p (h n) -> p h n", h=4 * nh),
                                                      r.to_broadcast([128, 4 * nh, 128 // nh]), ACT.Copy), v, t)
                hn.give(z, a3)

                def fourth():
                    b3, bw = PB.take()
                    for t4 in range(4):
                        P.mm(lambda e, t4=t4: e.transpose(PS[:, 512 * b3 + 128 * t4:512 * b3 + 128 * t4 + 128],
                                                          sq[:, 128 * t4:128 * t4 + 128], ident), bw, a3)
                    t = P.mark()
                    K1R.give(i, t)
                    v2 = P.do("V", lambda e: e.scalar_tensor_tensor(out=out, in0=out, scalar=gcol, in1=ps(b3),
                                                                    op0=ALU.mult, op1=ALU.mult), t, a0)
                    PB.give(b3, v2)
                    res["t"] = v2
                later.append(fourth)
            later.append(third)
        later.append(second)
        return res

    stM = ExitStack()
    KT = sbt(stM, "KT", [128, 4, T])
    stX = ExitStack()
    X = sbt(stX, "X1", [128, 8, T])
    t_cols = P.dma("S", "col", lambda e: e.dma_start(cols[:, :], d["cols"]))
    t_cst = P.dma("S", "cst", lambda e: e.dma_start(mats[:, :], d["mats"]))
    xt = {}
    for half in range(2):
        sl = slice(512 * half, 512 * half + 512)
        for k in range(8):
            xt[k, half] = P.dma("S", f"x{k}" if half == 0 else f"y{k}",
                                lambda e, k=k, sl=sl: e.dma_start(X[:, k, sl], d["xT"][k][:, sl]))
        if half == 0:
            load_unit()
            load_unit()
    t_gq = P.do("V", lambda e: e.tensor_scalar(gq1, col("q_norm_g"), 0.125, None, ALU.mult), t_cols)
    t_gq = P.do("V", lambda e: e.tensor_scalar(gq2, col("q_norm_w_2"), 0.125, None, ALU.mult), t_cols)
    load_unit()
    sm = new_sum("V")
    ht = {}
    start = next_norm(X, "g_mix", ht)
    for half in range(2):
        sl = slice(512 * half, 512 * half + 512)
        for k in range(8):
            sm.add(X[:, k, sl], sl, xt[k, half])
        start(half, sm, xt, None)
        if half == 0:
            for _ in range(2):
                conv_unit()
                load_unit()
            flush()

    QT = []
    qk_t = []

    def cons_qk(n):
        def cons(half, b, tok):
            dst, g = (KT, col("k_norm_g")) if n < 4 else (QT[0], gq1)
            qk_t.append(headnorm(half, b, tok, dst[:, n % 4, 512 * half:512 * half + 512], g))
        return 8, Hhk, Hlk, ht, cons
    dense_pair(cons_qk(0), cons_qk(1), fused=(6, 7))
    x_dead = [ht[7, 1], ht[6, 1]]
    stX.close()
    QT.append(sbt(stM, "QT", [128, 4, T]))
    Vt = sbt(stM, "Vt", [128, 8, 512])
    PP = sbt(stM, "PP", [128, 3, T])
    PT = sbt(stM, "PT", [128, 2, T])
    YX = sbt(stM, "YX", [128, T])
    YC = sbt(stM, "YC", [128, 2, T])
    ZC = sbt(stM, "ZC", [128, 1, T + 2])
    mn = sbt(stM, "mn", [128, 64])
    sx = sbt(stM, "sx", [128, 64])
    rx = sbt(stM, "rx", [128, 64])
    for e in "VAG":
        P.wait(e, x_dead)
    for n in range(2, 8):
        dense(*cons_qk(n))
    flush()
    QT = QT[0]
    v_t = []

    def cons_v(i, b, tok):
        a = P.do("A", lambda e: e.activation(Vt[:, i, :], ps(b), ACT.Copy), tok)
        PB.give(b, a)
        v_t.append(a)
    dense_tok(ht, cons_v)

    def attention(steps, names, qk, bias, vv, out, pre=None, post=None, mid=None, vo=lambda h: 64 * (h % 2)):
        PPb, PTb, mnb, sxb, rxb = names
        pp = Ring(3)
        pt = Ring(2)
        q = {}

        def stage0(s):
            if pre:
                pre(s)
            h, i = steps[s]
            W = 128 * (i + 1)
            nb = 1 if W <= 512 else 2
            b, bw = PB.take(nb)
            for c in range(nb):
                w = min(512, W - 512 * c)
                pairs, tk = qk(h, i, 512 * c, w)
                for n, (lh, rh) in enumerate(pairs):
                    P.mm(lambda e, b=b, c=c, w=w, lh=lh, rh=rh, n=n: e.matmul(
                        ps(b + c, w), lh, rh, start=(n == 0), stop=(n == len(pairs) - 1)), bw, tk)
            t = P.mark()
            if mid:
                mid(s, t)
            p, pw = pp.take()
            bap, bt, brel = bias(h, i, W)
            v = P.do("V", lambda e: e.tensor_tensor_reduce(
                out=PPb[:, p, 0:W], in0=PS[:, 512 * b:512 * b + W], in1=bap, scale=-1.0, scalar=3.0e38,
                op0=ALU.add, op1=ALU.min, accum_out=mnb[:, s % 64:s % 64 + 1]), t, bt, pw)
            PB.give(b, v, k=nb)
            brel(v)
            a = P.do("A", lambda e: e.activation(PPb[:, p, 0:W], PPb[:, p, 0:W], ACT.Exp, bias=mnb[:, s % 64:s % 64 + 1],
                                                 scale=-1.0, accum_out=sxb[:, s % 64:s % 64 + 1]), v)
            q[s] = (W, nb, p, a)

        def stage1(s):
            W, nb, p, a = q[s]
            h, i = steps[s]
            b, bw = PB.take(nb)
            for c in range(i + 1):
                P.mm(lambda e, c=c: e.transpose(PS[:, 512 * b + 128 * c:512 * b + 128 * c + 128],
                                                PPb[:, p, 128 * c:128 * c + 128], ident), bw, a, t_cst)
            t = P.mark()
            pp.give(p, t)
            r = P.do("V", lambda e: e.reciprocal(rxb[:, s % 64:s % 64 + 1], sxb[:, s % 64:s % 64 + 1]), a)
            k, kw = pt.take()
            tt = []
            for c in range(nb):
                w = min(512, W - 512 * c)
                src = ps(b + c, w)
                dst = PTb[:, k, 512 * c:512 * c + w]
                if c == 0:
                    tt.append(P.do("A", lambda e, dst=dst, src=src: e.activation(dst, src, ACT.Copy), t, kw))
                else:
                    tt.append(P.do("V", lambda e, dst=dst, src=src: e.tensor_copy(dst, src), t, kw))
            PB.give(b, *tt, k=nb)
            q[s] = (k, tt, r)

        def stage2(s):
            h, i = steps[s]
            k, tt, r = q.pop(s)
            b, bw = PB.take()
            for c in range(i + 1):
                va, vt = vv(h, c)
                P.mm(lambda e, c=c, va=va: e.matmul(ps(b, 128), PTb[:, k, 128 * c:128 * c + 128], va,
                                                    start=(c == 0), stop=(c == i)), bw, tt, vt)
            t = P.mark()
            pt.give(k, t)
            oap, ow = out(h, i)
            o = vo(h)
            v = P.do("V", lambda e: e.tensor_scalar(oap, PS[:, 512 * b + o:512 * b + o + 64],
                                                    rxb[:, s % 64:s % 64 + 1], None, ALU.mult), t, r, ow)
            PB.give(b, v)
            if post:
                post(s, v)

        n = len(steps)
        for s in range(n + 3):
            if 2 <= s <= n + 1:
                stage1(s - 2)
            if s < n:
                stage0(s)
            if s >= 3:
                stage2(s - 3)
            yield

    tb = {"free": None}

    def load_tb(h):
        if h < 8:
            tb[h] = P.dma("S", "t0", lambda e: e.dma_start(rr[:, :], d["T1"][h]), tb["free"])
    load_tb(0)
    steps = [(h, i) for h in range(8) for i in range(8)]

    def qk1(h, i, c, w):
        r = slice(64 * (h % 2), 64 * (h % 2) + 64)
        return [(QT[r, h // 2, 128 * i:128 * i + 128], KT[r, h // 2, c:c + w])], [x["t"] for x in qk_t]

    def bias1(h, i, W):
        def rel(v):
            if i == 7:
                tb["free"] = v
                load_tb(h + 1)
        return rr[:, T - W:T], tb[h], rel

    ya_t = {}
    qk_done = {}

    def post1(s, v):
        ya_t[steps[s]] = v

    def ya(h):
        return YX[:, :] if h < 2 else QT[:, h // 2 - 1, :]

    def out1(h, i):
        return ya(h).rearrange("p (i n) -> p i n", i=8)[:, i, 64 * (h % 2):64 * (h % 2) + 64], [P.mark()]

    bg.append(attention(steps, (PP, PT, mn, sx, rx), qk1, bias1,
                        lambda h, c: (Vt[:, c, 128 * (h // 2):128 * (h // 2) + 128], v_t), out1, post=post1))
    yk_t, yr_t = {0: [], 1: []}, {}
    YR = Vt.rearrange("p a b -> p (a b)").rearrange("p (k n) -> p k n", k=4)
    ga = cols[:, COL["g_out_attn"]:COL["g_out_attn"] + 4].rearrange("p (c n) -> p c n", n=1).to_broadcast([128, 4, 128])

    def ya_norm():
        yall = ya_t[steps[-1]]
        for i in range(8):
            for q4 in range(4):
                k, w = K1R.take()
                src = ya(2 * q4).rearrange("p (i n) -> p i n", i=8)[:, i, :]
                a = P.do("A", lambda e, i=i, k=k, q4=q4, src=src: e.activation(
                    K1[:, k, 0:128], src, ACT.Square, accum_out=sml[:, 4 * i + q4:4 * i + q4 + 1]), yall, w)
                K1R.give(k, a)
            yield
            yield
        v = P.do("V", lambda e: e.tensor_reduce(sml[:, 80:88], sml[:, 0:32].rearrange("p (i n) -> p i n", i=8),
                                                mybir.AxisListType.X, ALU.add), a)
        a = P.do("A", lambda e: e.activation(sml[:, 88:96], sml[:, 80:88], ACT.Sqrt, bias=col("eps6"), scale=1.0 / 512),
                 v, t_cols)
        v0 = P.do("V", lambda e: e.reciprocal(sml[:, 80:88], sml[:, 88:96]), a)
        yield
        tr = {}
        for i in range(9):
            if i < 8:
                srcs = [ya(2 * q4).rearrange("p (i n) -> p i n", i=8)[:, i, :] for q4 in range(4)]
                for q4 in range(4):
                    src = srcs[q4]
                    if q4 % 2:
                        v2 = P.do("V", lambda e, i=i, src=src: e.tensor_scalar(src, src, sml[:, 80 + i:81 + i], None,
                                                                               ALU.mult), v0)
                    else:
                        a2 = P.do("A", lambda e, i=i, src=src: e.activation(src, src, ACT.Copy,
                                                                            scale=sml[:, 80 + i:81 + i]), v0)
                tr[i] = srcs, [v2, a2]
            if i:
                srcs, w = tr[i - 1]
                b, bw = PB.take()
                for c in range(4):
                    P.mm(lambda e, b=b, c=c, srcs=srcs: e.transpose(PS[:, 512 * b + 128 * c:512 * b + 128 * c + 128],
                                                                    srcs[c], ident), bw, w)
                t = P.mark()
                v = P.do("V", lambda e, b=b, i=i: e.tensor_tensor(
                    KT[:, :, 128 * i - 128:128 * i], ps(b).rearrange("p (c n) -> p c n", c=4), ga, ALU.mult), t)
                PB.give(b, v)
                yk_t[(i - 1) // 4].append(v)
            yield
            yield

    bg.append(ya_norm())
    pace[0] = 2
    zpad = P.do("V", lambda e: e.memset(ZC[:, :, 0:2], 0.0))
    smc = new_sum("G")
    st = {"zc": [None], "yc": [None, None]}
    yc_t = []
    for j in range(4):
        z = j % 2

        def cons_c(half, b, tok, z=z, j=j):
            a = P.do("A", lambda e: e.activation(ZC[:, 0, 2 + 512 * half:514 + 512 * half], ps(b), ACT.Copy), tok,
                     st["zc"][0])
            PB.give(b, a)
            st["ca", half] = a

        def cons_x(half, b, tok, z=z, j=j):
            zs = ZC[:, 0, 2 + 512 * half:514 + 512 * half]
            v = P.do("V", lambda e: e.tensor_tensor(zs, ps(b), zs, ALU.mult), tok, st["ca", half], zpad)
            PB.give(b, v)
            if half:
                y = YC[:, z, :]
                v = P.do("V", lambda e: e.tensor_scalar(y, ZC[:, 0, 2:T + 2], col("conv_w", 8 + j), col("conv_b", j),
                                                        ALU.mult, ALU.add), v, st["yc"][z])
                v = P.do("V", lambda e: e.scalar_tensor_tensor(out=y, in0=ZC[:, 0, 1:T + 1], scalar=col("conv_w", 4 + j),
                                                               in1=y, op0=ALU.mult, op1=ALU.add), v)
                v = P.do("V", lambda e: e.scalar_tensor_tensor(out=y, in0=ZC[:, 0, 0:T], scalar=col("conv_w", j),
                                                               in1=y, op0=ALU.mult, op1=ALU.add), v)
                st["zc"][0] = v
                st["y"] = v

        def cons_b(half, b, tok, z=z, j=j):
            sl = slice(512 * half, 512 * half + 512)
            v = P.do("V", lambda e: e.tensor_tensor(YC[:, z, sl], ps(b), YC[:, z, sl], ALU.mult), tok, st["y"])
            PB.give(b, v)
            a = smc.add(YC[:, z, sl], sl, v)
            if half:
                if j == 3:
                    return
                t = P.dma("S", f"z{z}", lambda e: e.dma_start(d["yscr"][j], YC[:, z, :]), v)
                st["yc"][z] = [t, a]
                yc_t.append(t)
        dense(8, Hhk, Hlk, ht, cons_c)
        dense(8, Hhk, Hlk, ht, cons_x)
        if j == 3:
            drain()
            pace[0] = 3
            for k in range(3):
                yr_t[k] = P.dma("S", f"y{k}", lambda e, k=k: e.dma_start(YR[:, k, :], d["yscr"][k]), yc_t[k],
                                ya_t[steps[-1]])
        dense(8, Hhk, Hlk, ht, cons_b)
    win_done = P.mark()
    drain()
    ahead()
    yh = {}
    for half in range(2):
        sl = slice(512 * half, 512 * half + 512)
        for c in range(4):
            yh[4 + c, half] = list(split(Hh[:, 4 + c, sl], Hl[:, 4 + c, sl], KT[:, c, sl], yk_t[half], win_done,
                                         eng="V" if c % 2 else "G"))
    for half in range(2):
        rnorm(4, half, [smc.done[512 * half, 512 * half + 512]], lambda b, t, half=half: norm_half(
            yh, half, lambda k: YR[:, k, :] if k < 3 else YC[:, 1, :], "g_out_conv", b, t,
            lambda k, half: yr_t[k] if k < 3 else None, win_done, range(4)))

    def close1():
        rr_free["t"] = tb["free"]
        stM.close()
        return list(yh.values()) + [P.mark()]

    def tok_to_h(srcs, i, j0, w, scale, gain, eng="V", hw=None):
        b, bw = PB.take()
        for c in range(4):
            P.mm(lambda e, c=c: e.transpose(PS[:, 512 * b + 128 * c:512 * b + 128 * c + 128], srcs[c], ident),
                 bw, w, t_cst)
        t = P.mark()
        pv = ps(b).rearrange("p (c n) -> p c n", c=4)
        k, kw = K1R.take()
        tmp = K1[:, k, 0:512].rearrange("p (c n) -> p c n", c=4)
        if gain is not None:
            v = P.do("V", lambda e: e.tensor_tensor(tmp, pv, gain, ALU.mult), t, kw)
        else:
            v = P.do("V", lambda e: e.tensor_copy(tmp, pv), t, kw)
        PB.give(b, v)
        a, l = split(Hh[:, j0:j0 + 4, 128 * i:128 * i + 128], Hl[:, j0:j0 + 4, 128 * i:128 * i + 128], tmp, v, hw, eng)
        K1R.give(k, a, l)
        return t, a, l

    def out_proj(name, src, srct, yh, close, gname, at):
        order = (4, 5, 6, 7, 0, 1, 2, 3)
        us = [use_unit(), use_unit()]
        bb, tok0 = products(us, [8, 8], [(Hhk, Hlk, yh)] * 2, 0, at, order)
        dead = close()
        st = ExitStack()
        X = sbt(st, name, [128, 8, T])
        xt = [P.dma("S", f"x{k}", lambda e, k=k: e.dma_start(X[:, k, :], src[k]), dead, srct) for k in range(8)]
        sm = new_sum("G")
        xo, ht = {}, {}
        start = next_norm(X, gname, ht)

        def cons_m(m):
            def cons(half, b, tok):
                sl = slice(512 * half, 512 * half + 512)
                v = P.do("V", lambda e: e.tensor_tensor(X[:, m, sl], ps(b), X[:, m, sl], ALU.add), tok, xt[m])
                PB.give(b, v)
                sm.add(X[:, m, sl], sl, v, m >= 6)
                xo[m, half] = v
                if m == 7:
                    start(half, sm, xo, tok)
            return 8, Hhk, Hlk, yh, cons
        for m in range(2):
            cons_m(m)[4](0, bb[m], tok0)
        for m in range(2):
            (b,), tok = products([us[m]], [8], [(Hhk, Hlk, yh)], 1, order=order)
            done_unit(us[m][0], tok)
            cons_m(m)[4](1, b, tok)
        for m in range(2, 6):
            dense(*cons_m(m), order=order)
        dense_pair(cons_m(6), cons_m(7), order=order)
        return st, X, xo, ht

    def ffn(X, name, xo, ht, conv, last):
        st = ExitStack()
        hdone = P.mark()
        HGh = sbt(st, "HGh" + name, [128, 5, T], F32R)
        HGl = sbt(st, "HGl" + name, [128, 5, T], F32R)
        GB = sbt(st, "GB" + name, [128, 2, T])
        SG = sbt(st, "SG" + name, [128, T + 2])
        zp = P.do("V", lambda e: e.memset(SG[:, 0:2], 0.0), hdone)
        hg_free = [hdone]
        s = {"sg": hdone}
        gbf = [hdone, hdone]
        nxo = {}
        for g, (fa, fb) in enumerate(GROUPS):
            hg_t = {}

            def cons_g(f):
                z = f % 2

                def cons(half, b, tok):
                    gs = GB[:, z, 512 * half:512 * half + 512]
                    if not conv:
                        s["silu", half] = P.do("A", lambda e: e.activation(gs, ps(b), ACT.Silu), tok, gbf[z])
                        PB.give(b, s["silu", half])
                        return
                    o = 512 * half
                    a = P.do("A", lambda e: e.activation(SG[:, 2 + o:514 + o], ps(b), ACT.Copy), tok, s["sg"], zp)
                    PB.give(b, a)
                    v = P.do("V", lambda e: e.tensor_scalar(gs, SG[:, 2 + o:514 + o], col("ffn_conv_w", 44 + f),
                                                            col("ffn_conv_b", f), ALU.mult, ALU.add), a, gbf[z])
                    v = P.do("V", lambda e: e.scalar_tensor_tensor(
                        out=gs, in0=SG[:, 1 + o:513 + o], scalar=col("ffn_conv_w", 22 + f), in1=gs,
                        op0=ALU.mult, op1=ALU.add), v)
                    v = P.do("V", lambda e: e.scalar_tensor_tensor(
                        out=gs, in0=SG[:, o:512 + o], scalar=col("ffn_conv_w", f), in1=gs,
                        op0=ALU.mult, op1=ALU.add), v)
                    if half:
                        s["sg"] = v
                    s["silu", half] = P.do("A", lambda e: e.activation(gs, gs, ACT.Silu), v)
                return 8, Hhk, Hlk, ht, cons

            def cons_u(f):
                z = f % 2

                def cons(half, b, tok):
                    sl = slice(512 * half, 512 * half + 512)
                    gs = GB[:, z, sl]
                    v = P.do("V", lambda e: e.tensor_tensor(gs, ps(b), gs, ALU.mult), tok, s["silu", half])
                    PB.give(b, v)
                    a, l = split(HGh[:, f - fa, sl], HGl[:, f - fa, sl], gs, v, hg_free, eng="V")
                    gbf[z] = [a, l]
                    hg_t[f - fa, half] = [a, l]
                return 8, Hhk, Hlk, ht, cons

            def cons_d(m):
                def cons(half, b, tok):
                    sl = slice(512 * half, 512 * half + 512)
                    v = P.do("V", lambda e: e.tensor_tensor(X[:, m, sl], ps(b), X[:, m, sl], ALU.add), tok,
                             xo[m, half], nxo.get((m, half)))
                    PB.give(b, v)
                    nxo[m, half] = v
                    if g == len(GROUPS) - 1:
                        last(m, half, nxo, tok)
                return fb - fa, hk(HGh), hk(HGl), hg_t, cons
            for f in range(fa, fb):
                if f == 0:
                    dense_pair(cons_g(f), cons_u(f), fused=(2, 5))
                else:
                    dense(*cons_g(f))
                    dense(*cons_u(f))
            for m in range(6):
                dense(*cons_d(m))
            if g < len(GROUPS) - 1:
                dense(*cons_d(6))
                dense(*cons_d(7))
                hg_free = [P.mark()]
            else:
                dense_pair(cons_d(6), cons_d(7))
        st.close()
        return nxo

    stX, X, xo, ht = out_proj("X2", d["xT"], None, yh, close1, "g_ffn", (0, 2))
    htp, smp = {}, new_sum("G")
    startp = next_norm(X, "g_ple", htp)

    def last1(m, half, nxo, tok):
        sl = slice(512 * half, 512 * half + 512)
        smp.add(X[:, m, sl], sl, nxo[m, half], m >= 6)
        if m == 7:
            startp(half, smp, nxo, tok)
    xo = ffn(X, "1", xo, ht, True, last1)
    ht = htp

    hd = P.mark()
    stP = ExitStack()
    PR = sbt(stP, "PR", [128, 2, T])
    Ph = sbt(stP, "Ph", [128, 2, T], F32R)
    Pl = sbt(stP, "Pl", [128, 2, T], F32R)
    SGP = sbt(stP, "SGP", [128, 2, T])
    pt = P.dma("S", "sp", lambda e: e.dma_start(PR[:, :, :], d["pT"]), hd, list(xo.values()))
    sgf = {(z, half): hd for z in range(2) for half in range(2)}
    nsm = new_sum("G")
    nxo = {}
    hb = {}
    startb = next_norm(X, "norm1_w_2", hb)
    spt = []
    sg_t = {}

    def cons_g(m):
        z = m % 2

        def cons(half, b, tok):
            a = P.do("A", lambda e: e.activation(SGP[:, z, 512 * half:512 * half + 512], ps(b), ACT.Sigmoid), tok, sgf[z, half])
            PB.give(b, a)
            sg_t[m, half] = a
        return 8, Hhk, Hlk, ht, cons

    def cons_p(m):
        z = m % 2

        def cons(half, b, tok):
            sl = slice(512 * half, 512 * half + 512)
            v = P.do("V", lambda e: e.tensor_tensor(SGP[:, z, sl], ps(b), SGP[:, z, sl], ALU.mult), tok, sg_t[m, half])
            PB.give(b, v)
            v = P.do("V", lambda e: e.tensor_tensor(X[:, m, sl], SGP[:, z, sl], X[:, m, sl], ALU.add), v, xo[m, half])
            sgf[z, half] = v
            nsm.add(X[:, m, sl], sl, v, m >= 6)
            nxo[m, half] = v
            if half:
                spt.append(P.dma("S", f"x{m}", lambda e: e.dma_start(d["spill"][m], X[:, m, :]), v))
            if m == 7:
                startb(half, nsm, nxo, tok)
        return 2, hk(Ph), hk(Pl), p_t, cons
    dense_pair(cons_g(0), cons_g(1), fused=(2, 5))
    p_t = list(split(Ph[:, :, :], Pl[:, :, :], PR[:, :, :], pt, hd))
    dense(*cons_p(0))
    dense(*cons_p(1))
    for m in range(2, 7):
        dense(*cons_g(m))
        dense(*cons_p(m))
    dense_pair(cons_g(7), cons_p(7))
    hd = P.mark()
    stP.close()

    ht = hb
    un_iq = use_unit()
    (b_iq,), t_iq = products([un_iq], [8], [(Hhk, Hlk, ht)], 0, at=(2, 6, 7))
    stX.close()
    dead = [ht[7, 1], ht[6, 1], hd] + spt
    for e in "VAG":
        P.wait(e, dead)
    stN = ExitStack()
    KS = sbt(stN, "KS", [128, T], F32R)
    VA = sbt(stN, "VA", [128, 8, 64])
    SC = sbt(stN, "SC", [128, 4224])
    IW = sbt(stN, "IW", [128, 8, 4])
    stI = ExitStack()
    IQ = sbt(stI, "IQ", [128, T])
    IK = sbt(stI, "IK", [128, T])
    CT = sbt(stI, "CT", [128, T])
    KA = sbt(stI, "KA", [128, T])
    IWT = sbt(stI, "IWT", [128, T])
    wkv = sbt(stI, "wkv", [128, 192])
    rb = sbt(stI, "rb", [32, 8 + 384])
    RR = sbt(stI, "RR", [128, 8, 384])
    ct = {}
    tkv = P.dma("S", "rl", lambda e: e.dma_start(wkv[:, :], d["wkv"]), dead)
    trb = P.dma("S", "rb", lambda e: e.dma_start(rb[:, :], d["rb"]), dead)
    def copy_cons(dst, fn=None, eng="A", tag=None):
        def cons(half, b, tok):
            sl = slice(512 * half, 512 * half + 512)
            if eng == "A":
                v = P.do("A", lambda e: e.activation(dst[:, sl], ps(b), fn or ACT.Copy), tok, ct.get(tag + "f"))
            else:
                v = P.do("V", lambda e: e.tensor_copy(dst[:, sl], ps(b)), tok, ct.get(tag + "f"))
            PB.give(b, v)
            ct.setdefault(tag, [])
            ct[tag] = [v] if half == 0 else ct[tag] + [v]
        return cons

    cons_iq = copy_cons(IQ[:, :], tag="iq")
    cons_iq(0, b_iq, t_iq)
    (b_iq,), t_iq = products([un_iq], [8], [(Hhk, Hlk, ht)], 1)
    done_unit(un_iq[0], t_iq)
    cons_iq(1, b_iq, t_iq)
    dense(8, Hhk, Hlk, ht, copy_cons(IWT[:, :], tag="iw"))
    for h in range(8):
        b, bw = PB.take()
        P.mm(lambda e, b=b, h=h: e.matmul(ps(b, 384), rb[:, h:h + 1].to_broadcast([32, 128]), rb[:, 8:392],
                                          start=True, stop=True), bw, trb)
        t = P.mark()
        a = P.do("A", lambda e, b=b, h=h: e.activation(RR[:, h, :], ps(b, 384), ACT.Copy), t)
        PB.give(b, a)
    t = P.dma("S", "rb", lambda e: e.dma_start(d["rscr"], RR[:, :, :]), a)
    t_scr = t
    ct["ik"] = []
    for half in range(2):
        b, bw = PB.take()
        P.mm(lambda e, b=b, half=half: e.matmul(ps(b), mat("sel"), IWT[:, 512 * half:512 * half + 512],
                                                start=True, stop=True), bw, ct["iw"], t_cst)
        t = P.mark()
        a = P.do("A", lambda e, b=b, half=half: e.activation(IK[:, 512 * half:512 * half + 512], ps(b), ACT.Copy), t)
        PB.give(b, a)
        ct["ik"].append(a)
    b, bw = PB.take(2)
    for i in range(8):
        P.mm(lambda e, i=i: e.transpose(PS[:, 512 * b + 128 * i:512 * b + 128 * i + 128],
                                        IWT[:, 128 * i:128 * i + 128], ident), bw, ct["iw"])
    t = P.mark()
    iwv = PS[:, 512 * b:512 * b + 1024].rearrange("p (i n) -> p i n", i=8)[:, :, 32:36]
    t_iw = P.do("V", lambda e: e.tensor_scalar(IW[:, :, :], iwv, 0.5, None, ALU.mult), t)
    PB.give(b, t_iw, k=2)
    SOFF = {}
    at = 0
    for i in range(2, 8):
        SOFF[i] = at
        at += 128 * (i + 1)
    ct["sc"] = {}
    ixr = Ring(2)
    IX = sbt(stI, "IX", [128, 2, T])

    def index_scores(i):
        W = 128 * (i + 1)
        nb = 1 if W <= 512 else 2
        sc = SC[:, SOFF[i]:SOFF[i] + W]
        for h in range(4):
            b, bw = PB.take(nb)
            r = slice(32 * h, 32 * h + 32)
            for c in range(nb):
                w = min(512, W - 512 * c)
                P.mm(lambda e, c=c, w=w, r=r: e.matmul(ps(b + c, w), IQ[r, 128 * i:128 * i + 128],
                                                       IK[r, 512 * c:512 * c + w], start=True, stop=True),
                     bw, ct["iq"], ct["ik"])
            t = P.mark()
            k, kw = ixr.take()
            a = P.do("A", lambda e, k=k, b=b: e.activation(IX[:, k, 0:W], PS[:, 512 * b:512 * b + W], ACT.Relu,
                                                           scale=32.0 ** -0.5), t, kw)
            PB.give(b, a, k=nb)
            if h == 0:
                v = P.do("V", lambda e, k=k: e.tensor_scalar(sc, IX[:, k, 0:W], IW[:, i, 0:1], None, ALU.mult), a, t_iw)
            else:
                v = P.do("V", lambda e, k=k, h=h: e.scalar_tensor_tensor(
                    out=sc, in0=IX[:, k, 0:W], scalar=IW[:, i, h:h + 1], in1=sc, op0=ALU.mult, op1=ALU.add), a, v)
            ixr.give(k, v)
            yield
        d_ = sc[:, W - 128:W]
        v = P.do("V", lambda e: e.scalar_tensor_tensor(out=d_, in0=mat("adm"), scalar=1.0e8, in1=d_, op0=ALU.mult,
                                                       op1=ALU.add), v, t_cst)
        ct["sc"][i] = v

    cu = sml[:, 32:38].bitcast(I32)
    xm = sml[:, 38:44].bitcast(I32)
    cand = sml[:, 44:50]
    cnt = sml[:, 50:56]
    kb_ = sml[:, 56:62].bitcast(I32)
    thr = sml[:, 64:70]

    def topk():
        junk = acc[:, :].bitcast(mybir.dt.bfloat16)
        jt = [None, None]
        v = P.do("V", lambda e: e.memset(cu, 0))
        v = P.do("V", lambda e: e.memset(xm, -1), v)
        for bit in range(31, -1, -1):
            imm = (1 << bit) - (1 << 32 if bit == 31 else 0)
            if bit == 31:
                v = P.do("V", lambda e: e.memset(cand.bitcast(I32), 0), v)
            else:
                v = P.do("V", lambda e, imm=imm: e.tensor_scalar(cand.bitcast(I32), cu, imm, None, ALU.bitwise_or), v)
                v = P.do("V", lambda e: e.tensor_tensor(cand.bitcast(I32), cand.bitcast(I32), xm, ALU.bitwise_xor), v)
            for i in range(2, 8):
                W = 128 * (i + 1)
                c = P.do("V", lambda e, i=i, W=W: e.tensor_scalar(
                    junk[:, T * (i % 2):T * (i % 2) + W], SC[:, SOFF[i]:SOFF[i] + W], cand[:, i - 2:i - 1], None, ALU.is_ge, ALU.add,
                    accum_out=cnt[:, i - 2:i - 1]), v, ct["sc"][i], jt[i % 2])
                jt[i % 2] = c
                yield
            if bit == 31:
                v = P.do("V", lambda e: e.tensor_scalar(kb_, cnt, 255.5, -2147483648.0, ALU.is_ge, ALU.mult), c)
                v = P.do("V", lambda e: e.tensor_copy(cu, kb_), v)
                w_ = P.do("V", lambda e: e.tensor_scalar(cnt, cnt, 255.5, None, ALU.is_ge), v)
                w_ = P.do("V", lambda e: e.tensor_scalar(xm, cnt, -2147483647.0 - 1.0, None, ALU.mult), w_)
                w2 = P.do("V", lambda e: e.tensor_scalar(kb_, cnt, 1.0, None, ALU.subtract), w_)
                v = P.do("V", lambda e: e.tensor_tensor(xm, xm, kb_, ALU.bitwise_or), w2)
            else:
                v = P.do("V", lambda e, bit=bit: e.tensor_scalar(kb_, cnt, 255.5, float(1 << bit), ALU.is_ge, ALU.mult), c)
                v = P.do("V", lambda e: e.tensor_tensor(cu, cu, kb_, ALU.bitwise_or), v)
            yield
        v = P.do("V", lambda e: e.tensor_tensor(thr.bitcast(I32), cu, xm, ALU.bitwise_xor), v)
        ct["thr"] = v

    for i in range(2, 8):
        bg.append(index_scores(i))
    cn = []

    def cons_c(half, b, tok):
        cn.append(headnorm(half, b, tok, CT[:, 512 * half:512 * half + 512], col("kv_norm_w_2"), one=True))
    dense(8, Hhk, Hlk, ht, cons_c)
    flush()
    kn = []
    for half in range(2):
        b, bw = PB.take()
        P.mm(lambda e, b=b, half=half: e.matmul(ps(b), wkv[:, 0:128], CT[:, 512 * half:512 * half + 512],
                                                start=True, stop=True), bw, [x["t"] for x in cn], tkv)
        t = P.mark()
        kn.append(headnorm(half, b, t, KA[:, 512 * half:512 * half + 512], col("k_norm_w_2")))
    b, bw = PB.take()
    for i in range(8):
        P.mm(lambda e, i=i: e.matmul(PS[:, 512 * b + 64 * i:512 * b + 64 * i + 64], CT[:, 128 * i:128 * i + 128],
                                     wkv[:, 128:192], start=True, stop=True), bw)
    t = P.mark()
    t_va = P.do("A", lambda e: e.activation(VA[:, :, :], ps(b).rearrange("p (i n) -> p i n", i=8), ACT.Copy), t)
    PB.give(b, t_va)
    flush()
    a = P.do("A", lambda e: e.activation(KS[:, :], KA[:, :], ACT.Copy), [x["t"] for x in kn])
    t_ks = P.do("V", lambda e: e.tensor_tensor(KS[64:128, :], KA[64:128, :], KS[64:128, :].bitcast(F32), ALU.subtract), a,
                [x["t"] for x in kn])
    drain()
    idead = [t_va, t_ks, t] + [x["t"] for x in kn + cn] + [v for v in ct["sc"].values()] + [t_iw, t_scr]
    stI.close()
    stR = ExitStack()
    VB = sbt(stR, "VB", [128, 2, 8, 128])
    DQ = sbt(stR, "DQ", [128, 1536])
    CS = sbt(stR, "CS", [128, 2, T])
    QR = sbt(stR, "QR", [128, 2, T])
    KR = sbt(stR, "KR", [128, 2, T])
    GG = sbt(stR, "GG", [128, 2, T])
    RW = rr
    YT = sbt(stR, "YT", [128, 8, 128])
    K2 = sbt(stR, "K2", [128, 2, 512])
    SD = sbt(stR, "SD", [128, 2, 256])
    KD = sbt(stR, "KD", [128, 2, 128])
    ST = sbt(stR, "ST", [128, 2, 64])
    bst = sbt(stR, "bst", [128, 16, 6])
    bag = sbt(stR, "bag", [128, 16, 2])
    rsd = sbt(stR, "rsd", [128, 16])
    for e in "VAG":
        P.wait(e, idead)
    t_cs = P.dma("S", "sp", lambda e: e.dma_start(CS[:, :, :], d["cs"]), idead)
    t_dq = P.dma("S", "rl", lambda e: e.dma_start(DQ[:, :], d["dq"]), idead, rr_free["t"], acc_free["t"])
    P.wait("A", rr_free["t"])
    P.wait("V", acc_free["t"])
    bg2.append(topk())
    rel_t = {z: None for z in ((n, y) for n in ("r", "gg") for y in range(2))}
    rel_t["yt"] = None
    ob_t = []

    def rotary(dst, free):
        out = []
        for half in range(2):
            sl = slice(512 * half, 512 * half + 512)
            b, bw = PB.take()
            P.mm(lambda e, b=b, sl=sl: e.matmul(ps(b), mat("perm"), RW[:, sl], start=True, stop=True), bw, ct["rw"])
            t = P.mark()
            g = P.do("G", lambda e, sl=sl: e.tensor_tensor(dst[:, sl], RW[:, sl], CS[:, 0, sl], ALU.mult),
                     ct["rw"], t_cs, free)
            k, kw = K1R.take()
            v = P.do("V", lambda e, b=b, sl=sl, k=k: e.tensor_tensor(K1[:, k, 0:512], ps(b), CS[:, 1, sl], ALU.mult),
                     t, kw, t_cs)
            PB.give(b, v)
            g2 = P.do("G", lambda e, sl=sl, k=k: e.tensor_tensor(dst[:, sl], dst[:, sl], K1[:, k, 0:512], ALU.add), v, g)
            K1R.give(k, g2)
            out.append(g2)
        ct["rwf"] = [t, g]
        return out

    k2r = Ring(2)

    def retention(j, y, qr, kr, vbt, ggt):
        QRy, KRy, VBy, GGy = QR[:, y, :], KR[:, y, :], VB[:, y, :, :], GG[:, y, :]
        for c in range(8):
            sl = slice(128 * c, 128 * c + 128)
            z = c % 2
            b, bw = PB.take(2)
            for h in range(2):
                r = slice(64 * h, 64 * h + 64)
                P.mm(lambda e, b=b, h=h, r=r, sl=sl: e.matmul(ps(b + h, 128), KRy[r, sl], QRy[r, sl], start=True,
                                                              stop=True), bw, kr, qr)
            t = P.mark()
            sdv = SD[:, z, :].rearrange("p (h n) -> p h n", h=2)
            v_sd = P.do("V", lambda e, b=b, sdv=sdv: e.tensor_tensor(
                sdv, PS[:, 512 * b:512 * b + 1024].rearrange("p (h n) -> p h n", h=2)[:, :, 0:128],
                DQ[:, 256 * j:256 * j + 256].rearrange("p (h n) -> p h n", h=2), ALU.mult), t, ct.get(("sdf", z)), t_dq)
            PB.give(b, v_sd, k=2)
            b, bw = PB.take()
            P.mm(lambda e, b=b, sl=sl: e.transpose(ps(b, 128), KRy[:, sl], ident), bw)
            t = P.mark()
            for h in range(2):
                a_kd = P.do("A", lambda e, b=b, h=h, z=z: e.activation(
                    KD[:, z, 64 * h:64 * h + 64], ps(b, 128)[:, 64 * h:64 * h + 64], ACT.Copy,
                    scale=col("kdec", 2 * j + h)), t, ct.get(("kdf", z)))
            PB.give(b, a_kd)
            yield
            b, bw = PB.take(2)
            for h in range(2):
                r = slice(64 * h, 64 * h + 64)
                o = slice(512 * (b + h), 512 * (b + h) + 64)
                P.mm(lambda e, z=z, h=h, o=o, c=c: e.matmul(
                    PS[:, o], SD[:, z, 128 * h:128 * h + 128], VBy[:, c, 64 * h:64 * h + 64],
                    start=True, stop=(c == 0)), bw, v_sd, vbt)
                if c:
                    P.mm(lambda e, z=z, h=h, o=o, r=r, sl=sl: e.matmul(
                        PS[:, o], QRy[r, sl], ST[r, z, :], start=False, stop=True), ct["st"])
            t_y = P.mark()
            ct["sdf", z] = t_y
            yv = PS[:, 512 * b:512 * b + 1024].rearrange("p (h n) -> p h n", h=2)[:, :, 0:64]
            a_y = P.do("A", lambda e, c=c, yv=yv: e.activation(YT[:, c, :].rearrange("p (h n) -> p h n", h=2), yv,
                                                               ACT.Copy), t_y, rel_t["yt"])
            PB.give(b, a_y, k=2)
            if c < 7:
                b, bw = PB.take()
                P.mm(lambda e, b=b, z=z, c=c: e.matmul(ps(b, 128), KD[:, z, :], VBy[:, c, :],
                                                       start=True, stop=True), bw, a_kd)
                t = P.mark()
                ct["kdf", z] = t
                sv = []
                for h in range(2):
                    r = slice(64 * h, 64 * h + 64)
                    o = slice(512 * b + 64 * h, 512 * b + 64 * h + 64)
                    if c == 0:
                        sv.append(P.do("V", lambda e, r=r, o=o, z=z: e.tensor_copy(ST[r, 1 - z, :], PS[r, o]), t, t_y))
                    else:
                        sv.append(P.do("V", lambda e, r=r, o=o, z=z: e.scalar_tensor_tensor(
                            out=ST[r, 1 - z, :], in0=ST[r, z, :], scalar=cols[r, COL["g128"] + j:COL["g128"] + j + 1],
                            in1=PS[r, o], op0=ALU.mult, op1=ALU.add), t, t_y, ct["st"]))
                PB.give(b, *sv)
                ct["st"] = sv
            for h in range(2):
                v = P.do("V", lambda e, h=h, c=c: e.bn_stats(bst[:, 2 * c + h, :], YT[:, c, 64 * h:64 * h + 64]), a_y)
                v_bag = P.do("V", lambda e, h=h, c=c: e.bn_aggr(bag[:, 2 * c + h, :], bst[:, 2 * c + h, :]), v)
            yield
        rel_t["r", y] = t_y
        vg = P.do("V", lambda e: e.tensor_copy(rsd[:, :], bag[:, :, 1]), v_bag)
        a = P.do("A", lambda e: e.activation(rsd[:, :], rsd[:, :], ACT.Sqrt, bias=col("eps5")), vg)
        v = P.do("V", lambda e: e.reciprocal(rsd[:, :], rsd[:, :]), a)
        for c in range(8):
            for h in range(2):
                v2 = P.do("V", lambda e, c=c, h=h: e.tensor_scalar(
                    YT[:, c, 64 * h:64 * h + 64], YT[:, c, 64 * h:64 * h + 64], bag[:, 2 * c + h, 0:1],
                    rsd[:, 2 * c + h:2 * c + h + 1], ALU.subtract, ALU.mult), v, a_y)
        yield
        b, bw = PB.take(2)
        for c in range(8):
            P.mm(lambda e, b=b, c=c: e.transpose(PS[:, 512 * b + 128 * c:512 * b + 128 * c + 128], YT[:, c, :], ident),
                 bw, v2)
        t = P.mark()
        rel_t["yt"] = t
        for half in range(2):
            sl = slice(512 * half, 512 * half + 512)
            k, kw = k2r.take()
            a = P.do("A", lambda e, b=b, half=half, k=k: e.activation(
                K2[:, k, :], ps(b + half), ACT.Identity, bias=col("ret_gn_b_2", j), scale=col("ret_gn_w_2", j)), t, kw)
            PB.give(b + half, a)
            v = P.do("V", lambda e, k=k, sl=sl: e.tensor_tensor(GGy[:, sl], K2[:, k, :], GGy[:, sl], ALU.mult),
                     a, ggt)
            k2r.give(k, v)
        t = P.dma("S", f"y{j}", lambda e: e.dma_start(d["yscr"][j], GGy), v)
        ob_t.append(t)
        rel_t["gg", y] = t
        yield

    for j in range(4):
        y = j % 2
        dense(8, Hhk, Hlk, ht, copy_cons(RW[:, :], tag="rw"))
        qr = rotary(QR[:, y, :], rel_t["r", y])
        qdv = DQ[:, 1024 + 128 * j:1024 + 128 * j + 128].rearrange("p (a n) -> p a n", a=1).to_broadcast([128, 8, 128])
        q8 = QR[:, y, :].rearrange("p (a n) -> p a n", a=8)
        qd = P.do("G", lambda e, qdv=qdv, q8=q8: e.tensor_tensor(q8, q8, qdv, ALU.mult), qr, t_dq)
        dense(8, Hhk, Hlk, ht, copy_cons(RW[:, :], tag="rw"))
        kr = rotary(KR[:, y, :], rel_t["r", y])
        dense(8, Hhk, Hlk, ht, copy_cons(RW[:, :], tag="rw"))
        b, bw = PB.take(2)
        for c in range(8):
            P.mm(lambda e, b=b, c=c: e.transpose(PS[:, 512 * b + 128 * c:512 * b + 128 * c + 128],
                                                 RW[:, 128 * c:128 * c + 128], ident), bw, ct["rw"])
        t = P.mark()
        ct["rwf"] = [t]
        vbt = []
        for half in range(2):
            vbt.append(P.do("A", lambda e, b=b, half=half, y=y: e.activation(
                VB[:, y, 4 * half:4 * half + 4, :], ps(b + half).rearrange("p (c n) -> p c n", c=4), ACT.Copy),
                t, rel_t["r", y]))
        PB.give(b, vbt[1], k=2)
        ct["ggf"] = rel_t["gg", y]
        dense(8, Hhk, Hlk, ht, copy_cons(GG[:, y, :], fn=ACT.Silu, tag="gg"))
        drain()
        bg.append(retention(j, y, [qd], kr, vbt, ct["gg"]))
    qa_t, qs_t = {}, []
    stage = [GG[:, 0, :], rr[:, :]]
    sfree = [rel_t["gg", 0], ct["rwf"]]
    for j in range(4):
        z = j % 2
        P.wait("A", sfree[z])
        P.wait("V", sfree[z])
        mine = []

        def cons(half, b, tok, z=z, mine=mine):
            mine.append(headnorm(half, b, tok, stage[z][:, 512 * half:512 * half + 512], gq2))
        dense(8, Hhk, Hlk, ht, cons)

        def put(j=j, z=z, mine=mine):
            if not all("t" in x for x in mine):
                later.append(put)
                return
            sfree[z] = P.dma("S", f"q{j}", lambda e: e.dma_start(d["qscr"][j], stage[z]), [x["t"] for x in mine])
            qs_t.append(sfree[z])
        later.append(put)
        while j == 1 and len(qs_t) < 1 or j == 2 and len(qs_t) < 2:
            run_later(1)
    q0 = d["qscr"]
    q_st, q_t, q_free = {}, {}, {}

    def load_q(i, g):
        k, kw = K1R.take()
        src = bass.AP(tensor=q0.tensor, offset=4 * g * 64 * T + 128 * i, ap=[[T, 64], [64 * T, 4], [1, 128]])
        q_st[g] = k, [P.dma("S", f"{'bz'[z]}{k}", lambda e, z=z: e.dma_start(
            K1[64 * z:64 * z + 64, k, :].rearrange("p (h n) -> p h n", h=4), src), kw, qs_t[2 * g], qs_t[2 * g + 1])
            for z in range(2)]

    load_q(0, 0)
    flush()
    win_done = P.mark()
    drain()
    ret_dead = [P.mark(), vbt, ob_t, qd, kr, qs_t[0], qs_t[2]] + [P.do("V", lambda e: e.memset(sml[:, 98:99], 0.0)),
                                                      P.do("A", lambda e: e.activation(sml[:, 99:100], ident[:, 0:1], ACT.Copy))]
    stR.close()
    QH = sbt(stN, "QH", [128, 8, 128], F32R)
    QL = sbt(stN, "QL", [128, 8, 128], F32R)
    BN = sbt(stN, "BN", [128, 8, 256])
    for e in "VAG":
        P.wait(e, ret_dead)
    r0 = d["rscr"]
    rsrc = bass.AP(tensor=r0.tensor, offset=127, ap=[[8 * 384 - 1, 128], [384, 8], [1, 256]])
    t_bn = P.dma("S", "rb", lambda e: e.dma_start(BN[:, :, :], rsrc), t_scr, ret_dead)
    load_q(0, 1)

    def split_q(i, g):
        k, t = q_st[g]
        a, l = split(QH[:, 4 * g:4 * g + 4, :], QL[:, 4 * g:4 * g + 4, :],
                     K1[:, k, :].rearrange("p (h n) -> p h n", h=4), t, q_free.get(g), eng="G")
        K1R.give(k, a, l)
        q_t[i, g] = [a, l]
    while bg2:
        tick()
    yh = {}
    rdead = [win_done]

    stA = ExitStack()
    MM = sbt(stA, "MM", [128, 2, T])
    MN = sbt(stA, "MN", [128, 2, 256])
    SE = [acc, rr]
    PP2 = sbt(stA, "PP2", [128, 3, T])
    PT2 = sbt(stA, "PT2", [128, 2, T])
    YA2 = sbt(stA, "YA2", [128, 2, 512])
    mn2 = sbt(stA, "mn2", [128, 64])
    sx2 = sbt(stA, "sx2", [128, 64])
    rx2 = sbt(stA, "rx2", [128, 64])
    one = sbt(stA, "one", [128, 1])
    for e in "VAG":
        P.wait(e, rdead)
    t_one = P.do("V", lambda e: e.memset(one[:, :], 1.0))
    need = sml[:, 72:80]
    mt = {}
    mm_free = [None, None]

    eq_f = [None]

    def chosen(i):
        W = 128 * (i + 1)
        if i == 2:
            P.wait("V", qs_t[3])
        sc = SC[:, SOFF[i]:SOFF[i] + W]
        th = thr[:, i - 2:i - 1]
        eq, rk = SE[0][:, 0:W], SE[1][:, 0:W]
        v1 = P.do("V", lambda e: e.tensor_scalar(eq, sc, th, None, ALU.is_equal), ct["thr"], eq_f)
        yield
        v2 = P.do("V", lambda e: e.tensor_tensor_scan(rk, one[:, 0:1].to_broadcast([128, W]), eq, 0.0, ALU.mult, ALU.add),
                  v1, t_one)
        yield
        v3 = P.do("V", lambda e: e.tensor_scalar(sc, sc, th, None, ALU.is_gt, ALU.add, accum_out=need[:, i:i + 1]), v1)
        v4 = P.do("V", lambda e: e.tensor_scalar(need[:, i:i + 1], need[:, i:i + 1], -1.0, 256.0, ALU.mult, ALU.add), v3)
        yield
        v5 = P.do("V", lambda e: e.scalar_tensor_tensor(out=eq, in0=rk, scalar=need[:, i:i + 1], in1=eq,
                                                        op0=ALU.is_le, op1=ALU.mult), v4, v2)
        yield
        mt["eq"] = P.do("V", lambda e: e.tensor_tensor(eq, eq, sc, ALU.add), v5)

    def mask(i):
        W = 128 * (i + 1)
        nr = min(256, W)
        if i < 2:
            v = P.do("V", lambda e: e.memset(MN[:, i % 2, 0:nr], 0.0), mt.get(("mn", i % 2)))
            v = P.do("V", lambda e: e.tensor_copy(MN[:, i % 2, nr - 128:nr], mat("adm")), v)
            mt[i] = v
            return
        eq = SE[0][:, 0:W]
        v7 = P.do("V", lambda e: e.tensor_scalar(MM[:, 0, 0:W], eq, -NEG, NEG, ALU.mult, ALU.add), mt["eq"], mm_free)
        mt[i] = P.do("V", lambda e: e.tensor_copy(MN[:, i % 2, :], MM[:, 0, W - 256:W]), v7, mt.get(("mn", i % 2)))
        mt["m1"] = P.do("G", lambda e: e.tensor_scalar(MM[:, 1, 0:W], eq, -NEG, NEG, ALU.mult, ALU.add), mt["eq"], mm_free)
        eq_f[0] = [mt["m1"], mt[i]]

    steps2 = [(h, i) for i in range(8) for h in range(8)]
    bt = {}

    def pre2(s):
        h, i = steps2[s]
        if h == 0:
            mask(i)
        elif 1 <= i < 7:
            if h == 1:
                ct["mg"] = chosen(i + 1)
            for _ in ct["mg"] if h == 7 else (next(ct["mg"]),) if h < 5 else ():
                pass
        z = h % 2
        W = 128 * (i + 1)
        nr = min(256, W)
        g = P.do("G", lambda e: e.tensor_tensor(MM[:, z, W - nr:W], MN[:, i % 2, 0:nr], BN[:, h, 256 - nr:256], ALU.add),
                 mt[i], mm_free[z], t_bn, mt.get("m1"))
        mt["mn", i % 2] = g
        bt[s] = g
        ct["s"] = s
        if h == 1 and i:
            split_q(i, 1)
        if h == 5 and i < 7:
            split_q(i + 1, 0)
        if h == 2 and i < 7:
            load_q(i + 1, 0)
        if h == 6 and i < 7:
            load_q(i + 1, 1)

    def mid2(s, t):
        h, i = steps2[s]
        if h % 4 == 3:
            q_free[h // 4] = t

    def bias2(h, i, W):
        z = h % 2

        def rel(v):
            mm_free[z] = v
        return MM[:, z, 0:W], bt[ct["s"]], rel

    def qk2(h, i, c, w):
        return [(QH[:, h, :], KS[:, c:c + w]), (QL[:, h, :], KS[:, c:c + w])], [q_t[i, h // 4], t_ks]

    ya_f = [None, None]
    ya_t = []
    yat = {0: [], 1: []}

    b_st = {}

    def load_b(j, half):
        k, kw = K1R.take()
        b_st[j, half] = k, P.dma("S", f"b{k}", lambda e: e.dma_start(
            K1[:, k, :], d["yscr"][j][:, 512 * half:512 * half + 512]), ob_t[j], kw)

    def split_b(j, half):
        sl = slice(512 * half, 512 * half + 512)
        k, t = b_st[j, half]
        a, l = split(Hh[:, 4 + j, sl], Hl[:, 4 + j, sl], K1[:, k, :], t, win_done, eng="G")
        K1R.give(k, a, l)
        yh[4 + j, half] = [a, l]

    def post2(s, v):
        h, i = steps2[s]
        if h == 1:
            load_b(i % 4, i // 4)
        if h == 4:
            split_b(i % 4, i // 4)
        ya_t.append(v)
        if h == 7:
            t, a, l = tok_to_h([YA2[:, i % 2, 128 * c:128 * c + 128] for c in range(4)], i, 0, ya_t[-8:], None, None,
                               hw=win_done, eng="G")
            ya_f[i % 2] = t
            yat[i // 4] += [a, l]

    split_q(0, 0)
    split_q(0, 1)
    bg.append(attention(steps2, (PP2, PT2, mn2, sx2, rx2), qk2, bias2,
              lambda h, c: (VA[:, c, :].rearrange("p (a n) -> p a n", a=1).to_broadcast([128, 2, 64]), t_va),
              lambda h, i: (YA2[:, i % 2, 64 * h:64 * h + 64], ya_f[i % 2]), pre=pre2, post=post2, mid=mid2))
    drain()
    for j in range(4):
        for half in range(2):
            yh[j, half] = yat[half]
    acc_free["t"] = rr_free["t"] = ya_t[-1]

    def close2():
        stA.close()
        stN.close()
        return [yat[1], P.mark(), ya_t[-1], yh[7, 1], bt[63]]
    stX, X, xo, ht = out_proj("X3", d["spill"], spt, yh, close2, "norm2_w_2", (2, 5))
    outs = []

    def last2(m, half, nxo, tok):
        if half:
            outs.append(P.dma("S", "out", lambda e: e.dma_start(d["out"][m], X[:, m, :]), nxo[m, 0], nxo[m, 1]))
    ffn(X, "2", xo, ht, False, last2)
    P.wait("S", outs[-1])
    assert ws["use"] == len(units), (ws, len(units))

    stX.close()
    ctx.close()


def _consts(np):
    f = np.float32
    p = np.arange(128)
    m = {}
    m["col1"] = np.stack([np.full(128, 1.0 / 1024), (p < 64) / 64.0, (p >= 64) / 64.0, np.full(128, 1.0 / 128),
                          np.full(128, 1.0 / 512)], axis=1).astype(f)
    m["sel"] = ((p[:, None] < 32) & (p[:, None] == p[None, :] % 32)).astype(f)
    m["ident"] = np.eye(128, dtype=f)
    pm = np.zeros((128, 128), f)
    for b in (0, 64):
        for i in range(32):
            pm[b + 32 + i, b + i] = -1.0
            pm[b + i, b + 32 + i] = 1.0
    m["perm"] = pm
    m["adm"] = np.where((p[:, None] < 64) & (p[None, :] >= 64), f(NEG), f(0)).astype(f)
    h = np.arange(8)
    lg = np.log1p(-(2.0 ** (-5.0 - h)))
    D = np.zeros((128, 8, 128), np.float64)
    rel = p[None, :] - p[:, None]
    for n in range(8):
        D[:, n, :] = np.where(rel >= 0, np.exp(-(p[:, None] + 1.0) * lg[n]), 0.0) * 0.125
    m["D"] = D.reshape(128, 1024).astype(f)
    qd = np.zeros((128, 4, 128), np.float64)
    for j in range(4):
        for half in range(2):
            qd[64 * half:64 * half + 64, j, :] = np.exp((p + 1.0) * lg[2 * j + half])[None, :]
    m["qdec"] = qd.reshape(128, 512).astype(f)
    mats = np.concatenate([m[n] for n, _ in MATS], axis=1)
    dq = np.concatenate([m["D"], m["qdec"]], axis=1)
    kdec = (np.exp((127.0 - p)[:, None] * lg[None, :]) * 0.125).astype(f)
    g128 = np.zeros((128, 4), f)
    for j in range(4):
        for half in range(2):
            g128[64 * half:64 * half + 64, j] = np.exp(128 * lg[2 * j + half])
    dist = 896 + p[:, None] - np.arange(1024)[None, :]
    c = ((dist <= 128).astype(int) + ((dist % 4 == 0) & (dist <= 512)) + (dist % 16 == 0)) * (dist >= 0)
    base = np.where(c > 0, np.log(np.maximum(c, 1)), NEG)
    T1 = np.stack([np.where(c > 0, base - (2.0 ** -(n + 1.0)) * dist, NEG) for n in range(8)]).astype(f)
    inv = (10000.0 ** (-np.arange(32, dtype=np.float64) / 32)).astype(f)
    ang = (np.arange(1024, dtype=f)[None, :] * inv[p % 32][:, None]).astype(f).astype(np.float64)
    cs = np.stack([np.cos(ang), np.sin(ang)], axis=1).astype(f)
    rel = np.arange(384) - 255
    n = np.abs(rel)
    nf = np.maximum(n, 1).astype(f)
    large = 8 + (np.log(nf / f(8)) / f(np.log(16.0)) * f(8)).astype(np.int32)
    bucket = np.where(rel > 0, 16, 0) + np.where(n < 8, n, np.minimum(large, 15))
    oh = (np.arange(32)[:, None] == bucket[None, :]).astype(f)
    oh[15, :] -= 1.0
    return mats, dq, kdec, g128, T1, cs, oh


def kernel(**inputs):
    import numpy as np
    import concourse.bacc as _bacc
    from concourse.bass_utils import run_bass_kernel_spmd as _run

    x = {k: np.asarray(v) for k, v in inputs.items()}
    f = np.float32
    mats, dq, kdec, g128, T1, cs, oh = _consts(np)

    def fm(w):
        K, N = w.shape
        return w.reshape(K // 128, 128, N // 128, 128).transpose(2, 1, 0, 3).reshape(N // 128, 128, K)

    def tm(w):
        return w.reshape(4, 2, 128, 512).transpose(0, 2, 1, 3).reshape(4, 128, 1024)

    w1, w2 = x["w_in"][0], x["w_in_2"][0]
    a = {}
    a["xT"] = x["x"][0].T.reshape(8, 128, 1024)
    a["pT"] = x["p"][0, 0].T.reshape(2, 128, 1024).transpose(1, 0, 2)
    a["wqk1"] = fm(np.concatenate([w1[:, 2048:2560], w1[:, 1536:2048]], axis=1))
    a["wv1"] = tm(w1[:, 2560:3072])
    wb, wc, wx = w1[:, 0:512], w1[:, 512:1024], w1[:, 1024:1536]
    a["wc1"] = fm(np.concatenate([w[:, 128 * j:128 * j + 128] for j in range(4) for w in (wc, wx, wb)], axis=1))
    a["wo1"] = fm(x["w_out"][0])
    a["wg1"], a["wu1"] = fm(x["w_gate"][0]), fm(x["w_up"][0])
    a["wd1"] = fm(x["w_down"][0])
    a["wpg"], a["wpp"] = fm(x["w_ple_gate"][0]), fm(x["w_ple_proj"][0])
    o = np.cumsum([0, 512, 128, 128, 32, 4, 512, 512, 512, 512])
    qa, ckv, iq, ik, iw, qb, kb, vb, gb = (w2[:, o[n]:o[n + 1]] for n in range(9))
    parts = [iq, ik, iw, np.zeros((1024, 92), f), ckv]
    for j in range(4):
        s = slice(128 * j, 128 * j + 128)
        parts += [qb[:, s], kb[:, s], vb[:, s], gb[:, s]]
    parts += [qa]
    a["wi2"] = fm(np.concatenate(parts, axis=1))
    a["wo2"] = fm(x["w_out_2"][0])
    a["wg2"], a["wu2"], a["wd2"] = fm(x["w_gate_2"][0]), fm(x["w_up_2"][0]), fm(x["w_down_2"][0])
    uk = x["w_uk_2"][0]
    a["wkv"] = np.concatenate([uk, uk, x["w_uv_2"][0]], axis=1)
    a["rb"] = np.concatenate([x["rel_bias_2"], oh], axis=1)
    a["T1"], a["cs"], a["mats"], a["dq"] = T1, cs, mats, dq

    def pp(v):
        return v.reshape(-1, 128).T

    c = {n: pp(x[n][0]) for n in ("g_mix", "g_ffn", "g_ple", "norm1_w_2", "norm2_w_2", "g_out_conv", "g_out_attn",
                                  "kv_norm_w_2", "ret_gn_w_2", "ret_gn_b_2")}
    c["conv_w"], c["conv_b"] = pp(x["conv_w"][0].reshape(-1)), pp(x["conv_b"][0])
    c["ffn_conv_w"], c["ffn_conv_b"] = pp(x["ffn_conv_w"][0].reshape(-1)), pp(x["ffn_conv_b"][0])
    for n in ("q_norm_g", "k_norm_g", "q_norm_w_2", "k_norm_w_2"):
        c[n] = np.concatenate([x[n][0], x[n][0]])[:, None]
    c["kdec"], c["g128"] = kdec, g128
    c["eps6"], c["eps5"] = np.full((128, 1), 1e-6, f), np.full((128, 1), 1e-5, f)
    a["cols"] = np.concatenate([c[n] for n, _ in COLS], axis=1)

    nc = _bacc.Bacc("TRN2", target_bir_lowering=False, num_devices=1)
    arrays, d = {}, {}
    for n, v in a.items():
        v = np.ascontiguousarray(v)
        assert v.dtype == f, n
        arrays["in_" + n] = v
        d[n] = nc.dram_tensor("in_" + n, v.shape, F32, kind="ExternalInput").ap()
    d["out"] = nc.dram_tensor("out_0", (8, 128, 1024), F32, kind="ExternalOutput").ap()
    d["spill"] = nc.dram_tensor("spill", (8, 128, 1024), F32, kind="Internal").ap()
    d["rscr"] = nc.dram_tensor("rscr", (128, 8, 384), F32, kind="Internal").ap()
    d["qscr"] = nc.dram_tensor("qscr", (4, 128, 1024), F32, kind="Internal").ap()
    d["yscr"] = nc.dram_tensor("yscr", (4, 128, 1024), F32, kind="Internal").ap()
    build(nc, d)
    r = _run(nc, [arrays], core_ids=[0])
    return np.ascontiguousarray(r.results[0]["out_0"].reshape(1024, 1024).T)[None]
```
